# Optimizing a Trainium2 kernel written in Bass

```python
import jax, jax.numpy as jnp
from jax import lax
import numpy as np

D_MODEL = 1024
BATCH = 1
SEQ = 1024
DEPTH = 1
DEC_BATCH = 8
DEC_SEQ = 1
PAST_LEN = 2048
PAGE_SIZE = 128

HEAD_DIM = 64
N_Q_HEADS = 8
N_KV_HEADS = 2
GQA_GROUP = N_Q_HEADS // N_KV_HEADS
WINDOW = 128
ROT_DIM = HEAD_DIM // 4
ROPE_THETA = 500000.0
N_HGRN_HEADS = 8
HGRN_DK = 64
HGRN_DV = 64
HGRN_CHUNK = 64
D_ATTN = N_Q_HEADS * HEAD_DIM
D_KV = N_KV_HEADS * HEAD_DIM
D_HGRN_K = N_HGRN_HEADS * HGRN_DK
D_HGRN = N_HGRN_HEADS * HGRN_DV
D_MIX = D_ATTN + D_HGRN
IN_SPLITS = (D_ATTN, D_KV, D_KV, D_HGRN_K, D_HGRN_K, D_HGRN, D_HGRN)
IN_COLS = sum(IN_SPLITS)
D_FF = 2816
EPS = 1e-6
NEG_INF = -1e30

kernel_name = "hymba_swa_sink_hgrn2_macaron_step"

def rms_norm(x, g):
    xf = x.astype(jnp.float32)
    r = xf * lax.rsqrt(jnp.mean(xf * xf, axis=-1, keepdims=True) + EPS)
    return (r * g.astype(jnp.float32)).astype(x.dtype)

def half_step_ffn(x, g_pre, g_post, w_gu, w_down):
    h = rms_norm(x, g_pre)
    gate, up = jnp.split(h @ w_gu, 2, axis=-1)
    y = (jax.nn.silu(gate) * up) @ w_down
    return x + 0.5 * rms_norm(y, g_post)

def partial_rope(x, pos):
    half = ROT_DIM // 2
    inv = ROPE_THETA ** (-jnp.arange(half, dtype=jnp.float32) / half)
    ang = pos[:, None] * inv[None, :]
    cos = jnp.cos(ang)[:, None, :]
    sin = jnp.sin(ang)[:, None, :]
    xf = x.astype(jnp.float32)
    x1, x2, rest = xf[..., :half], xf[..., half:ROT_DIM], xf[..., ROT_DIM:]
    out = jnp.concatenate([x1 * cos - x2 * sin, x2 * cos + x1 * sin, rest], axis=-1)
    return out.astype(x.dtype)

def sink_softmax(s, mask, sink):
    s = jnp.where(mask, s, NEG_INF)
    m = jnp.maximum(jnp.max(s, axis=-1, keepdims=True), sink)
    p = jnp.exp(s - m)
    denom = jnp.sum(p, axis=-1, keepdims=True) + jnp.exp(sink - m)
    return p / denom

def mixer_inputs(proj, pos, lb):
    B, T, _ = proj.shape
    offs = [int(o) for o in np.cumsum(IN_SPLITS)[:-1]]
    q, k, v, hq, hf, hi, hg = jnp.split(proj, offs, axis=-1)
    q = partial_rope(q.reshape(B, T, N_Q_HEADS, HEAD_DIM), pos)
    k = partial_rope(k.reshape(B, T, N_KV_HEADS, HEAD_DIM), pos)
    v = v.reshape(B, T, N_KV_HEADS, HEAD_DIM)
    hq = hq.reshape(B, T, N_HGRN_HEADS, HGRN_DK).astype(jnp.float32) * (HGRN_DK ** -0.5)
    lbh = lb.reshape(N_HGRN_HEADS, HGRN_DK)
    f = lbh + (1.0 - lbh) * jax.nn.sigmoid(hf.reshape(B, T, N_HGRN_HEADS, HGRN_DK).astype(jnp.float32))
    logf = jnp.log(f)
    hk = 1.0 - f
    hv = hi.reshape(B, T, N_HGRN_HEADS, HGRN_DV).astype(jnp.float32)
    hg = hg.reshape(B, T, N_HGRN_HEADS, HGRN_DV)
    return q, k, v, hq, hk, logf, hv, hg

def swa_prompt(q, k, v, sinks):
    B, T, _, _ = q.shape
    nb = T // WINDOW
    qb = q.reshape(B, nb, WINDOW, N_KV_HEADS, GQA_GROUP, HEAD_DIM)
    pad = jnp.zeros((B, WINDOW, N_KV_HEADS, HEAD_DIM), k.dtype)
    kp = jnp.concatenate([pad, k], axis=1)
    vp = jnp.concatenate([pad.astype(v.dtype), v], axis=1)
    kb = jnp.concatenate([kp[:, :T].reshape(B, nb, WINDOW, N_KV_HEADS, HEAD_DIM),
                          k.reshape(B, nb, WINDOW, N_KV_HEADS, HEAD_DIM)], axis=2)
    vb = jnp.concatenate([vp[:, :T].reshape(B, nb, WINDOW, N_KV_HEADS, HEAD_DIM),
                          v.reshape(B, nb, WINDOW, N_KV_HEADS, HEAD_DIM)], axis=2)
    s = jnp.einsum('bnqhgd,bnkhd->bnhgqk', qb, kb).astype(jnp.float32) * (HEAD_DIM ** -0.5)
    i = jnp.arange(WINDOW)[:, None]
    j = jnp.arange(2 * WINDOW)[None, :]
    rel = i + WINDOW - j
    band = (rel >= 0) & (rel < WINDOW)
    valid = band[None] & ((jnp.arange(nb)[:, None, None] > 0) | (j[None] >= WINDOW))
    sink = sinks.astype(jnp.float32).reshape(1, 1, N_KV_HEADS, GQA_GROUP, 1, 1)
    p = sink_softmax(s, valid[None, :, None, None], sink)
    o = jnp.einsum('bnhgqk,bnkhd->bnqhgd', p.astype(vb.dtype), vb)
    keep = min(WINDOW, T)
    return o.reshape(B, T, D_ATTN), k[:, T - keep:], v[:, T - keep:]

def swa_sample(q, k, v, win_k, win_v, sinks):
    B, T, _, _ = q.shape
    W = win_k.shape[1]
    keys = jnp.concatenate([win_k.astype(k.dtype), k], axis=1)
    vals = jnp.concatenate([win_v.astype(v.dtype), v], axis=1)
    qg = q.reshape(B, T, N_KV_HEADS, GQA_GROUP, HEAD_DIM)
    s = jnp.einsum('bqhgd,bkhd->bhgqk', qg, keys).astype(jnp.float32) * (HEAD_DIM ** -0.5)
    kpos = jnp.concatenate([PAST_LEN - W + jnp.arange(W), PAST_LEN + jnp.arange(T)])
    qpos = PAST_LEN + jnp.arange(T)
    rel = qpos[:, None] - kpos[None, :]
    valid = (rel >= 0) & (rel < WINDOW)
    sink = sinks.astype(jnp.float32).reshape(1, N_KV_HEADS, GQA_GROUP, 1, 1)
    p = sink_softmax(s, valid, sink)
    o = jnp.einsum('bhgqk,bkhd->bqhgd', p.astype(vals.dtype), vals)
    return o.reshape(B, T, D_ATTN), keys[:, T:], vals[:, T:]

def hgrn2_chunk(S, q, k, logf, v):
    C = q.shape[1]
    G = jnp.cumsum(logf, axis=1)
    o_inter = jnp.einsum('bchk,bhkv->bchv', q * jnp.exp(G), S)
    tri = jnp.tril(jnp.ones((C, C), dtype=bool))
    diff = G[:, :, None] - G[:, None, :]
    decay = jnp.where(tri[None, :, :, None, None], jnp.exp(jnp.minimum(diff, 0.0)), 0.0)
    A = jnp.einsum('bthk,bshk,btshk->bhts', q, k, decay)
    o_intra = jnp.einsum('bhts,bshv->bthv', A, v)
    GC = G[:, -1]
    kd = k * jnp.exp(GC[:, None] - G)
    S_new = jnp.exp(GC)[..., None] * S + jnp.einsum('bshk,bshv->bhkv', kd, v)
    return S_new, o_inter + o_intra

def hgrn2_prompt(hq, hk, logf, hv):
    B, T = hq.shape[:2]
    C = min(HGRN_CHUNK, T)
    nc = T // C

    def to_chunks(a):
        return a.reshape(B, nc, C, *a.shape[2:]).swapaxes(0, 1)

    S0 = jnp.zeros((B, N_HGRN_HEADS, HGRN_DK, HGRN_DV), jnp.float32)
    S, o = lax.scan(lambda S, xs: hgrn2_chunk(S, *xs), S0,
                    (to_chunks(hq), to_chunks(hk), to_chunks(logf), to_chunks(hv)))
    return o.swapaxes(0, 1).reshape(B, T, N_HGRN_HEADS, HGRN_DV), S

def mixer_output(att, ho, hg, out_g, w_o):
    B, T, _ = att.shape
    hn = rms_norm(ho, out_g) * jax.nn.silu(hg.astype(jnp.float32))
    cat = jnp.concatenate([att, hn.reshape(B, T, D_HGRN).astype(att.dtype)], axis=-1)
    return cat @ w_o

def setup_inputs(seed: int = 0) -> dict:
    key = jax.random.key(seed)
    ks = jax.random.split(key, 24)
    f32 = jnp.float32

    def w(k, shape, fan_in):
        return jax.random.normal(k, shape, f32) * fan_in ** -0.5

    def gain(k, shape):
        return 1.0 + 0.05 * jax.random.normal(k, shape, f32)

    win_keep = min(WINDOW, PAST_LEN)
    return {
        "x_prompt": jax.random.normal(ks[0], (BATCH, SEQ, D_MODEL), f32),
        "x_sample": jax.random.normal(ks[1], (DEC_BATCH, DEC_SEQ, D_MODEL), f32),
        "cache_win_k": jax.random.normal(ks[2], (DEPTH, DEC_BATCH, win_keep, N_KV_HEADS, HEAD_DIM), f32),
        "cache_win_v": jax.random.normal(ks[3], (DEPTH, DEC_BATCH, win_keep, N_KV_HEADS, HEAD_DIM), f32),
        "state_hgrn": 0.3 * jax.random.normal(ks[4], (DEPTH, DEC_BATCH, N_HGRN_HEADS, HGRN_DK, HGRN_DV), f32),
        "ffn1_pre_g": gain(ks[5], (DEPTH, D_MODEL)),
        "ffn1_post_g": gain(ks[6], (DEPTH, D_MODEL)),
        "ffn1_w_gu": w(ks[7], (DEPTH, D_MODEL, 2 * D_FF), D_MODEL),
        "ffn1_w_down": w(ks[8], (DEPTH, D_FF, D_MODEL), D_FF),
        "mix_pre_g": gain(ks[9], (DEPTH, D_MODEL)),
        "mix_post_g": gain(ks[10], (DEPTH, D_MODEL)),
        "w_in": w(ks[11], (DEPTH, D_MODEL, IN_COLS), D_MODEL),
        "attn_sinks": 0.5 * jax.random.normal(ks[12], (DEPTH, N_Q_HEADS), f32),
        "hgrn_lb": 0.1 * jax.random.normal(ks[13], (DEPTH + 1, D_HGRN_K), f32),
        "hgrn_out_g": gain(ks[14], (DEPTH, HGRN_DV)),
        "w_out": w(ks[15], (DEPTH, D_MIX, D_MODEL), D_MIX),
        "ffn2_pre_g": gain(ks[16], (DEPTH, D_MODEL)),
        "ffn2_post_g": gain(ks[17], (DEPTH, D_MODEL)),
        "ffn2_w_gu": w(ks[18], (DEPTH, D_MODEL, 2 * D_FF), D_MODEL),
        "ffn2_w_down": w(ks[19], (DEPTH, D_FF, D_MODEL), D_FF),
    }

def reference(x_prompt, x_sample, cache_win_k, cache_win_v, state_hgrn,
              ffn1_pre_g, ffn1_post_g, ffn1_w_gu, ffn1_w_down,
              mix_pre_g, mix_post_g, w_in, attn_sinks, hgrn_lb, hgrn_out_g, w_out,
              ffn2_pre_g, ffn2_post_g, ffn2_w_gu, ffn2_w_down):
    T_p = x_prompt.shape[1]
    T_s = x_sample.shape[1]
    pos_p = jnp.arange(T_p, dtype=jnp.float32)
    pos_s = PAST_LEN + jnp.arange(T_s, dtype=jnp.float32)
    lb_all = jnp.cumsum(jax.nn.softmax(hgrn_lb.astype(jnp.float32), axis=0), axis=0)

    xp, xs = x_prompt, x_sample
    wk_p, wv_p, S_p_all, wk_s, wv_s, S_s_all = [], [], [], [], [], []
    for l in range(DEPTH):
        xp = half_step_ffn(xp, ffn1_pre_g[l], ffn1_post_g[l], ffn1_w_gu[l], ffn1_w_down[l])
        xs = half_step_ffn(xs, ffn1_pre_g[l], ffn1_post_g[l], ffn1_w_gu[l], ffn1_w_down[l])

        q, k, v, hq, hk, logf, hv, hg = mixer_inputs(rms_norm(xp, mix_pre_g[l]) @ w_in[l], pos_p, lb_all[l])
        att, nk, nv = swa_prompt(q, k, v, attn_sinks[l])
        ho, S_p = hgrn2_prompt(hq, hk, logf, hv)
        xp = xp + rms_norm(mixer_output(att, ho, hg, hgrn_out_g[l], w_out[l]), mix_post_g[l])
        wk_p.append(nk)
        wv_p.append(nv)
        S_p_all.append(S_p.astype(x_prompt.dtype))

        q, k, v, hq, hk, logf, hv, hg = mixer_inputs(rms_norm(xs, mix_pre_g[l]) @ w_in[l], pos_s, lb_all[l])
        att, nk, nv = swa_sample(q, k, v, cache_win_k[l], cache_win_v[l], attn_sinks[l])
        S_s, ho = hgrn2_chunk(state_hgrn[l].astype(jnp.float32), hq, hk, logf, hv)
        xs = xs + rms_norm(mixer_output(att, ho, hg, hgrn_out_g[l], w_out[l]), mix_post_g[l])
        wk_s.append(nk.astype(cache_win_k.dtype))
        wv_s.append(nv.astype(cache_win_v.dtype))
        S_s_all.append(S_s.astype(state_hgrn.dtype))

        xp = half_step_ffn(xp, ffn2_pre_g[l], ffn2_post_g[l], ffn2_w_gu[l], ffn2_w_down[l])
        xs = half_step_ffn(xs, ffn2_pre_g[l], ffn2_post_g[l], ffn2_w_gu[l], ffn2_w_down[l])

    return (xp, xs, jnp.stack(wk_p), jnp.stack(wv_p), jnp.stack(S_p_all),
            jnp.stack(wk_s), jnp.stack(wv_s), jnp.stack(S_s_all))


_drawn_inputs = setup_inputs


def setup_inputs(seed=0):
    import zlib

    import numpy as np

    out = dict(_drawn_inputs(seed))
    spreads = {}
    factors = {'attn_sinks': 8.0, 'ffn2_post_g': 3.614}
    for name, (base, spread) in spreads.items():
        noise = np.random.default_rng([zlib.crc32(name.encode()), seed]).standard_normal(out[name].shape)
        drawn = base * np.exp(spread * noise) if base else spread * noise
        out[name] = __import__('jax').numpy.asarray(drawn.astype(out[name].dtype))
    for name, factor in factors.items():
        out[name] = (out[name] * factor).astype(out[name].dtype)
    return out
```

```python
from contextlib import ExitStack

import numpy as np

import concourse.bass as bass
from concourse import mybir

F32 = mybir.dt.float32
F32R = mybir.dt.float32r
U32 = mybir.dt.uint32
ALU = mybir.AluOpType
ACT = mybir.ActivationFunctionType
AX_X = mybir.AxisListType.X

P = 128
D_MODEL, D_FF = 1024, 2816
N_PROMPT, N_SAMPLE, PAST_LEN = 1024, 8, 2048
TOK = N_PROMPT + N_SAMPLE
NG = 3
GW = TOK // NG
KT = D_MODEL // P
HT = D_FF // P
HEAD, N_HEADS, N_KV, GQA = 64, 8, 2, 4
WINDOW, ROT, THETA = 128, 16, 500000.0
EPS, NEG = 1e-6, -1e30
CH = 128
N_CH = N_PROMPT // CH
TPH = 4
IN_TILES = 22
F_MIN = 2.0 ** -32
LEVELS = (8, 16, 32, 64)
SUB = 8

FFN_STEPS = HT // 2
FFN_GRANULES, FFN_UNITS = 6, 4 * NG + NG * KT
G_IN = FFN_STEPS * FFN_GRANULES
G_OUT = G_IN + IN_TILES
G_FFN2 = G_OUT + KT
U_IN = FFN_STEPS * FFN_UNITS
U_OUT = U_IN + NG * IN_TILES
U_FFN2 = U_OUT + NG * KT
UNIT_CREDIT, EVAC_CREDIT, READY_CREDIT = FFN_UNITS, NG, 3

V_GAIN = {"ffn1_pre": 0, "ffn1_post": 8, "mix_pre": 16, "mix_post": 24, "ffn2_pre": 32, "ffn2_post": 40}
V_LB0, V_LB1, V_OUTG, V_SINK, V_SINKT, NV = 48, 52, 56, 57, 65, 67
M_LVL, M_SUB, M_BAND, M_FIRST, M_ROT, NM = 0, 512, 640, 896, 1152, 1280


class Seq:

    def __init__(self, eng, sem):
        self.eng, self.sem, self.n, self.i, self.per, self.left = eng, sem, 0, None, 0, 0

    def __call__(self, ins):
        self.n += 1
        ins.then_inc(self.sem, 1)
        self.eng.wait_ge(self.sem, self.n if self.i is None else self.i * self.per + self.n)

    def enter(self, i, per):
        self.i, self.per, self.at = i, per, self.n

    def leave(self, times):
        assert self.n - self.at == self.per, (self.n - self.at, self.per)
        self.n = self.at + times * self.per
        self.i = None


def build(nc, ins, outs):
    ctx = ExitStack()
    with ctx:
        sems = {}

        def sem(name):
            sems[name] = ctx.enter_context(nc.semaphore(name))
            return sems[name]

        at = [(nc.sbuf_base + 31) // 32 * 32]
        end = nc.sbuf_usable_end

        def put(name, shape, dt, offset=None):
            size = 4 * int(np.prod(shape[1:]))
            if offset is None:
                offset = at[0]
                at[0] += (size + 31) // 32 * 32
            assert offset + size <= end, (name, offset + size - end)
            return nc.alloc_sbuf_tensor_at(name, shape, dt, offset=offset)

        vecs = put("vecs", [P, NV], F32)
        half_gain = put("half_gain", [P, 2, KT], F32)
        lb = put("lb", [P, 3, TPH], F32)
        ident = put("ident", [P, P], F32)
        ones = put("ones", [P, P], F32)
        head_ones = put("head_ones", [P, P], F32)
        rms = put("rms", [P, NG, GW], F32)
        raw = [put(f"raw{s}", [P, 1024], F32) for s in range(2)]
        w_hi = [put(f"w_hi{s}", [P, 1024], F32R) for s in range(2)]
        w_lo = [put(f"w_lo{s}", [P, 1024], F32R) for s in range(2)]
        x_at = at[0]
        x_hi = put("x_hi", [P, NG, KT, GW], F32R)
        x_lo = put("x_lo", [P, NG, KT, GW], F32R)
        x_end = zone = at[0]

        y = put("y", [P, NG, KT, GW], F32)
        resid = put("resid", [P, NG, KT, GW], F32)
        h = put("h", [P, NG, 4, GW], F32R)
        sq = put("sq", [P, KT, GW], F32)
        raw.append(put("raw2", [P, 1024], F32))
        w_hi.append(put("w_hi2", [P, 1024], F32R))
        w_lo.append(put("w_lo2", [P, 1024], F32R))
        silu_at = at[0]
        silu_g = put("silu_g", [P, NG, GW], F32)
        prod = put("prod", [P, NG, GW], F32)
        root = put("root", [P, 2, GW], F32, silu_at)
        rms_y = put("rms_y", [P, 2, GW], F32, silu_at + NG * GW * 4)

        at[0] = zone
        R = put("proj", [P, 5 * TPH, TOK], F32)
        f_reg, hq_reg, hi_reg, q_reg, hg_reg = (R[:, TPH * j:TPH * (j + 1), :] for j in range(5))
        chunk = lambda j, c: R[:, TPH * j:TPH * (j + 1), bass.ds(c * CH, CH)]
        k_gate = put("k_gate", [P, TPH, TOK], F32)
        kv = put("kv", [P, 2, TOK], F32)
        f_s = put("f_s", [P, TPH, N_SAMPLE], F32)
        mixc = put("mixc", [P, NM], F32)
        kt_s = put("kt_s", [P, 2, N_SAMPLE], F32)
        qu_s = put("qu_s", [P, TPH, N_SAMPLE], F32)
        qt_s = put("qt_s", [P, TPH, N_SAMPLE], F32)
        q_s = put("q_s", [P, TPH, N_SAMPLE], F32)
        k_win = put("k_win", [P, 2 * CH], F32)
        hi_c = put("hi_c", [P, TPH, CH], F32)
        hi_at = zone + 2 * TPH * TOK * 4
        state_s = put("state_s", [P, TPH, N_SAMPLE, HEAD], F32, zone)
        k_win_s = put("k_win_s", [P, N_SAMPLE, WINDOW], F32, zone + 8192)
        v_win_s = put("v_win_s", [P, N_SAMPLE, P], F32, zone + 12288)
        c_sq = put("c_sq", [P, TPH, GW], F32, hi_at)
        c_root = put("c_root", [P, TPH, GW], F32, hi_at + 8192)
        at[0] = x_at
        rope_c = put("rope_c", [P, TOK], F32)
        rope_s = put("rope_s", [P, TOK], F32)
        G = put("G", [P, TPH, CH], F32)
        dif = put("dif", [P, 2, TPH, CH], F32)
        dec = put("dec", [P, 2, TPH, CH], F32)
        q_dec = put("q_dec", [P, 2, TPH, CH], F32)
        k_dec = put("k_dec", [P, 2, TPH, CH], F32)
        A = put("A", [P, N_HEADS, CH], F32)
        V = put("V", [P, N_HEADS * HEAD], F32)
        kdT = put("kdT", [P, N_HEADS * HEAD], F32)
        qg = put("qg", [P, TPH, CH], F32)
        kd = put("kd", [P, TPH, CH], F32)
        state = put("state", [P, TPH, HEAD], F32)
        g_end = put("g_end", [P, TPH], F32)
        q_rot = put("q_rot", [P, TPH, CH], F32)
        rc_at = at[0]
        rot_c = put("rot_c", [P, TPH, CH], F32)
        rs_at = at[0]
        rot_s = put("rot_s", [P, TPH, CH], F32)
        v_win = put("v_win", [P, 2 * CH], F32)
        v_at = at[0]
        v_c = put("v_c", [P, CH], F32)
        rotk_c = put("rotk_c", [P, CH], F32)
        rotk_s = put("rotk_s", [P, CH], F32)
        sm_at = at[0]
        sm = put("sm", [P, 2, GQA * 2 * CH], F32)
        pt_at = at[0]
        pT = put("pT", [P, 2, GQA * 2 * CH], F32)
        m_cur = mixc[:, M_FIRST:M_FIRST + 2 * CH]
        mx = put("mx", [P, 2, GQA], F32)
        nm = put("nm", [P, 2, GQA], F32)
        es = put("es", [P, 2, GQA], F32)
        rsum = put("rsum", [P, 2, GQA], F32)
        rden = put("rden", [P, 2, GQA], F32)
        pT_s = put("pT_s", [P, 2 * N_SAMPLE * GQA], F32)
        st_s = put("st_s", [P, 8, 2 * N_SAMPLE], F32)
        hv_s = put("hv_s", [P, N_HEADS * HEAD], F32, rc_at)
        pick = put("pick", [P, N_SAMPLE, HEAD], F32, rs_at)
        v_row = put("v_row", [P, P], F32, v_at)
        sm_s = put("sm_s", [P, 2 * N_SAMPLE, WINDOW], F32, sm_at)
        kv_s = put("kv_s", [P, TPH, N_SAMPLE, HEAD], F32, pt_at)
        assert at[0] <= x_end, at[0] - x_end

        PS = ctx.enter_context(nc.psum_tensor("PS", [P, 8, 512], F32))

        raw_full = [sem(f"raw_full{s}") for s in range(3)]
        for n in ("consts_in w_gained w_hi_done w_ready unit_done unit_evac x_split_lo x_split_hi x_new "
                  "y_scaled sq_done ss_done var_done root_done rms_done spilled gain_done ones_done "
                  "y_zero silu_done h_ready mixc_in smp_in out_in sig_done f_done fmax_done ln_done k_done "
                  "scan_done hic_done vt_done vc_done d_done e_done gend_done qk_done lvl_done a_done kdt_done kdtc_done "
                  "o_done oc_done s_done s_scaled s_upd st_zero vst_done ropq_done kvp_done t0_done ts_done qs_done kw_shift kw_done "
                  "vw_done sc_done sm_done mx_done m_done nm_done es_ready es_done exp_done den_done rd_done p_done pt_done "
                  "ptc_done att_done attc_done mcur_done "
                  "csq_done css_done cvar_done croot_done crms_done co_done cg_done ch_done cat_hi cat_lo_a cat_lo_h y_copied "
                  "pool_held dve_held a_ps p_ps v_ps d_s a_s v_s h_hi_done h_lo_done dve_seq act_seq pool_seq cleared").split():
            sem(n)
        resid_full = [sem(f"resid_full{g}") for g in range(NG)]
        S = sems

        norms = [("S", 0, g) for g in range(NG)]
        for b in range(LAST_B + 1):
            if b < 2:
                norms += [("F", b, 0), ("F", b, 1), ("S", b + 1, 0), ("F", b, 2), ("S", b + 1, 1), ("S", b + 1, 2)]
            else:
                norms += [("F", b, g) for g in range(NG)]
        norm_no = {n: i for i, n in enumerate(norms)}
        border = {b: [n for n in norms if (n[0] == "F" and n[1] == b) or (n[0] == "S" and n[1] == b + 1)]
                  for b in range(-1, 3)}
        GAIN_F = {0: half_gain[:, 0, :], 1: vecs[:, V_GAIN["mix_post"]:V_GAIN["mix_post"] + 8], 2: half_gain[:, 1, :]}

        block = ctx.enter_context(nc.Block())

        @block.sync
        def _(sp):
            sp.dma_start(vecs[:], ins["vecs"]).then_inc(S["consts_in"], 16)
            sp.dma_start(ident[:], ins["ident"]).then_inc(S["consts_in"], 16)
            sp.dma_start(head_ones[:], ins["head_ones"]).then_inc(S["consts_in"], 16)
            for g in range(NG):
                sp.dma_start(resid[:, g], ins["x"][g]).then_inc(resid_full[g], 16)

            def load(n, s, src):
                sp.wait_ge(S["w_ready"], n + 2)
                sp.dma_start(raw[s][:], src).then_inc(raw_full[s], 16)

            def ffn_loads(w_gu, w_down, n0):
                with sp.Fori(0, FFN_STEPS) as i:
                    for o in range(4):
                        load(n0 + 6 * i + o, o % 3, w_gu[4 * i + o])
                    for o in range(2):
                        load(n0 + 6 * i + 4 + o, (4 + o) % 3, w_down[2 * i + o])

            def border_moves(b, start, residual, spill_to):
                for g in range(NG):
                    sp.wait_ge(S["unit_done"], UNIT_CREDIT + start)
                    sp.dma_start(resid[:, g], residual[g]).then_inc(resid_full[g], 16)
                for g in range(NG):
                    sp.wait_ge(S["x_new"], NG * b + g + 1)
                    sp.dma_start(spill_to[g], resid[:, g]).then_inc(S["spilled"], 16)

            ffn_loads(ins["w_gu1"], ins["w_down1"], 0)
            if LAST_B > 0:
                load(G_IN, 0, ins["w_in"][0])
                load(G_IN + 1, 1, ins["w_in"][1])
            border_moves(0, 1, ins["x"], outs["y"] if LAST_B == 0 else outs["x1"])
            if LAST_B > 0:
                sp.wait_ge(S["unit_evac"], EVAC_CREDIT + U_IN + 1)
                sp.dma_start(mixc[:], ins["mixc"]).then_inc(S["mixc_in"], 16)
                with sp.Fori(1, IN_TILES // 2) as p:
                    for o in range(2):
                        load(G_IN + 2 * p + o, o, ins["w_in"][2 * p + o])
                for o in range(2):
                    load(G_OUT + o, o, ins["w_out"][o])
                sp.wait_ge(S["unit_done"], UNIT_CREDIT + U_OUT)
                sp.dma_start(rope_c[:], ins["rope"][0]).then_inc(S["mixc_in"], 16)
                sp.dma_start(rope_s[:], ins["rope"][1]).then_inc(S["mixc_in"], 16)
                sp.wait_ge(S["scan_done"], 4 * N_CH)
                sp.dma_start(state_s[:], ins["state"]).then_inc(S["smp_in"], 16)
                sp.dma_start(k_win_s[:, :, 0:WINDOW - 1], ins["k_cache"]).then_inc(S["smp_in"], 16)
                sp.dma_start(v_win_s[0:WINDOW - 1], ins["v_cache"]).then_inc(S["smp_in"], 16)
                sp.wait_ge(S["kw_done"], N_CH + 1)
                sp.dma_start(outs["k_win"], k_win[:, CH:]).then_inc(S["out_in"], 16)
                sp.wait_ge(S["vw_done"], N_CH + 1)
                sp.dma_start(outs["v_win"], v_win[:, CH:]).then_inc(S["out_in"], 16)
                sp.wait_ge(S["s_upd"], N_CH + 1)
                sp.dma_start(outs["state"], state[:]).then_inc(S["out_in"], 16)
                sp.wait_ge(S["smp_in"], 48)
                sp.wait_ge(S["a_s"], 1)
                sp.dma_start(pick[0:N_SAMPLE], ins["pick"]).then_inc(S["smp_in"], 16)
                sp.wait_ge(S["v_ps"], 1)
                sp.dma_start(v_win_s[WINDOW - 1:WINDOW], v_row[0:N_SAMPLE]).then_inc(S["p_ps"], 16)
                sp.wait_ge(S["p_ps"], 16)
                sp.dma_start(outs["v_win_s"], v_win_s[:]).then_inc(S["out_in"], 16)
                sp.wait_ge(S["d_s"], 1)
                sp.dma_start(outs["k_win_s"], k_win_s[:]).then_inc(S["out_in"], 16)
                sp.wait_ge(S["d_s"], 2)
                sp.dma_start(outs["state_s"], state_s[:]).then_inc(S["out_in"], 16)
                with sp.Fori(1, KT // 2) as p:
                    for o in range(2):
                        load(G_OUT + 2 * p + o, o, ins["w_out"][2 * p + o])
                if LAST_B == 2:
                    load(G_FFN2, 0, ins["w_gu2"][0])
                    load(G_FFN2 + 1, 1, ins["w_gu2"][1])
                sp.wait_ge(S["spilled"], 16 * NG)
                sp.wait_ge(S["out_in"], 96)
                border_moves(1, U_OUT + 1, outs["x1"], outs["y"] if LAST_B == 1 else outs["x2"])
                if LAST_B == 2:
                    load(G_FFN2 + 2, 2, ins["w_gu2"][2])
                    load(G_FFN2 + 3, 0, ins["w_gu2"][3])
                    for o in range(2):
                        load(G_FFN2 + 4 + o, 1 + o, ins["w_down2"][o])
                    with sp.Fori(1, FFN_STEPS) as i:
                        for o in range(4):
                            load(G_FFN2 + 6 * i + o, o % 3, ins["w_gu2"][4 * i + o])
                        for o in range(2):
                            load(G_FFN2 + 6 * i + 4 + o, 1 + o, ins["w_down2"][2 * i + o])
                    sp.wait_ge(S["spilled"], 32 * NG)
                    border_moves(2, U_FFN2 + 1, outs["x2"], outs["y"])
            sp.wait_ge(S["spilled"], 16 * NG * (LAST_B + 1))

        @block.tensor
        def _(pe):
            pe.sem_inc(S["unit_done"], UNIT_CREDIT)

            def unit(g, u, pairs):
                pe.wait_ge(S["unit_evac"], u + 1)
                last = len(pairs) - 1
                for k, (w, v) in enumerate(pairs):
                    (wh, wl), (vh, vl) = w, v
                    nc.tensor.matmul(PS[:, g, :GW], wh, vh, start=(k == 0), stop=False)
                    nc.tensor.matmul(PS[:, g, :GW], wh, vl, start=False, stop=False)
                    mm = nc.tensor.matmul(PS[:, g, :GW], wl, vh, start=False, stop=(k == last))
                mm.then_inc(S["unit_done"], 1)

            def project(n, s, u):
                pe.wait_ge(S["w_ready"], READY_CREDIT + n + 1)
                for g in range(NG):
                    unit(g, u + g, [((w_hi[s][:, k * P:(k + 1) * P], w_lo[s][:, k * P:(k + 1) * P]),
                                     (x_hi[:, g, k, :], x_lo[:, g, k, :])) for k in range(KT)])

            def norm_sum(n):
                i = norm_no[n]
                pe.wait_ge(S["sq_done"], i + 1)
                if i >= 2:
                    pe.wait_ge(S["var_done"], i - 1)
                for m in range(KT):
                    mm = nc.tensor.matmul(PS[:, 3 + i % 2, :GW], ones[:], sq[:, m, :], start=(m == 0), stop=(m == KT - 1))
                mm.then_inc(S["ss_done"], 1)

            def down(g, i, u, step_h):
                pe.wait_ge(S["h_lo_done"], step_h + NG + g + 1)
                for m in range(KT):
                    unit((g * KT + m) % 3, u + 12 + g * KT + m,
                         [((w_hi[1 + t][:, m * P:(m + 1) * P], w_lo[1 + t][:, m * P:(m + 1) * P]),
                           (h[:, g, 2 * t, :], h[:, g, 2 * t + 1, :])) for t in range(2)])

            def ffn(n0, u0, f, split, b):
                pe.wait_ge(S["x_split_lo"], NG * split + NG)
                def gates(i):
                    for o in range(4):
                        project(n0 + 6 * i + o, o % 3, u0 + 36 * i + 3 * o)
                with pe.Fori(0, FFN_STEPS - 1) as i:
                    gates(i)
                    pe.wait_ge(S["w_ready"], READY_CREDIT + n0 + 6 * i + 6)
                    for g in range(NG):
                        down(g, i, u0 + 36 * i, 6 * FFN_STEPS * f + 6 * i)
                i = FFN_STEPS - 1
                gates(i)
                pe.wait_ge(S["w_ready"], READY_CREDIT + n0 + 6 * i + 6)
                down(0, i, u0 + 36 * i, 6 * FFN_STEPS * f + 6 * i)
                down(1, i, u0 + 36 * i, 6 * FFN_STEPS * f + 6 * i)
                norm_sum(("F", b, 0))
                down(2, i, u0 + 36 * i, 6 * FFN_STEPS * f + 6 * i)
                for n in border[b][1:]:
                    norm_sum(n)

            pe.wait_ge(S["ones_done"], 1)
            pe.wait_ge(S["consts_in"], 48)
            for n in border[-1]:
                norm_sum(n)
            ffn(0, 0, 0, 0, 0)
            if LAST_B == 0:
                return

            pe.wait_ge(S["x_split_lo"], 2 * NG)
            with pe.Fori(0, IN_TILES // 2) as p:
                for o in range(2):
                    project(G_IN + 2 * p + o, o, U_IN + 6 * p + 3 * o)

            def pair(j):
                return PS[:, 2 * j:2 * j + 2, :].rearrange("p a b -> p (a b)")

            def to_tokens(bank, src, first_col=0):
                for j in range(TPH):
                    mm = nc.tensor.transpose(PS[:, bank, j * P:(j + 1) * P], src[:, j, :], ident[:])
                return mm

            pe.wait_ge(S["unit_evac"], EVAC_CREDIT + U_OUT)
            pe.wait_ge(S["mixc_in"], 48)
            pe.wait_ge(S["st_zero"], 3)
            with pe.Fori(0, N_CH) as c:
                pe.wait_ge(S["hic_done"], c + 1)
                pe.wait_ge(S["attc_done"], c + 1)
                to_tokens(6, hi_c).then_inc(S["vt_done"], 1)
                for l in range(5):
                    pe.wait_ge(S["qk_done"], 12 + 12 * c + 3 + 2 * l)
                    if l == 1:
                        pe.wait_ge(S["ptc_done"], 2 + 2 * c - 1)
                    if l == 2:
                        pe.wait_ge(S["ptc_done"], 2 + 2 * c)
                    if l >= 3:
                        pe.wait_ge(S["a_done"], 5 * c + l - 2)
                    for hd in range(N_HEADS):
                        p0, t = HEAD * (hd % 2), hd // 2
                        mm = nc.tensor.matmul(PS[:, 2 * (l % 3) + hd % 2, t * CH:(t + 1) * CH], k_dec[p0:p0 + HEAD, l % 2, t, :],
                                              q_dec[p0:p0 + HEAD, l % 2, t, :], start=True, stop=True)
                    mm.then_inc(S["lvl_done"], 1)
                pe.wait_ge(S["qk_done"], 12 + 12 * c + 12)
                pe.wait_ge(S["vw_done"], c + VW_CREDIT)
                pe.wait_ge(S["kw_done"], c + KW_CREDIT)
                to_tokens(7, kd).then_inc(S["kdt_done"], 1)
                pe.wait_ge(S["vc_done"], c + 1)
                pe.wait_ge(S["a_done"], 5 * c + 5)
                pe.wait_ge(S["s_upd"], c + 1)
                for hd in range(N_HEADS):
                    p0, t = HEAD * (hd % 2), hd // 2
                    nc.tensor.matmul(PS[p0:p0 + HEAD, 6, t * CH:(t + 1) * CH], V[:, hd * HEAD:(hd + 1) * HEAD],
                                     A[:, TPH * (hd % 2) + t, :], start=True, stop=False)
                    mm = nc.tensor.matmul(PS[p0:p0 + HEAD, 6, t * CH:(t + 1) * CH], state[p0:p0 + HEAD, t, :],
                                          qg[p0:p0 + HEAD, t, :], start=False, stop=True)
                mm.then_inc(S["o_done"], 1)
                pe.wait_ge(S["kdtc_done"], c + 1)
                for hd in range(N_HEADS):
                    p0, t = HEAD * (hd % 2), hd // 2
                    mm = nc.tensor.matmul(PS[p0:p0 + HEAD, 7, t * HEAD:(t + 1) * HEAD], kdT[:, hd * HEAD:(hd + 1) * HEAD],
                                          V[:, hd * HEAD:(hd + 1) * HEAD], start=True, stop=True)
                mm.then_inc(S["s_done"], 1)
                pe.wait_ge(S["oc_done"], c + 1)
                nc.tensor.matmul(PS[:, 6, :], mixc[:, M_ROT:M_ROT + P], chunk(3, c),
                                 start=True, stop=True).then_inc(S["ropq_done"], 1)
                pe.wait_ge(S["s_upd"], c + 2)
                pe.wait_ge(S["vst_done"], c + 1)
                nc.tensor.matmul(PS[:, 7, 0:CH], mixc[:, M_ROT:M_ROT + P], kv[:, 0, bass.ds(c * CH, CH)], start=True, stop=True)
                nc.tensor.transpose(PS[:, 7, CH:2 * CH], v_c[:], ident[:]).then_inc(S["kvp_done"], 1)
                pe.wait_ge(S["qs_done"], c + 1)
                pe.wait_ge(S["kw_done"], c + 1 + KW_CREDIT)
                for n in range(2):
                    j2 = (5 + n) % 3
                    pe.wait_ge(S["a_done"], 5 * c + 3 + n)
                    for j in range(GQA):
                        mm = nc.tensor.matmul(pair(j2)[:, j * 2 * CH:(j + 1) * 2 * CH], q_rot[HEAD * n:HEAD * (n + 1), j, :],
                                              k_win[HEAD * n:HEAD * (n + 1), :], start=True, stop=True)
                    mm.then_inc(S["sc_done"], 1)
                for n in range(2):
                    j2 = (7 + n) % 3
                    pe.wait_ge(S["p_done"], 2 * c + n + 1)
                    if n == 0:
                        pe.wait_ge(S["a_done"], 5 * c + 5)
                    else:
                        pe.wait_ge(S["sm_done"], 2 * c + 1)
                    for b in range(2 * GQA):
                        mm = nc.tensor.transpose(pair(j2)[:, b * CH:(b + 1) * CH], sm[:, n, b * CH:(b + 1) * CH], ident[:])
                    mm.then_inc(S["pt_done"], 1)
                pe.wait_ge(S["ts_done"], 2 * c + 1)
                pe.wait_ge(S["vw_done"], c + 1 + VW_CREDIT)
                for n in range(2):
                    pe.wait_ge(S["ptc_done"], 2 + 2 * c + n + 1)
                    for half in range(2):
                        mm = nc.tensor.matmul(PS[HEAD * n:HEAD * (n + 1), 6, :], v_win[:, half * CH + HEAD * n:half * CH + HEAD * (n + 1)],
                                              pT[:, n, :].rearrange("p (j a t) -> p a j t", j=GQA, a=2)[:, half],
                                              start=(half == 0), stop=(half == 1))
                    mm.then_inc(S["att_done"], 1)

            ST = slice(N_PROMPT, TOK)
            pe.wait_ge(S["attc_done"], N_CH + 1)
            pe.wait_ge(S["s_upd"], N_CH + 1)
            pe.wait_ge(S["vw_done"], N_CH + VW_CREDIT)
            pe.wait_ge(S["kw_done"], N_CH + KW_CREDIT)
            nc.tensor.matmul(PS[:, 6, 0:TPH * N_SAMPLE], mixc[:, M_ROT:M_ROT + P], q_reg[:, :, ST], start=True, stop=True)
            nc.tensor.matmul(PS[:, 6, 32:32 + N_SAMPLE], mixc[:, M_ROT:M_ROT + P], kv[:, 0, ST], start=True, stop=True)
            nc.tensor.transpose(PS[0:N_SAMPLE, 7, 0:P], kv[:, 1, ST], ident[:])
            for j in range(TPH):
                tr = nc.tensor.transpose(PS[0:N_SAMPLE, 5, j * P:(j + 1) * P], hi_reg[:, j, ST], ident[:])
            tr.then_inc(S["a_s"], 1)
            pe.wait_ge(S["v_ps"], 2)
            pe.wait_ge(S["smp_in"], 64)
            for b in range(N_SAMPLE):
                for o in range(2):
                    mm = nc.tensor.matmul(PS[HEAD * o:HEAD * (o + 1), b // 2, 256 * (b % 2):256 * (b % 2) + 256],
                                          pick[0:N_SAMPLE, b, :],
                                          hv_s[0:N_SAMPLE, :].rearrange("b (t o v) -> b o t v", o=2, v=HEAD)[:, o],
                                          start=True, stop=True)
            mm.then_inc(S["a_s"], 1)
            pe.wait_ge(S["d_s"], 1)
            pe.wait_ge(S["a_ps"], 1)
            for n in range(2):
                for b in range(N_SAMPLE):
                    at_ = n * N_SAMPLE + b
                    mm = nc.tensor.matmul(PS[0:GQA, at_ // 4, CH * (at_ % 4):CH * (at_ % 4) + CH],
                                          q_s[HEAD * n:HEAD * (n + 1), :, b], k_win_s[HEAD * n:HEAD * (n + 1), b, :],
                                          start=True, stop=True)
            mm.then_inc(S["a_s"], 1)
            pe.wait_ge(S["d_s"], 2)
            for b in range(N_SAMPLE):
                for hd in range(N_HEADS):
                    p0, t = HEAD * (hd % 2), hd // 2
                    mm = nc.tensor.matmul(PS[p0:p0 + HEAD, 7, t * N_SAMPLE + b:t * N_SAMPLE + b + 1],
                                          state_s[p0:p0 + HEAD, t, b, :], hq_reg[p0:p0 + HEAD, t, N_PROMPT + b:N_PROMPT + b + 1],
                                          start=True, stop=True)
            mm.then_inc(S["a_s"], 1)
            pe.wait_ge(S["d_s"], 3)
            for at_ in range(2 * N_SAMPLE):
                mm = nc.tensor.transpose(PS[:, 4, at_ * GQA:(at_ + 1) * GQA], sm_s[0:GQA, at_, :], ident[0:GQA, 0:GQA])
            mm.then_inc(S["a_s"], 1)
            pe.wait_ge(S["v_ps"], 3)
            pe.wait_ge(S["p_ps"], 16)
            for n in range(2):
                for b in range(N_SAMPLE):
                    at_ = n * N_SAMPLE + b
                    mm = nc.tensor.matmul(PS[HEAD * n:HEAD * (n + 1), 5, :].rearrange("p (x j b) -> p x j b", x=16, b=N_SAMPLE)[:, 0, :, b],
                                          v_win_s[:, b, HEAD * n:HEAD * (n + 1)], pT_s[:, at_ * GQA:(at_ + 1) * GQA],
                                          start=True, stop=True)
            mm.then_inc(S["a_s"], 1)

            for g in range(NG):
                pe.wait_ge(S["csq_done"], g + 1)
                if g == 0:
                    pe.wait_ge(S["v_ps"], 5)
                else:
                    pe.wait_ge(S["cvar_done"], g)
                for j in range(TPH):
                    mm = nc.tensor.matmul(PS[:, 3 + j, :GW], head_ones[:], c_sq[:, j, :], start=True, stop=True)
                mm.then_inc(S["css_done"], 1)

            pe.wait_ge(S["cat_lo_a"], NG)
            pe.wait_ge(S["cat_lo_h"], NG)
            with pe.Fori(0, KT // 2) as p:
                for o in range(2):
                    project(G_OUT + 2 * p + o, o, U_OUT + 6 * p + 3 * o)
            for n in border[1]:
                norm_sum(n)
            if LAST_B == 2:
                ffn(G_FFN2, U_FFN2, 1, 2, 2)

        @block.gpsimd
        def _(pool):
            nc.gpsimd.memset(ones[:], 1.0).then_inc(S["ones_done"], 1)

            def gain(s, use, col):
                pool.wait_ge(raw_full[s], 16 * use + 16)
                wv = raw[s][:].rearrange("p (k c) -> p k c", k=KT)
                gv = vecs[:, col:col + KT].unsqueeze(2).broadcast_to([P, KT, P])
                nc.gpsimd.tensor_tensor(wv, wv, gv, ALU.mult).then_inc(S["w_gained"], 1)

            def split_lo(n):
                _, b, g = n
                pool.wait_ge(S["x_split_hi"], NG * b + g + 1)
                nc.gpsimd.tensor_tensor(x_lo[:, g], resid[:, g], x_hi[:, g].bitcast(F32), ALU.subtract)\
                    .then_inc(S["x_split_lo"], 1)

            def border_pool(b):
                for n in border[b]:
                    if n[0] == "S":
                        split_lo(n)

            pool.wait_ge(S["consts_in"], 48)
            nc.gpsimd.memset(y[:], 0.0).then_inc(S["y_zero"], 1)
            gain(0, 0, V_GAIN["ffn1_pre"])
            gain(1, 0, V_GAIN["ffn1_pre"])
            border_pool(-1)
            gain(2, 0, V_GAIN["ffn1_pre"])
            gain(0, 1, V_GAIN["ffn1_pre"])
            with pool.Fori(1, FFN_STEPS) as i:
                for o in range(4):
                    gain(o % 3, 2 * i + o // 3, V_GAIN["ffn1_pre"])
            if LAST_B > 0:
                gain(0, 22, V_GAIN["mix_pre"])
            border_pool(0)
            if LAST_B == 0:
                return
            with pool.Fori(0, IN_TILES // 2 - 1) as p:
                gain(1, G_IN // 3 + p, V_GAIN["mix_pre"])
                gain(0, G_IN // 3 + 1 + p, V_GAIN["mix_pre"])
            gain(1, G_IN // 3 + IN_TILES // 2 - 1, V_GAIN["mix_pre"])
            pool.wait_ge(S["unit_done"], UNIT_CREDIT + U_OUT)
            nc.gpsimd.memset(state[:], 0.0).then_inc(S["st_zero"], 1)
            nc.gpsimd.memset(k_win[:], 0.0).then_inc(S["st_zero"], 1)
            nc.gpsimd.memset(v_win[:], 0.0).then_inc(S["st_zero"], 1)
            pool.sem_inc(S["qk_done"], 12)
            pool.wait_ge(S["fmax_done"], 1)
            pool.wait_ge(S["mixc_in"], 48)
            pool.wait_ge(S["unit_evac"], EVAC_CREDIT + U_OUT)
            pool.wait_ge(S["st_zero"], 3)
            hq_of = lambda c: chunk(1, c)
            kg_of = lambda c: k_gate[:, :, bass.ds(c * CH, CH)]
            def held():
                pool.sem_inc(S["pool_held"], 1)

            with pool.Fori(0, N_CH) as c:
                pool.wait_ge(S["e_done"], 8 + 8 * c + 1)
                pool.wait_ge(S["o_done"], c + 1)
                held()
                nc.gpsimd.tensor_tensor(qg[:], hq_of(c), dec[:, 0], ALU.mult).then_inc(S["qk_done"], 1)
                for l in range(5):
                    pool.wait_ge(S["lvl_done"], (5 + 5 * c + l - 1) if l >= 2 else (5 * c + 5 - l))
                    eq, ek = (1, 2) if l == 0 else (2 + l, 2 + l)
                    pool.wait_ge(S["e_done"], 8 + 8 * c + eq + 1)
                    held()
                    nc.gpsimd.tensor_tensor(q_dec[:, l % 2], hq_of(c), dec[:, eq % 2], ALU.mult).then_inc(S["qk_done"], 1)
                    pool.wait_ge(S["e_done"], 8 + 8 * c + ek + 1)
                    held()
                    nc.gpsimd.tensor_tensor(k_dec[:, l % 2], kg_of(c), dec[:, ek % 2], ALU.mult).then_inc(S["qk_done"], 1)
                pool.wait_ge(S["e_done"], 8 + 8 * c + 8)
                pool.wait_ge(S["kdt_done"], c + 1)
                held()
                nc.gpsimd.tensor_tensor(kd[:], kg_of(c), dec[:, 1], ALU.mult).then_inc(S["qk_done"], 1)
                pool.wait_ge(S["ts_done"], 2 * c + 2)
                held()
                nc.gpsimd.tensor_tensor(rot_c[:], chunk(3, c),
                                        rope_c[:, bass.ds(c * CH, CH)].unsqueeze(1).broadcast_to([P, TPH, CH]),
                                        ALU.mult).then_inc(S["t0_done"], 1)
                nc.gpsimd.tensor_tensor(rotk_c[:], kv[:, 0, bass.ds(c * CH, CH)], rope_c[:, bass.ds(c * CH, CH)],
                                        ALU.mult).then_inc(S["t0_done"], 1)
                pool.wait_ge(S["att_done"], 2 * c + 2)
                held()
                nc.gpsimd.tensor_copy(k_win[:, 0:CH], k_win[:, CH:]).then_inc(S["kw_shift"], 1)
                nc.gpsimd.tensor_copy(v_win[:, 0:CH], v_win[:, CH:]).then_inc(S["kw_shift"], 1)
                for n in range(2):
                    pool.wait_ge(S["rd_done"], 2 * c + n + 1)
                    pv = sm[:, n, :].rearrange("p (j t) -> p j t", j=GQA)
                    nc.gpsimd.tensor_tensor(pv, pv, rden[:, n, :].unsqueeze(2).broadcast_to([P, GQA, 2 * CH]),
                                            ALU.mult).then_inc(S["p_done"], 1)
            for g in range(NG):
                pool.wait_ge(S["cat_hi"], 2 * g + 1)
                nc.gpsimd.tensor_tensor(x_lo[:, g, 0:TPH], q_reg[:, :, g * GW:(g + 1) * GW],
                                        x_hi[:, g, 0:TPH].bitcast(F32), ALU.subtract).then_inc(S["cat_lo_a"], 1)
            if LAST_B == 2:
                gain(0, 37, V_GAIN["ffn2_pre"])
                gain(1, 37, V_GAIN["ffn2_pre"])
            border_pool(1)
            if LAST_B == 2:
                pool.wait_ge(S["x_new"], 2 * NG)
                nc.gpsimd.memset(y[:], 0.0).then_inc(S["y_zero"], 1)
                gain(2, 22, V_GAIN["ffn2_pre"])
                gain(0, 38, V_GAIN["ffn2_pre"])
                with pool.Fori(1, FFN_STEPS) as i:
                    for o in range(4):
                        gain(o % 3, (22 if o == 2 else 37) + 2 * i + o // 3, V_GAIN["ffn2_pre"])

        @block.scalar
        def _(act):
            def split_hi(s, n_gained, use, prior_unit):
                if n_gained is None:
                    act.wait_ge(raw_full[s], 16 * use + 16)
                else:
                    act.wait_ge(S["w_gained"], n_gained)
                act.wait_ge(S["unit_done"], UNIT_CREDIT + prior_unit)
                nc.scalar.activation(w_hi[s][:], raw[s][:], ACT.Copy).then_inc(S["w_hi_done"], 1)

            def square(n, src):
                i = norm_no[n]
                if i >= 1:
                    act.wait_ge(S["ss_done"], i)
                nc.scalar.activation(sq[:], src, ACT.Square).then_inc(S["sq_done"], 1)

            def take_root(n):
                i = norm_no[n]
                act.wait_ge(S["var_done"], i + 1)
                nc.scalar.activation(root[:, i % 2, :], root[:, i % 2, :], ACT.Sqrt).then_inc(S["root_done"], 1)

            def border_act(b, y_evac):
                for n in border[b]:
                    kind, c, g = n
                    if kind == "F":
                        act.wait_ge(S["unit_evac"], EVAC_CREDIT + y_evac[g])
                        square(n, y[:, g])
                    else:
                        if b < 0:
                            act.wait_ge(resid_full[g], 16)
                        else:
                            act.wait_ge(S["x_new"], NG * b + g + 1)
                        nc.scalar.activation(x_hi[:, g], resid[:, g], ACT.Copy).then_inc(S["x_split_hi"], 1)
                        square(n, resid[:, g])
                    take_root(n)

            def ffn(n0, u0, f, slot_uses, gained0, before_first, b, nxt):
                def silus(i, t):
                    for g in range(NG):
                        act.wait_ge(S["unit_evac"], EVAC_CREDIT + u0 + 36 * i + 6 * t + g + 1)
                        nc.scalar.activation(silu_g[:, g], silu_g[:, g], ACT.Silu).then_inc(S["silu_done"], 1)

                def h_his(i, t):
                    for g in range(NG):
                        act.wait_ge(S["h_ready"], 6 * FFN_STEPS * f + 6 * i + 3 * t + g + 1)
                        if t == 0 and g == 0:
                            act.wait_ge(S["unit_done"], UNIT_CREDIT + u0 + 36 * i)
                        nc.scalar.activation(h[:, g, 2 * t, :], prod[:, g], ACT.Copy).then_inc(S["h_hi_done"], 1)

                def step(i, last):
                    u = u0 + 36 * i
                    g0 = gained0 + 4 * i
                    use = lambda s, k: slot_uses[s] + 2 * i + k
                    split_hi(1, g0 + 2, use(1, 0), u)
                    silus(i, 0)
                    split_hi(2, g0 + 3, use(2, 0), u)
                    h_his(i, 0)
                    split_hi(0, g0 + 4, use(0, 1), u + 3)
                    silus(i, 1)
                    split_hi(1, None, use(1, 1), u + 6)
                    split_hi(2, None, use(2, 1), u + 9)
                    h_his(i, 1)
                    if not last:
                        split_hi(0, g0 + 5, use(0, 2), u + 12)
                    elif nxt is not None:
                        split_hi(0, g0 + 5, use(0, 2), u + 12)

                if before_first is not None:
                    split_hi(0, gained0 + 1, slot_uses[0], before_first)
                with act.Fori(0, FFN_STEPS - 1) as i:
                    step(i, False)
                step(FFN_STEPS - 1, True)
                border_act(b, [u0 + 36 * (FFN_STEPS - 1) + 12 + KT * (g + 1) for g in range(NG)])

            act.wait_ge(S["dve_seq"], 3)
            nc.scalar.activation(lb[:, 0:2], lb[:, 0:2], ACT.Exp).then_inc(S["cleared"], 1)
            border_act(-1, None)
            ffn(0, 0, 0, [0, 0, 0], 0, -24, 0, None if LAST_B == 0 else 1)
            if LAST_B == 0:
                return

            def in_hi(n, s, use):
                split_hi(s, 44 + n + 1, use, U_IN + 3 * (n - 1))

            def in_his(p):
                in_hi(2 * p + 1, 1, 22 + p)
                in_hi(2 * p + 2, 0, 23 + p)

            with act.Fori(0, 2) as p:
                in_his(p)
            act.wait_ge(S["unit_evac"], EVAC_CREDIT + U_IN + 3 * TPH)
            nc.scalar.activation(f_reg, f_reg, ACT.Sigmoid).then_inc(S["sig_done"], 1)
            in_hi(5, 1, 24)
            in_hi(6, 0, 25)
            act.wait_ge(S["fmax_done"], 1)
            nc.scalar.activation(f_reg, f_reg, ACT.Ln).then_inc(S["ln_done"], 1)
            with act.Fori(3, IN_TILES // 2 - 1) as p:
                in_his(p)
            in_hi(IN_TILES - 1, 1, 22 + IN_TILES // 2 - 1)
            split_hi(0, None, 22 + IN_TILES // 2, U_IN + 3 * (IN_TILES - 1))

            act.sem_inc(S["e_done"], 8)
            act.sem_inc(S["ptc_done"], 2)
            act.sem_inc(S["attc_done"], 1)
            act.sem_inc(S["vw_done"], VW_CREDIT)
            act.wait_ge(S["unit_evac"], EVAC_CREDIT + U_OUT)
            act.wait_ge(S["st_zero"], 3)
            READS = [1, 2, 3, 5, 7, 9, 11, 12]
            with act.Fori(0, N_CH) as c:
                act.wait_ge(S["vt_done"], c + VT_CREDIT)
                nc.scalar.activation(hi_c[:], chunk(2, c), ACT.Copy).then_inc(S["hic_done"], 1)

                def decay(e, out, src, scale):
                    act.wait_ge(S["qk_done"], 12 + 12 * c + READS[e - 2] if e >= 2 else 12 * c + READS[6 + e])
                    nc.scalar.activation(out, src, ACT.Exp, scale=scale).then_inc(S["e_done"], 1)

                act.wait_ge(S["scan_done"], 4 * c + 4)
                decay(0, dec[:, 0], G[:], 1.0)
                act.wait_ge(S["s_upd"], c + 1)
                nc.scalar.activation(g_end[:], G[:, :, CH - 1], ACT.Exp).then_inc(S["gend_done"], 1)
                act.wait_ge(S["d_done"], 10 * c + 1)
                decay(1, dec[:, 1], dif[:, 0], 1.0)
                decay(2, dec[:, 0], dif[:, 0], -1.0)
                act.wait_ge(S["vt_done"], c + VT_CREDIT + 1)
                act.wait_ge(S["s_done"], c + SD_CREDIT)
                nc.scalar.activation(V[:], PS[:, 6, :], ACT.Copy).then_inc(S["vc_done"], 1)
                for l in range(1, 5):
                    act.wait_ge(S["d_done"], 10 * c + 1 + 2 * l)
                    decay(2 + l, dec[:, (2 + l) % 2], dif[:, l % 2], 1.0)
                act.wait_ge(S["d_done"], 10 * c + 10)
                decay(7, dec[:, 1], dif[:, 1], 1.0)
                act.wait_ge(S["kdt_done"], c + 2)
                nc.scalar.activation(kdT[:], PS[:, 7, :], ACT.Copy).then_inc(S["kdtc_done"], 1)
                act.wait_ge(S["kvp_done"], c + 1)
                nc.scalar.activation(v_c[:], kv[:, 1, bass.ds(c * CH, CH)], ACT.Copy).then_inc(S["vst_done"], 1)
                act.wait_ge(S["o_done"], c + 2)
                nc.scalar.activation(chunk(1, c), PS[:, 6, :].rearrange("p (t c) -> p t c", t=TPH),
                                     ACT.Copy).then_inc(S["oc_done"], 1)
                act.wait_ge(S["kvp_done"], c + 2)
                act.wait_ge(S["kw_shift"], 2 * c + 2)
                nc.scalar.activation(v_win[:, CH:], PS[:, 7, CH:2 * CH], ACT.Copy).then_inc(S["vw_done"], 1)
                for n in range(2):
                    act.wait_ge(S["es_ready"], 2 * c + n + 1)
                    nc.scalar.activation(es[:, n, :], es[:, n, :], ACT.Exp).then_inc(S["es_done"], 1)
                    for j in range(GQA):
                        cols = sm[:, n, j * 2 * CH:(j + 1) * 2 * CH]
                        last = nc.scalar.activation(cols, cols, ACT.Exp, bias=nm[:, n, j:j + 1], accum_out=rsum[:, n, j:j + 1])
                    last.then_inc(S["exp_done"], 1)
                for n in range(2):
                    act.wait_ge(S["pt_done"], 2 * c + n + 1)
                    act.wait_ge(S["att_done"], 2 * c + n + 1)
                    nc.scalar.activation(pT[:, n, :], PS[:, 2 * ((7 + n) % 3):2 * ((7 + n) % 3) + 2, :].rearrange("p a b -> p (a b)"),
                                         ACT.Copy).then_inc(S["ptc_done"], 1)
                act.wait_ge(S["att_done"], 2 * c + 4)
                nc.scalar.activation(chunk(3, c), PS[:, 6, :].rearrange("p (t c) -> p t c", t=TPH),
                                     ACT.Copy).then_inc(S["attc_done"], 1)

            ST = slice(N_PROMPT, TOK)
            act.wait_ge(S["a_s"], 1)
            nc.scalar.activation(v_row[0:N_SAMPLE], PS[0:N_SAMPLE, 7, 0:P], ACT.Copy).then_inc(S["v_ps"], 1)
            nc.scalar.activation(hv_s[0:N_SAMPLE], PS[0:N_SAMPLE, 5, :], ACT.Copy).then_inc(S["v_ps"], 1)
            act.wait_ge(S["v_s"], 1)
            nc.scalar.activation(st_s[0:GQA, 3, :], st_s[0:GQA, 3, :], ACT.Exp).then_inc(S["sig_done"], 1)
            nc.scalar.activation(sm_s[0:GQA], sm_s[0:GQA], ACT.Exp).then_inc(S["sig_done"], 1)
            act.wait_ge(S["a_s"], 5)
            nc.scalar.activation(pT_s[:], PS[:, 4, 0:2 * N_SAMPLE * GQA], ACT.Copy).then_inc(S["v_ps"], 1)
            nc.scalar.activation(hq_reg[:, :, ST], PS[:, 7, 0:TPH * N_SAMPLE].rearrange("p (t b) -> p t b", t=TPH),
                                 ACT.Copy).then_inc(S["v_ps"], 1)
            act.wait_ge(S["a_s"], 6)
            nc.scalar.activation(q_reg[:, :, ST], PS[:, 5, 0:TPH * N_SAMPLE].rearrange("p (t b) -> p t b", t=TPH),
                                 ACT.Copy).then_inc(S["v_ps"], 1)

            act.wait_ge(S["v_ps"], 5)
            gs = lambda r, g: r[:, :, g * GW:(g + 1) * GW]
            for g in range(NG):
                if g >= 1:
                    act.wait_ge(S["css_done"], g)
                nc.scalar.activation(c_sq[:], gs(hq_reg, g), ACT.Square).then_inc(S["csq_done"], 1)
                nc.scalar.activation(x_hi[:, g, 0:TPH], gs(q_reg, g), ACT.Copy).then_inc(S["cat_hi"], 1)
                act.wait_ge(S["cvar_done"], g + 1)
                nc.scalar.activation(c_root[:], c_root[:], ACT.Sqrt).then_inc(S["croot_done"], 1)
                nc.scalar.activation(gs(hg_reg, g), gs(hg_reg, g), ACT.Silu).then_inc(S["cg_done"], 1)
                act.wait_ge(S["ch_done"], g + 1)
                nc.scalar.activation(x_hi[:, g, TPH:], gs(hq_reg, g), ACT.Copy).then_inc(S["cat_hi"], 1)

            split_hi(1, None, 33, U_OUT)
            with act.Fori(1, KT // 2) as p:
                split_hi(0, None, 33 + p, U_OUT + 6 * p - 3)
                split_hi(1, None, 33 + p, U_OUT + 6 * p)
            if LAST_B == 2:
                split_hi(0, 67, 37, U_FFN2 - 3)
            border_act(1, [U_FFN2] * NG)
            if LAST_B == 2:
                ffn(G_FFN2, U_FFN2, 1, [37, 37, 22], 66, None, 2, None)

        @block.vector
        def _(dve):
            seq = Seq(dve, S["dve_seq"])
            dve.sem_inc(S["unit_evac"], EVAC_CREDIT)
            dve.sem_inc(S["w_ready"], READY_CREDIT)
            dve.wait_ge(S["consts_in"], 48)
            for j, name in enumerate(("ffn1_post", "ffn2_post")):
                nc.vector.tensor_scalar(half_gain[:, j, :], vecs[:, V_GAIN[name]:V_GAIN[name] + 8], 0.5, None, ALU.mult)\
                    .then_inc(S["gain_done"], 1)
            dve.wait_ge(S["gain_done"], 2)

            def split_lo(n, s):
                dve.wait_ge(S["w_hi_done"], n + 1)
                nc.vector.tensor_tensor(w_lo[s][:], raw[s][:], w_hi[s][:].bitcast(F32), ALU.subtract)\
                    .then_inc(S["w_ready"], 1)

            def norm_tail(n):
                i = norm_no[n]
                kind, b, g = n
                dve.wait_ge(S["ss_done"], i + 1)
                if i >= 2:
                    dve.wait_ge(S["rms_done"], i - 1)
                nc.vector.tensor_scalar(root[:, i % 2, :], PS[:, 3 + i % 2, :GW], 1.0 / D_MODEL, EPS, ALU.mult, ALU.add)\
                    .then_inc(S["var_done"], 1)
                dve.wait_ge(S["root_done"], i + 1)
                dst = rms[:, g, :] if kind == "S" else rms_y[:, i % 2, :]
                nc.vector.reciprocal(dst, root[:, i % 2, :]).then_inc(S["rms_done"], 1)

            def finish(n):
                _, b, g = n
                i = norm_no[n]
                q = NG * b + g
                dve.wait_ge(S["rms_done"], i + 1)
                rb = rms_y[:, i % 2, :].unsqueeze(1).broadcast_to([P, KT, GW])
                nc.vector.tensor_tensor(y[:, g], y[:, g], rb, ALU.mult).then_inc(S["y_scaled"], 1)
                dve.wait_ge(S["y_scaled"], q + 1)
                dve.wait_ge(resid_full[g], 16 * (b + 2))
                for m in range(KT):
                    st = nc.vector.scalar_tensor_tensor(resid[:, g, m, :], y[:, g, m, :], GAIN_F[b][:, m:m + 1],
                                                        resid[:, g, m, :], ALU.mult, ALU.add)
                st.then_inc(S["x_new"], 1)

            def border_dve(b):
                for n in border[b]:
                    norm_tail(n)
                    if n[0] == "F":
                        finish(n)
                dve.wait_ge(S["rms_done"], norm_no[border[b][-1]] + 1)

            def ffn(n0, u0, f, b, nxt):
                def evac(u):
                    dve.wait_ge(S["unit_done"], UNIT_CREDIT + u + 1)

                def step(i, last):
                    u, n = u0 + 36 * i, n0 + 6 * i
                    for t in range(2):
                        split_lo(n + 2 * t + 1, (2 * t + 1) % 3)
                        for g in range(NG):
                            evac(u + 6 * t + g)
                            nc.vector.tensor_tensor(silu_g[:, g], PS[:, g, :GW], rms[:, g], ALU.mult).then_inc(S["unit_evac"], 1)
                        split_lo(n + 2 * t + 2, (2 * t + 2) % 3)
                        if t == 1:
                            split_lo(n + 5, 2)
                        for g in range(NG):
                            evac(u + 6 * t + 3 + g)
                            nc.vector.tensor_tensor(prod[:, g], PS[:, g, :GW], rms[:, g], ALU.mult).then_inc(S["unit_evac"], 1)
                            dve.wait_ge(S["unit_evac"], EVAC_CREDIT + u + 6 * t + 3 + g + 1)
                            dve.wait_ge(S["silu_done"], 6 * FFN_STEPS * f + 6 * i + 3 * t + g + 1)
                            nc.vector.tensor_tensor(prod[:, g], prod[:, g], silu_g[:, g], ALU.mult).then_inc(S["h_ready"], 1)
                        for g in range(NG):
                            dve.wait_ge(S["h_hi_done"], 6 * FFN_STEPS * f + 6 * i + 3 * t + g + 1)
                            nc.vector.tensor_tensor(h[:, g, 2 * t + 1, :], prod[:, g], h[:, g, 2 * t, :].bitcast(F32),
                                                    ALU.subtract).then_inc(S["h_lo_done"], 1)
                    if not last or nxt:
                        split_lo(n + 6, 0)
                    for d in range(NG * KT):
                        g, m = d // KT, d % KT
                        evac(u + 12 + d)
                        nc.vector.tensor_tensor(y[:, g, m, :], y[:, g, m, :], PS[:, d % 3, :GW], ALU.add).then_inc(S["unit_evac"], 1)

                if f == 0:
                    split_lo(n0, 0)
                dve.wait_ge(S["y_zero"], f + 1)
                with dve.Fori(0, FFN_STEPS - 1) as i:
                    step(i, False)
                step(FFN_STEPS - 1, True)
                border_dve(b)

            seq(nc.vector.tensor_tensor(lb[:, 0], vecs[:, V_LB0:V_LB0 + TPH], vecs[:, V_LB1:V_LB1 + TPH], ALU.max))
            seq(nc.vector.tensor_tensor(lb[:, 1], vecs[:, V_LB1:V_LB1 + TPH], lb[:, 0], ALU.subtract))
            seq(nc.vector.tensor_tensor(lb[:, 0], vecs[:, V_LB0:V_LB0 + TPH], lb[:, 0], ALU.subtract))
            dve.wait_ge(S["cleared"], 1)
            seq(nc.vector.tensor_tensor(lb[:, 2], lb[:, 0], lb[:, 1], ALU.add))
            seq(nc.vector.reciprocal(lb[:, 2], lb[:, 2]))
            seq(nc.vector.tensor_tensor(lb[:, 0], lb[:, 0], lb[:, 2], ALU.mult))
            seq(nc.vector.tensor_scalar(lb[:, 1], lb[:, 0], -1.0, 1.0, ALU.mult, ALU.add))

            border_dve(-1)
            ffn(0, 0, 0, 0, LAST_B > 0)
            if LAST_B == 0:
                return

            def in_tile(n, o, dst, scale, split=True):
                if split:
                    split_lo(G_IN + n + 1, 1 - o)
                for g in range(NG):
                    dve.wait_ge(S["unit_done"], UNIT_CREDIT + U_IN + 3 * n + g + 1)
                    if scale is None:
                        ev = nc.vector.tensor_tensor(dst(g), PS[:, g, :GW], rms[:, g], ALU.mult)
                    else:
                        ev = nc.vector.scalar_tensor_tensor(dst(g), PS[:, g, :GW], scale, rms[:, g], ALU.mult, ALU.mult)
                    ev.then_inc(S["unit_evac"], 1)

            def in_pair(p, scale=None):
                for o in range(2):
                    in_tile(2 * p + o, o, lambda g: R[:, 2 * p + o, g * GW:(g + 1) * GW], scale)

            with dve.Fori(0, 2) as p:
                in_pair(p)
            dve.wait_ge(S["sig_done"], 1)
            dve.wait_ge(S["spilled"], 16 * NG)
            for j in range(TPH):
                last = nc.vector.tensor_scalar(f_reg[:, j], f_reg[:, j], lb[:, 1, j:j + 1], lb[:, 0, j:j + 1], ALU.mult, ALU.add)
            seq(last)
            nc.vector.tensor_copy(f_s[:], f_reg[:, :, N_PROMPT:])
            seq(nc.vector.tensor_scalar(k_gate[:], f_reg, -1.0, 1.0, ALU.mult, ALU.add))
            nc.vector.tensor_scalar(f_reg, f_reg, F_MIN, None, ALU.max).then_inc(S["fmax_done"], 1)
            with dve.Fori(2, 4) as p:
                in_pair(p, HEAD ** -0.5)
            with dve.Fori(4, IN_TILES // 2 - 1) as p:
                in_pair(p)
            for o in range(2):
                in_tile(IN_TILES - 2 + o, o, lambda g: kv[:, o, g * GW:(g + 1) * GW], None)

            dve.sem_inc(S["lvl_done"], 5)
            dve.sem_inc(S["gend_done"], GE_CREDIT)
            dve.sem_inc(S["o_done"], 1)
            dve.sem_inc(S["kdt_done"], 1)
            dve.sem_inc(S["s_upd"], 1)
            dve.sem_inc(S["vt_done"], VT_CREDIT)
            dve.sem_inc(S["s_done"], SD_CREDIT)
            dve.sem_inc(S["kvp_done"], 1)
            dve.sem_inc(S["att_done"], 2)
            dve.sem_inc(S["ts_done"], 2)
            dve.sem_inc(S["kw_done"], KW_CREDIT)
            dve.wait_ge(S["mixc_in"], 48)
            dve.wait_ge(S["ln_done"], 1)
            dve.wait_ge(S["st_zero"], 3)
            DREADS = [3, 4, 5, 6, 7, 8]

            with dve.Fori(0, N_CH) as c:
                seq.enter(c, 9)
                tok = bass.ds(c * CH, CH)
                dve.wait_ge(S["gend_done"], c + GE_CREDIT)
                for j in range(TPH):
                    nc.vector.tensor_tensor_scan(G[:, j], ones[:], R[:, j, tok], 0.0, ALU.mult, ALU.add)\
                        .then_inc(S["scan_done"], 1)
                dve.wait_ge(S["scan_done"], 4 * c + 4)

                def free(d):
                    dve.wait_ge(S["e_done"], 8 + 8 * c + DREADS[d - 2] if d >= 2 else 8 * c + DREADS[4 + d])

                def blocks(ap, b):
                    return ap.rearrange("p t (n b) -> p (t n) b", b=b)

                def intra():
                    free(0)
                    gv = blocks(G[:], SUB)
                    nc.vector.tensor_tensor(blocks(dif[:, 0], SUB), gv,
                                            gv[:, :, SUB // 2 - 1:SUB // 2].broadcast_to([P, TPH * CH // SUB, SUB]),
                                            ALU.subtract).then_inc(S["d_done"], 1)

                def level(l):
                    b = LEVELS[l - 1]
                    gv, dv = blocks(G[:], 2 * b), blocks(dif[:, l % 2], 2 * b)
                    ref = gv[:, :, b - 1:b].broadcast_to([P, TPH * CH // (2 * b), b])
                    free(l)
                    nc.vector.tensor_tensor(dv[:, :, 0:b], ref, gv[:, :, 0:b], ALU.subtract).then_inc(S["d_done"], 1)
                    nc.vector.tensor_tensor(dv[:, :, b:], gv[:, :, b:], ref, ALU.subtract).then_inc(S["d_done"], 1)

                def to_end():
                    free(5)
                    nc.vector.tensor_tensor(dif[:, 1], G[:, :, CH - 1:CH].broadcast_to([P, TPH, CH]), G[:],
                                            ALU.subtract).then_inc(S["d_done"], 1)

                def weights(l):
                    dve.wait_ge(S["lvl_done"], 5 + 5 * c + l + 1)
                    src = PS[:, 2 * (l % 3):2 * (l % 3) + 2, :].rearrange("p a (h t) -> p (a h) t", t=CH)
                    if l == 0:
                        dve.wait_ge(S["o_done"], c + 1)
                        mask = mixc[:, M_SUB:M_SUB + CH].unsqueeze(1).broadcast_to([P, N_HEADS, CH])
                        nc.vector.tensor_tensor(A[:], src, mask, ALU.mult).then_inc(S["a_done"], 1)
                    else:
                        dve.wait_ge(S["a_done"], 5 * c + l)
                        at_ = M_LVL + (l - 1) * CH
                        mask = mixc[:, at_:at_ + CH].bitcast(U32).unsqueeze(1).broadcast_to([P, N_HEADS, CH])
                        dve.sem_inc(S["dve_held"], 1)
                        nc.vector.copy_predicated(A[:], mask, src).then_inc(S["a_done"], 1)

                intra()
                level(1)
                level(2)
                weights(0)
                level(3)
                weights(1)
                level(4)
                weights(2)
                to_end()
                weights(3)
                weights(4)
                dve.wait_ge(S["gend_done"], c + 1 + GE_CREDIT)
                dve.wait_ge(S["o_done"], c + 2)
                nc.vector.tensor_tensor(state[:], state[:], g_end[:].unsqueeze(2).broadcast_to([P, TPH, HEAD]),
                                        ALU.mult).then_inc(S["s_scaled"], 1)
                dve.wait_ge(S["s_scaled"], c + 1)
                dve.wait_ge(S["s_done"], c + 1 + SD_CREDIT)
                nc.vector.tensor_tensor(state[:], state[:], PS[:, 7, 0:TPH * HEAD].rearrange("p (t v) -> p t v", t=TPH),
                                        ALU.add).then_inc(S["s_upd"], 1)
                dve.wait_ge(S["ropq_done"], c + 1)
                nc.vector.tensor_tensor(rot_s[:], PS[:, 6, :].rearrange("p (t c) -> p t c", t=TPH),
                                        rope_s[:, tok].unsqueeze(1).broadcast_to([P, TPH, CH]), ALU.mult).then_inc(S["ts_done"], 1)
                dve.wait_ge(S["ts_done"], 2 * c + 3)
                dve.wait_ge(S["t0_done"], 2 * c + 2)
                nc.vector.tensor_tensor(q_rot[:], rot_c[:], rot_s[:], ALU.add).then_inc(S["qs_done"], 1)
                dve.wait_ge(S["vw_done"], c + 1 + VW_CREDIT)
                nc.vector.tensor_tensor(rotk_s[:], PS[:, 7, 0:CH], rope_s[:, tok], ALU.mult).then_inc(S["ts_done"], 1)
                dve.wait_ge(S["ts_done"], 2 * c + 4)
                dve.wait_ge(S["kw_shift"], 2 * c + 2)
                nc.vector.tensor_tensor(k_win[:, CH:], rotk_c[:], rotk_s[:], ALU.add).then_inc(S["kw_done"], 1)
                def sub_max(n):
                    dve.wait_ge(S["sc_done"], 2 * c + n + 1)
                    j2 = (5 + n) % 3
                    sv = sm[:, n, :].rearrange("p (j t) -> p j t", j=GQA)
                    nc.vector.scalar_tensor_tensor(sv, PS[:, 2 * j2:2 * j2 + 2, :].rearrange("p a (j t) -> p (a j) t", t=2 * CH),
                                                   HEAD ** -0.5, m_cur.unsqueeze(1).broadcast_to([P, GQA, 2 * CH]),
                                                   ALU.mult, ALU.add).then_inc(S["sm_done"], 1)
                    dve.wait_ge(S["sm_done"], 2 * c + n + 1)
                    sinks = vecs[:, V_SINK + GQA * n:V_SINK + GQA * (n + 1)]
                    seq(nc.vector.tensor_reduce(mx[:, n, :], sv, AX_X, ALU.max))
                    seq(nc.vector.tensor_tensor(mx[:, n, :], mx[:, n, :], sinks, ALU.max))
                    seq(nc.vector.tensor_scalar(nm[:, n, :], mx[:, n, :], -1.0, None, ALU.mult))
                    nc.vector.tensor_tensor(es[:, n, :], sinks, mx[:, n, :], ALU.subtract).then_inc(S["es_ready"], 1)

                def over(n):
                    dve.wait_ge(S["exp_done"], 2 * c + n + 1)
                    seq(nc.vector.tensor_tensor(rsum[:, n, :], rsum[:, n, :], es[:, n, :], ALU.add))
                    nc.vector.reciprocal(rden[:, n, :], rsum[:, n, :]).then_inc(S["rd_done"], 1)

                sub_max(0)
                sub_max(1)
                seq(nc.vector.tensor_copy(m_cur, mixc[:, M_BAND:M_BAND + 2 * CH]))
                over(0)
                over(1)
                seq.leave(N_CH)

            ST = slice(N_PROMPT, TOK)
            rc8 = rope_c[:, ST].unsqueeze(1).broadcast_to([P, TPH, N_SAMPLE])
            rs8 = rope_s[:, ST].unsqueeze(1).broadcast_to([P, TPH, N_SAMPLE])
            dve.wait_ge(S["a_s"], 1)
            dve.wait_ge(S["smp_in"], 48)
            nc.vector.tensor_tensor(qt_s[:], q_reg[:, :, ST], rc8, ALU.mult)
            nc.vector.tensor_tensor(qu_s[:], PS[:, 6, 0:TPH * N_SAMPLE].rearrange("p (t b) -> p t b", t=TPH), rs8, ALU.mult)
            nc.vector.tensor_tensor(kt_s[:, 0], kv[:, 0, ST], rope_c[:, ST], ALU.mult)
            seq(nc.vector.tensor_tensor(kt_s[:, 1], PS[:, 6, 32:32 + N_SAMPLE], rope_s[:, ST], ALU.mult))
            seq(nc.vector.tensor_tensor(q_s[:], qt_s[:], qu_s[:], ALU.add))
            nc.vector.tensor_tensor(k_win_s[:, :, WINDOW - 1], kt_s[:, 0], kt_s[:, 1], ALU.add).then_inc(S["d_s"], 1)
            seq(nc.vector.tensor_tensor(state_s[:].rearrange("p t b v -> p (t b) v"), state_s[:].rearrange("p t b v -> p (t b) v"),
                                        f_s[:].rearrange("p t b -> p (t b)").unsqueeze(2).broadcast_to([P, TPH * N_SAMPLE, HEAD]), ALU.mult))
            dve.wait_ge(S["a_s"], 2)
            for t in range(TPH):
                src = PS[:, 0:4, :].rearrange("p a (b t v) -> p t (a b) v", b=2, t=TPH)[:, t]
                kvp = nc.vector.tensor_tensor(kv_s[:, t], src, k_gate[:, t, ST].unsqueeze(2).broadcast_to([P, N_SAMPLE, HEAD]), ALU.mult)
            kvp.then_inc(S["a_ps"], 1)
            dve.wait_ge(S["a_ps"], 1)
            nc.vector.tensor_tensor(state_s[:], state_s[:], kv_s[:], ALU.add).then_inc(S["d_s"], 1)
            dve.wait_ge(S["a_s"], 3)
            W = 2 * N_SAMPLE
            seq(nc.vector.tensor_scalar(sm_s[0:GQA], PS[0:GQA, 0:4, :].rearrange("p a (i t) -> p (a i) t", t=CH),
                                        HEAD ** -0.5, None, ALU.mult))
            seq(nc.vector.tensor_reduce(st_s[0:GQA, 0, :], sm_s[0:GQA], AX_X, ALU.max))
            seq(nc.vector.tensor_copy(st_s[0:GQA, 1, :].rearrange("p (n b) -> p n b", n=2),
                                      vecs[0:GQA, V_SINKT:V_SINKT + 2].unsqueeze(2).broadcast_to([GQA, 2, N_SAMPLE])))
            seq(nc.vector.tensor_tensor(st_s[0:GQA, 2, :], st_s[0:GQA, 0, :], st_s[0:GQA, 1, :], ALU.max))
            nc.vector.tensor_tensor(st_s[0:GQA, 3, :], st_s[0:GQA, 1, :], st_s[0:GQA, 2, :], ALU.subtract)
            nc.vector.tensor_tensor(sm_s[0:GQA], sm_s[0:GQA], st_s[0:GQA, 2, :].unsqueeze(2).broadcast_to([GQA, W, WINDOW]),
                                    ALU.subtract).then_inc(S["v_s"], 1)
            dve.wait_ge(S["sig_done"], 3)
            seq(nc.vector.tensor_reduce(st_s[0:GQA, 4, :], sm_s[0:GQA], AX_X, ALU.add))
            seq(nc.vector.tensor_tensor(st_s[0:GQA, 5, :], st_s[0:GQA, 4, :], st_s[0:GQA, 3, :], ALU.add))
            seq(nc.vector.reciprocal(st_s[0:GQA, 6, :], st_s[0:GQA, 5, :]))
            nc.vector.tensor_tensor(sm_s[0:GQA], sm_s[0:GQA], st_s[0:GQA, 6, :].unsqueeze(2).broadcast_to([GQA, W, WINDOW]),
                                    ALU.mult).then_inc(S["d_s"], 1)

            gs = lambda r, g: r[:, :, g * GW:(g + 1) * GW]
            dve.wait_ge(S["out_in"], 96)
            for g in range(NG):
                dve.wait_ge(S["css_done"], g + 1)
                nc.vector.tensor_scalar(c_root[:], PS[:, 3:7, :GW], 1.0 / HEAD, EPS, ALU.mult, ALU.add).then_inc(S["cvar_done"], 1)
                dve.wait_ge(S["croot_done"], g + 1)
                nc.vector.reciprocal(c_root[:], c_root[:]).then_inc(S["crms_done"], 1)
                dve.wait_ge(S["crms_done"], g + 1)
                nc.vector.tensor_tensor(gs(hq_reg, g), gs(hq_reg, g), c_root[:], ALU.mult).then_inc(S["co_done"], 1)
                dve.wait_ge(S["co_done"], g + 1)
                dve.wait_ge(S["cg_done"], g + 1)
                nc.vector.scalar_tensor_tensor(gs(hq_reg, g), gs(hq_reg, g), vecs[:, V_OUTG:V_OUTG + 1], gs(hg_reg, g),
                                               ALU.mult, ALU.mult).then_inc(S["ch_done"], 1)
                dve.wait_ge(S["cat_hi"], 2 * g + 2)
                nc.vector.tensor_tensor(x_lo[:, g, TPH:], gs(hq_reg, g), x_hi[:, g, TPH:].bitcast(F32),
                                        ALU.subtract).then_inc(S["cat_lo_h"], 1)

            def out_pair(p, last):
                for o in range(2):
                    n = 2 * p + o
                    if not last or o == 0 or LAST_B == 2:
                        split_lo(G_OUT + n + 1, 1 - o)
                    for g in range(NG):
                        dve.wait_ge(S["unit_done"], UNIT_CREDIT + U_OUT + 3 * n + g + 1)
                        nc.vector.tensor_copy(y[:, g, n, :], PS[:, g, :GW]).then_inc(S["unit_evac"], 1)

            with dve.Fori(0, KT // 2 - 1) as p:
                out_pair(p, False)
            out_pair(KT // 2 - 1, True)
            border_dve(1)
            if LAST_B == 2:
                ffn(G_FFN2, U_FFN2, 1, 2, False)


LAST_B = 2
VW_CREDIT = KW_CREDIT = VT_CREDIT = SD_CREDIT = GE_CREDIT = 1


def tables():
    ident = np.eye(P, dtype=np.float32)
    head_ones = np.kron(np.eye(2), np.ones((HEAD, HEAD))).astype(np.float32)
    s, t = np.arange(CH)[:, None], np.arange(CH)[None]
    mixc = np.zeros((P, NM), np.float32)
    for i, b in enumerate(LEVELS):
        mixc[:, M_LVL + i * CH:M_LVL + (i + 1) * CH] = (s // (2 * b) == t // (2 * b)) & (s // b < t // b)
    mixc[:, M_SUB:M_SUB + CH] = (s // SUB == t // SUB) & (s <= t)
    key = np.arange(2 * CH)[None]
    rel = s + WINDOW - key
    band = (rel >= 0) & (rel < WINDOW)
    mixc[:, M_BAND:M_BAND + 2 * CH] = np.where(band, 0.0, NEG)
    mixc[:, M_FIRST:M_FIRST + 2 * CH] = np.where(band & (key >= WINDOW), 0.0, NEG)
    half = ROT // 2
    inv = np.float32(THETA) ** (-np.arange(half, dtype=np.float32) / np.float32(half))
    pos = np.concatenate([np.arange(N_PROMPT), np.full(N_SAMPLE, PAST_LEN)]).astype(np.float32)
    ang = inv[:, None] * pos[None]
    rope = np.zeros((2, P, TOK), np.float32)
    rope[0] = 1.0
    for h0 in (0, HEAD):
        for d in range(half):
            mixc[h0 + half + d, M_ROT + h0 + d] = -1.0
            mixc[h0 + d, M_ROT + h0 + half + d] = 1.0
            for at in (h0 + d, h0 + half + d):
                rope[0, at], rope[1, at] = np.cos(ang[d]), np.sin(ang[d])
    pick = np.repeat(np.eye(N_SAMPLE, dtype=np.float32)[:, :, None], HEAD, axis=2)
    return {"ident": ident, "head_ones": head_ones, "mixc": mixc, "rope": rope, "pick": pick}


def kernel(**inputs):
    import concourse.bacc as bacc
    from concourse.bass_utils import run_bass_kernel_spmd as run

    c = np.ascontiguousarray
    x = np.concatenate([inputs["x_prompt"][0], inputs["x_sample"][:, 0]], axis=0)
    arrays = {"x": c(x.reshape(NG, GW, KT, P).transpose(0, 3, 2, 1))}
    for f in ("1", "2"):
        w = inputs[f"ffn{f}_w_gu"][0].reshape(KT, P, 2, HT, P)
        arrays["w_gu" + f] = c(w.transpose(3, 2, 1, 0, 4)).reshape(2 * HT, P, KT * P)
        arrays["w_down" + f] = c(inputs[f"ffn{f}_w_down"][0].reshape(HT, P, D_MODEL))
    cols = [inputs[n][0].reshape(KT, P).T for n in
            ("ffn1_pre_g", "ffn1_post_g", "mix_pre_g", "mix_post_g", "ffn2_pre_g", "ffn2_post_g")]
    cols += [inputs["hgrn_lb"][r].reshape(TPH, P).T for r in range(2)]
    cols += [np.tile(inputs["hgrn_out_g"][0], 2)[:, None], np.tile(inputs["attn_sinks"][0][None], (P, 1)),
             np.tile(inputs["attn_sinks"][0].reshape(N_KV, GQA).T, (P // GQA, 1))]
    arrays["vecs"] = c(np.concatenate(cols, axis=1))
    w_in = inputs["w_in"][0]
    q, k, v, hq, hf, hi, hg = np.split(w_in, np.cumsum([512, 128, 128, 512, 512, 512])[:6], axis=1)
    q = q.reshape(D_MODEL, N_KV, GQA, HEAD).transpose(0, 2, 1, 3).reshape(D_MODEL, 512)
    w_in = np.concatenate([hf, hq, hi, q, hg, k, v], axis=1)
    arrays["w_in"] = c(w_in.reshape(KT, P, IN_TILES, P).transpose(2, 1, 0, 3)).reshape(IN_TILES, P, KT * P)
    w_out = inputs["w_out"][0]
    w_att = w_out[:512].reshape(N_KV, GQA, HEAD, D_MODEL).transpose(1, 0, 2, 3).reshape(512, D_MODEL)
    w_out = np.concatenate([w_att, w_out[512:]], axis=0)
    arrays["w_out"] = c(w_out.reshape(KT, P, KT, P).transpose(2, 1, 0, 3)).reshape(KT, P, KT * P)
    kc, vc = inputs["cache_win_k"][0], inputs["cache_win_v"][0]
    arrays["k_cache"] = c(kc[:, 1:].reshape(N_SAMPLE, WINDOW - 1, P).transpose(2, 0, 1))
    arrays["v_cache"] = c(vc[:, 1:].reshape(N_SAMPLE, WINDOW - 1, P).transpose(1, 0, 2))
    arrays["state"] = c(inputs["state_hgrn"][0].reshape(N_SAMPLE, TPH, 2, HEAD, HEAD)
                        .transpose(2, 3, 1, 0, 4)).reshape(P, TPH, N_SAMPLE, HEAD)
    arrays.update(tables())

    nc = bacc.Bacc("TRN2", target_bir_lowering=False, num_devices=1)
    ins = {k: nc.dram_tensor("in_" + k, v.shape, F32, kind="ExternalInput").ap() for k, v in arrays.items()}
    stream = (NG, P, KT, GW)
    shapes = {"y": stream, "k_win": (P, CH), "v_win": (P, CH), "state": (P, TPH, HEAD),
              "k_win_s": (P, N_SAMPLE, WINDOW), "v_win_s": (P, N_SAMPLE, P), "state_s": (P, TPH, N_SAMPLE, HEAD)}
    outs = {k: nc.dram_tensor("out_" + k, s, F32, kind="ExternalOutput").ap() for k, s in shapes.items()}
    for k in ("x1", "x2"):
        outs[k] = nc.dram_tensor("stream_" + k, stream, F32, kind="Internal").ap()
    build(nc, ins, outs)
    r = run(nc, [{"in_" + k: v for k, v in arrays.items()}], core_ids=[0]).results[0]
    yv = r["out_y"].transpose(0, 3, 2, 1).reshape(TOK, D_MODEL)
    kp = r["out_k_win"].T.reshape(1, 1, CH, N_KV, HEAD)
    vp = r["out_v_win"].reshape(1, 1, CH, N_KV, HEAD)
    sp = r["out_state"].reshape(2, HEAD, TPH, HEAD).transpose(2, 0, 1, 3).reshape(1, 1, N_HEADS, HEAD, HEAD)
    ks = r["out_k_win_s"].transpose(1, 2, 0).reshape(1, N_SAMPLE, WINDOW, N_KV, HEAD)
    vs = r["out_v_win_s"].transpose(1, 0, 2).reshape(1, N_SAMPLE, WINDOW, N_KV, HEAD)
    ss = r["out_state_s"].reshape(2, HEAD, TPH, N_SAMPLE, HEAD).transpose(3, 2, 0, 1, 4)\
        .reshape(1, N_SAMPLE, N_HEADS, HEAD, HEAD)
    return tuple(map(c, (yv[:N_PROMPT][None], yv[N_PROMPT:][:, None], kp, vp, sp, ks, vs, ss)))
```

```python
from contextlib import ExitStack

import numpy as np

import concourse.bass as bass
from concourse import mybir

F32 = mybir.dt.float32
F32R = mybir.dt.float32r
U32 = mybir.dt.uint32
ALU = mybir.AluOpType
ACT = mybir.ActivationFunctionType
AX_X = mybir.AxisListType.X

P = 128
D_MODEL, D_FF = 1024, 2816
N_PROMPT, N_SAMPLE, PAST_LEN = 1024, 8, 2048
TOK = N_PROMPT + N_SAMPLE
NG = 3
GW = TOK // NG
KT = D_MODEL // P
HT = D_FF // P
HEAD, N_HEADS, N_KV, GQA = 64, 8, 2, 4
WINDOW, ROT, THETA = 128, 16, 500000.0
EPS, NEG = 1e-6, -1e30
CH = 128
N_CH = N_PROMPT // CH
TPH = 4
IN_TILES = 22
F_MIN = 2.0 ** -32
LEVELS = (8, 16, 32, 64)
SUB = 8

FFN_STEPS = HT // 2
FFN_GRANULES, FFN_UNITS = 6, 4 * NG + NG * KT
G_IN = FFN_STEPS * FFN_GRANULES
G_OUT = G_IN + IN_TILES
G_FFN2 = G_OUT + KT
U_IN = FFN_STEPS * FFN_UNITS
U_OUT = U_IN + NG * IN_TILES
U_FFN2 = U_OUT + NG * KT
UNIT_CREDIT, EVAC_CREDIT, READY_CREDIT = FFN_UNITS, NG, 3

V_GAIN = {"ffn1_pre": 0, "ffn1_post": 8, "mix_pre": 16, "mix_post": 24, "ffn2_pre": 32, "ffn2_post": 40}
V_LB0, V_LB1, V_OUTG, V_SINK, V_SINKT, NV = 48, 52, 56, 57, 65, 67
M_LVL, M_SUB, M_BAND, M_FIRST, M_ROT, NM = 0, 512, 640, 896, 1152, 1280


class Seq:

    def __init__(self, eng, sem):
        self.eng, self.sem, self.n, self.i, self.per, self.left = eng, sem, 0, None, 0, 0

    def __call__(self, ins):
        self.n += 1
        ins.then_inc(self.sem, 1)
        self.eng.wait_ge(self.sem, self.n if self.i is None else self.i * self.per + self.n)

    def enter(self, i, per):
        self.i, self.per, self.at = i, per, self.n

    def leave(self, times):
        assert self.n - self.at == self.per, (self.n - self.at, self.per)
        self.n = self.at + times * self.per
        self.i = None


def build(nc, ins, outs):
    ctx = ExitStack()
    with ctx:
        sems = {}

        def sem(name):
            sems[name] = ctx.enter_context(nc.semaphore(name))
            return sems[name]

        at = [(nc.sbuf_base + 31) // 32 * 32]
        end = nc.sbuf_usable_end

        def put(name, shape, dt, offset=None):
            size = 4 * int(np.prod(shape[1:]))
            if offset is None:
                offset = at[0]
                at[0] += (size + 31) // 32 * 32
            assert offset + size <= end, (name, offset + size - end)
            return nc.alloc_sbuf_tensor_at(name, shape, dt, offset=offset)

        vecs = put("vecs", [P, NV], F32)
        half_gain = put("half_gain", [P, 2, KT], F32)
        lb = put("lb", [P, 3, TPH], F32)
        ident = put("ident", [P, P], F32)
        ones = put("ones", [P, P], F32)
        eps = put("eps", [P, 1], F32)
        head_ones = put("head_ones", [P, P], F32)
        rms = put("rms", [P, NG, GW], F32)
        raw = [put(f"raw{s}", [P, 1024], F32) for s in range(2)]
        w_hi = [put(f"w_hi{s}", [P, 1024], F32R) for s in range(2)]
        w_lo = [put(f"w_lo{s}", [P, 1024], F32R) for s in range(2)]
        x_at = at[0]
        x_hi = put("x_hi", [P, NG, KT, GW], F32R)
        x_lo = put("x_lo", [P, NG, KT, GW], F32R)
        x_end = zone = at[0]

        y = put("y", [P, NG, KT, GW], F32)
        resid = put("resid", [P, NG, KT, GW], F32)
        h_at = at[0]
        h = put("h", [P, NG, 4, GW], F32R)
        sq = put("sq", [P, KT, GW], F32)
        raw.append(put("raw2", [P, 1024], F32))
        w_hi.append(put("w_hi2", [P, 1024], F32R))
        w_lo.append(put("w_lo2", [P, 1024], F32R))
        silu_at = at[0]
        silu_g = put("silu_g", [P, NG, GW], F32)
        prod = put("prod", [P, NG, GW], F32)
        root = put("root", [P, 2, GW], F32, h_at + 2 * GW * 4)
        rms_y = put("rms_y", [P, 2, GW], F32, silu_at + NG * GW * 4)

        at[0] = zone
        R = put("proj", [P, 5 * TPH, TOK], F32)
        f_reg, hq_reg, hi_reg, q_reg, hg_reg = (R[:, TPH * j:TPH * (j + 1), :] for j in range(5))
        chunk = lambda j, c: R[:, TPH * j:TPH * (j + 1), bass.ds(c * CH, CH)]
        k_gate = put("k_gate", [P, TPH, TOK], F32)
        kv = put("kv", [P, 2, TOK], F32)
        f_s = put("f_s", [P, TPH, N_SAMPLE], F32)
        mixc = put("mixc", [P, NM], F32)
        kt_s = put("kt_s", [P, 2, N_SAMPLE], F32)
        qu_s = put("qu_s", [P, TPH, N_SAMPLE], F32)
        qt_s = put("qt_s", [P, TPH, N_SAMPLE], F32)
        q_s = put("q_s", [P, TPH, N_SAMPLE], F32)
        k_win = put("k_win", [P, 2 * CH], F32)
        hi_c = put("hi_c", [P, TPH, CH], F32)
        hi_at = zone + 2 * TPH * TOK * 4
        state_s = put("state_s", [P, TPH, N_SAMPLE, HEAD], F32, zone)
        k_win_s = put("k_win_s", [P, N_SAMPLE, WINDOW], F32, zone + 8192)
        v_win_s = put("v_win_s", [P, N_SAMPLE, P], F32, zone + 12288)
        c_sq = put("c_sq", [P, TPH, GW], F32, hi_at)
        c_root = put("c_root", [P, TPH, GW], F32, hi_at + 8192)
        at[0] = x_at
        rope_c = put("rope_c", [P, TOK], F32)
        rope_s = put("rope_s", [P, TOK], F32)
        G = put("G", [P, TPH, CH], F32)
        dif = put("dif", [P, 2, TPH, CH], F32)
        dec = put("dec", [P, 2, TPH, CH], F32)
        q_dec = put("q_dec", [P, 2, TPH, CH], F32)
        k_dec = put("k_dec", [P, 2, TPH, CH], F32)
        A = put("A", [P, N_HEADS, CH], F32)
        V = put("V", [P, N_HEADS * HEAD], F32)
        kdT = put("kdT", [P, N_HEADS * HEAD], F32)
        qg = put("qg", [P, TPH, CH], F32)
        kd = put("kd", [P, TPH, CH], F32)
        state = put("state", [P, TPH, HEAD], F32)
        g_end = put("g_end", [P, TPH], F32)
        q_rot = put("q_rot", [P, TPH, CH], F32)
        rc_at = at[0]
        rot_c = put("rot_c", [P, TPH, CH], F32)
        rs_at = at[0]
        rot_s = put("rot_s", [P, TPH, CH], F32)
        v_win = put("v_win", [P, 2 * CH], F32)
        v_at = at[0]
        v_c = put("v_c", [P, CH], F32)
        rotk_c = put("rotk_c", [P, CH], F32)
        rotk_s = put("rotk_s", [P, CH], F32)
        sm_at = at[0]
        sm = put("sm", [P, 2, GQA * 2 * CH], F32)
        pt_at = at[0]
        pT = put("pT", [P, 2, GQA * 2 * CH], F32)
        m_cur = mixc[:, M_FIRST:M_FIRST + 2 * CH]
        mx = put("mx", [P, 2, GQA], F32)
        nm = put("nm", [P, 2, GQA], F32)
        es = put("es", [P, 2, GQA], F32)
        rsum = put("rsum", [P, 2, GQA], F32)
        rden = put("rden", [P, 2, GQA], F32)
        pT_s = put("pT_s", [P, 2 * N_SAMPLE * GQA], F32)
        st_s = put("st_s", [P, 8, 2 * N_SAMPLE], F32)
        hv_s = put("hv_s", [P, N_HEADS * HEAD], F32, rc_at)
        pick = put("pick", [P, N_SAMPLE, HEAD], F32, rs_at)
        v_row = put("v_row", [P, P], F32, v_at)
        sm_s = put("sm_s", [P, 2 * N_SAMPLE, WINDOW], F32, sm_at)
        kv_s = put("kv_s", [P, TPH, N_SAMPLE, HEAD], F32, pt_at)
        assert at[0] <= x_end, at[0] - x_end

        PS = ctx.enter_context(nc.psum_tensor("PS", [P, 8, 512], F32))

        raw_full = [sem(f"raw_full{s}") for s in range(3)]
        for n in ("consts_in w_gained w_hi_done w_ready unit_done unit_evac x_split_lo x_split_hi x_new "
                  "y_scaled sq_done ss_done var_done sq_folded root_done rms_done eps_done spilled gain_done ones_done "
                  "y_zero silu_done h_ready mixc_in smp_in out_in sig_done f_done fmax_done ln_done k_done "
                  "scan_done hic_done vt_done vc_done d_done e_done gend_done qk_done lvl_done a_done kdt_done kdtc_done "
                  "o_done oc_done s_done s_scaled s_upd st_zero vst_done ropq_done kvp_done t0_done ts_done qs_done kw_shift kw_done "
                  "vw_done sc_done sm_done mx_done m_done nm_done es_ready es_done exp_done den_done rd_done p_done pt_done "
                  "ptc_done att_done attc_done mcur_done "
                  "csq_done css_done cvar_done croot_done crms_done co_done cg_done ch_done cat_hi_a cat_hi_h cat_lo_a cat_lo_h x_split_lo_late y_copied "
                  "pool_held dve_held a_ps p_ps v_ps d_s a_s v_s h_hi_done h_lo_done dve_seq act_seq pool_seq cleared").split():
            sem(n)
        resid_full = [sem(f"resid_full{g}") for g in range(NG)]
        S = sems

        norms = [("S", 0, g) for g in range(NG)]
        for b in range(3):
            norms += [("F", b, g) for g in range(NG)] + [("S", b + 1, g) for g in range(NG) if b < 2]
        norm_no = {n: i for i, n in enumerate(norms)}

        GAIN_F = {0: half_gain[:, 0, :], 1: vecs[:, V_GAIN["mix_post"]:V_GAIN["mix_post"] + 8], 2: half_gain[:, 1, :]}

        block = ctx.enter_context(nc.Block())

        @block.sync
        def _(sp):
            sp.dma_start(vecs[:], ins["vecs"]).then_inc(S["consts_in"], 16)
            sp.dma_start(ident[:], ins["ident"]).then_inc(S["consts_in"], 16)
            sp.dma_start(head_ones[:], ins["head_ones"]).then_inc(S["consts_in"], 16)
            for g in range(NG):
                sp.dma_start(resid[:, g], ins["x"][g]).then_inc(resid_full[g], 16)

            def load(n, s, src):
                sp.wait_ge(S["w_ready"], n + 2)
                sp.dma_start(raw[s][:], src).then_inc(raw_full[s], 16)

            def ffn_loads(w_gu, w_down, n0):
                with sp.Fori(0, FFN_STEPS) as i:
                    for o in range(4):
                        load(n0 + 6 * i + o, o % 3, w_gu[4 * i + o])
                    for o in range(2):
                        load(n0 + 6 * i + 4 + o, (4 + o) % 3, w_down[2 * i + o])

            def store_stream(b, to):
                for g in range(NG):
                    sp.wait_ge(S["x_new"], NG * b + g + 1)
                    sp.dma_start(to[g], resid[:, g]).then_inc(S["spilled"], 16)

            ffn_loads(ins["w_gu1"], ins["w_down1"], 0)
            load(G_IN, 0, ins["w_in"][0])
            load(G_IN + 1, 1, ins["w_in"][1])
            store_stream(0, outs["x1"])
            sp.wait_ge(S["rms_done"], norm_no[("S", 1, NG - 1)] + 1)
            sp.dma_start(mixc[:], ins["mixc"]).then_inc(S["mixc_in"], 16)
            with sp.Fori(1, IN_TILES // 2) as p:
                for o in range(2):
                    load(G_IN + 2 * p + o, o, ins["w_in"][2 * p + o])
            for o in range(2):
                load(G_OUT + o, o, ins["w_out"][o])
            sp.wait_ge(S["unit_done"], UNIT_CREDIT + U_OUT)
            sp.dma_start(rope_c[:], ins["rope"][0]).then_inc(S["mixc_in"], 16)
            sp.dma_start(rope_s[:], ins["rope"][1]).then_inc(S["mixc_in"], 16)
            sp.wait_ge(S["scan_done"], 4 * N_CH)
            sp.dma_start(state_s[:], ins["state"]).then_inc(S["smp_in"], 16)
            sp.dma_start(k_win_s[:, :, 0:WINDOW - 1], ins["k_cache"]).then_inc(S["smp_in"], 16)
            sp.dma_start(v_win_s[0:WINDOW - 1], ins["v_cache"]).then_inc(S["smp_in"], 16)
            sp.wait_ge(S["kw_done"], N_CH + 1)
            sp.dma_start(outs["k_win"], k_win[:, CH:]).then_inc(S["out_in"], 16)
            sp.wait_ge(S["vw_done"], N_CH + 1)
            sp.dma_start(outs["v_win"], v_win[:, CH:]).then_inc(S["out_in"], 16)
            sp.wait_ge(S["s_upd"], N_CH + 1)
            sp.dma_start(outs["state"], state[:]).then_inc(S["out_in"], 16)
            sp.wait_ge(S["smp_in"], 48)
            sp.wait_ge(S["a_s"], 1)
            sp.dma_start(pick[0:N_SAMPLE], ins["pick"]).then_inc(S["smp_in"], 16)
            sp.wait_ge(S["v_ps"], 1)
            sp.dma_start(v_win_s[WINDOW - 1:WINDOW], v_row[0:N_SAMPLE]).then_inc(S["p_ps"], 16)
            sp.wait_ge(S["p_ps"], 16)
            sp.dma_start(outs["v_win_s"], v_win_s[:]).then_inc(S["out_in"], 16)
            sp.wait_ge(S["d_s"], 1)
            sp.dma_start(outs["k_win_s"], k_win_s[:]).then_inc(S["out_in"], 16)
            sp.wait_ge(S["d_s"], 2)
            sp.dma_start(outs["state_s"], state_s[:]).then_inc(S["out_in"], 16)
            with sp.Fori(1, KT // 2) as p:
                for o in range(2):
                    load(G_OUT + 2 * p + o, o, ins["w_out"][2 * p + o])
            load(G_FFN2, 0, ins["w_gu2"][0])
            load(G_FFN2 + 1, 1, ins["w_gu2"][1])
            sp.wait_ge(S["spilled"], 16 * NG)
            sp.wait_ge(S["out_in"], 96)
            sp.wait_ge(S["unit_done"], UNIT_CREDIT + U_OUT + 2 * NG - 1)
            for g in range(NG):
                sp.dma_start(resid[:, g], outs["x1"][g]).then_inc(resid_full[g], 16)
            load(G_FFN2 + 2, 2, ins["w_gu2"][2])
            load(G_FFN2 + 3, 0, ins["w_gu2"][3])
            for o in range(2):
                load(G_FFN2 + 4 + o, 1 + o, ins["w_down2"][o])
            with sp.Fori(1, FFN_STEPS) as i:
                for o in range(4):
                    load(G_FFN2 + 6 * i + o, o % 3, ins["w_gu2"][4 * i + o])
                for o in range(2):
                    load(G_FFN2 + 6 * i + 4 + o, 1 + o, ins["w_down2"][2 * i + o])
            store_stream(2, outs["y"])
            sp.wait_ge(S["spilled"], 32 * NG)

        @block.tensor
        def _(pe):
            pe.sem_inc(S["unit_done"], UNIT_CREDIT)

            def unit(bank, u, pairs):
                pe.wait_ge(S["unit_evac"], u + 1)
                last = len(pairs) - 1
                for k, (w, v) in enumerate(pairs):
                    (wh, wl), (vh, vl) = w, v
                    nc.tensor.matmul(PS[:, bank, :GW], wh, vh, start=(k == 0), stop=False)
                    nc.tensor.matmul(PS[:, bank, :GW], wh, vl, start=False, stop=False)
                    mm = nc.tensor.matmul(PS[:, bank, :GW], wl, vh, start=False, stop=(k == last))
                mm.then_inc(S["unit_done"], 1)

            def project(n, s, u):
                pe.wait_ge(S["w_ready"], READY_CREDIT + n + 1)
                for g in range(NG):
                    unit(g, u + g, [((w_hi[s][:, k * P:(k + 1) * P], w_lo[s][:, k * P:(k + 1) * P]),
                                     (x_hi[:, g, k, :], x_lo[:, g, k, :])) for k in range(KT)])

            def pair_by_group(n, u, ready=None, mid=None):
                assert u % 3 == 0
                for g in range(NG):
                    if ready is not None:
                        ready(g)
                    for o in range(2):
                        if g == 0:
                            pe.wait_ge(S["w_ready"], READY_CREDIT + n + o + 1)
                        unit((2 * g + o) % 3, u + 2 * g + o,
                             [((w_hi[o][:, k * P:(k + 1) * P], w_lo[o][:, k * P:(k + 1) * P]),
                               (x_hi[:, g, k, :], x_lo[:, g, k, :])) for k in range(KT)])
                        if mid is not None and (g, o) == (NG - 1, 0):
                            mid()

            def norm_sum(n):
                i = norm_no[n]
                pe.wait_ge(S["sq_folded"], i + 1)
                if i >= 2:
                    pe.wait_ge(S["root_done"], i - 1)
                for m in range(KT // 2):
                    mm = nc.tensor.matmul(PS[:, 3 + i % 2, :GW], ones[:], sq[:, m, :], start=(m == 0), stop=(m == KT // 2 - 1))
                mm.then_inc(S["ss_done"], 1)

            def border_units(b, n, u):
                def ready(g):
                    if b >= 0 and g == 0:
                        norm_sum(("F", b, 1))
                        norm_sum(("F", b, 2))
                    if g > 0:
                        norm_sum(("S", b + 1, g - 1))
                    pe.wait_ge(S["x_split_lo"], NG * (b + 1) + g + 1)
                    if g == NG - 1:
                        pe.wait_ge(S["x_split_lo_late"], b + 2)
                pair_by_group(n, u, ready)
                norm_sum(("S", b + 1, NG - 1))

            def down(g, i, u, step_h, tiles=range(KT)):
                pe.wait_ge(S["h_lo_done"], step_h + NG + g + 1)
                for m in tiles:
                    unit((g * KT + m) % 3, u + 12 + g * KT + m,
                         [((w_hi[1 + t][:, m * P:(m + 1) * P], w_lo[1 + t][:, m * P:(m + 1) * P]),
                           (h[:, g, 2 * t, :], h[:, g, 2 * t + 1, :])) for t in range(2)])

            def ffn(n0, u0, f, b):
                def step(i, first, last):
                    u, step_h = u0 + 36 * i, 6 * FFN_STEPS * f + 6 * i
                    for o in range(2 if first else 0, 4):
                        project(n0 + 6 * i + o, o % 3, u + 3 * o)
                    pe.wait_ge(S["w_ready"], READY_CREDIT + n0 + 6 * i + 6)
                    for g in range(NG - 1 if last else NG):
                        down(g, i, u, step_h)
                    if last:
                        down(NG - 1, i, u, step_h, range(KT // 2))
                        norm_sum(("F", b, 0))
                        down(NG - 1, i, u, step_h, range(KT // 2, KT))

                step(0, True, False)
                with pe.Fori(1, FFN_STEPS - 1) as i:
                    step(i, False, False)
                step(FFN_STEPS - 1, False, True)

            pe.wait_ge(S["ones_done"], 1)
            pe.wait_ge(S["consts_in"], 48)
            border_units(-1, 0, 0)
            ffn(0, 0, 0, 0)
            border_units(0, G_IN, U_IN)

            with pe.Fori(1, IN_TILES // 2) as p:
                for o in range(2):
                    project(G_IN + 2 * p + o, o, U_IN + 6 * p + 3 * o)

            def pair(j):
                return PS[:, 2 * j:2 * j + 2, :].rearrange("p a b -> p (a b)")

            def to_tokens(bank, src, first_col=0):
                for j in range(TPH):
                    mm = nc.tensor.transpose(PS[:, bank, j * P:(j + 1) * P], src[:, j, :], ident[:])
                return mm

            pe.wait_ge(S["unit_evac"], EVAC_CREDIT + U_OUT)
            pe.wait_ge(S["mixc_in"], 48)
            pe.wait_ge(S["st_zero"], 4)
            with pe.Fori(0, N_CH) as c:
                def level(l):
                    pe.wait_ge(S["qk_done"], 12 + 12 * c + 3 + 2 * l)
                    if l >= 2:
                        pe.wait_ge(S["a_done"], 5 * c + l - 1)
                    w = CH if l == 0 else CH // 2
                    for hd in range(N_HEADS):
                        p0, t = HEAD * (hd % 2), hd // 2
                        mm = nc.tensor.matmul(PS[:, 2 * (l % 2) + hd % 2, t * w:(t + 1) * w], k_dec[p0:p0 + HEAD, l % 2, t, :],
                                              q_dec[p0:p0 + HEAD, l % 2, t, 0:w], start=True, stop=True)
                    mm.then_inc(S["lvl_done"], 1)

                def scores(n):
                    for j in range(GQA):
                        mm = nc.tensor.matmul(pair(2)[:, j * 2 * CH:(j + 1) * 2 * CH], q_rot[HEAD * n:HEAD * (n + 1), j, :],
                                              k_win[HEAD * n:HEAD * (n + 1), :], start=True, stop=True)
                    mm.then_inc(S["sc_done"], 1)

                def probs_by_key(n):
                    pe.wait_ge(S["p_done"], 2 * c + n + 1)
                    if n == 0:
                        pe.wait_ge(S["sm_done"], 2 * c + 2)
                    else:
                        pe.wait_ge(S["ptc_done"], 2 + 2 * c + 1)
                    for b in range(2 * GQA):
                        mm = nc.tensor.transpose(pair(2)[:, b * CH:(b + 1) * CH], sm[:, n, b * CH:(b + 1) * CH], ident[:])
                    mm.then_inc(S["pt_done"], 1)

                pe.wait_ge(S["ptc_done"], 2 + 2 * c)
                nc.tensor.matmul(PS[:, 4, :], mixc[:, M_ROT:M_ROT + P], chunk(3, c),
                                 start=True, stop=True).then_inc(S["ropq_done"], 1)
                pe.wait_ge(S["vst_done"], c + 1)
                nc.tensor.matmul(PS[:, 5, 0:CH], mixc[:, M_ROT:M_ROT + P], kv[:, 0, bass.ds(c * CH, CH)], start=True, stop=True)
                nc.tensor.transpose(PS[:, 5, CH:2 * CH], v_c[:], ident[:]).then_inc(S["kvp_done"], 1)
                level(0)
                pe.wait_ge(S["hic_done"], c + 1)
                pe.wait_ge(S["attc_done"], c + 1)
                to_tokens(6, hi_c).then_inc(S["vt_done"], 1)
                level(1)
                pe.wait_ge(S["qs_done"], c + 1)
                pe.wait_ge(S["kw_done"], c + 1 + KW_CREDIT)
                pe.wait_ge(S["vw_done"], c + 1 + VW_CREDIT)
                scores(0)
                level(2)
                level(3)
                pe.wait_ge(S["sm_done"], 2 * c + 1)
                scores(1)
                level(4)
                pe.wait_ge(S["qk_done"], 12 + 12 * c + 12)
                pe.wait_ge(S["s_upd"], c + 1)
                to_tokens(7, kd).then_inc(S["kdt_done"], 1)
                probs_by_key(0)
                pe.wait_ge(S["vc_done"], c + 1)
                pe.wait_ge(S["a_done"], 5 * c + 5)
                for hd in range(N_HEADS):
                    p0, t = HEAD * (hd % 2), hd // 2
                    nc.tensor.matmul(PS[p0:p0 + HEAD, 6, t * CH:(t + 1) * CH], V[:, hd * HEAD:(hd + 1) * HEAD],
                                     A[:, TPH * (hd % 2) + t, :], start=True, stop=False)
                    mm = nc.tensor.matmul(PS[p0:p0 + HEAD, 6, t * CH:(t + 1) * CH], state[p0:p0 + HEAD, t, :],
                                          qg[p0:p0 + HEAD, t, :], start=False, stop=True)
                mm.then_inc(S["o_done"], 1)
                pe.wait_ge(S["kdtc_done"], c + 1)
                for hd in range(N_HEADS):
                    p0, t = HEAD * (hd % 2), hd // 2
                    mm = nc.tensor.matmul(PS[p0:p0 + HEAD, 7, t * HEAD:(t + 1) * HEAD], kdT[:, hd * HEAD:(hd + 1) * HEAD],
                                          V[:, hd * HEAD:(hd + 1) * HEAD], start=True, stop=True)
                mm.then_inc(S["s_done"], 1)
                probs_by_key(1)
                pe.wait_ge(S["oc_done"], c + 1)
                for n in range(2):
                    pe.wait_ge(S["ptc_done"], 2 + 2 * c + n + 1)
                    for half in range(2):
                        mm = nc.tensor.matmul(PS[HEAD * n:HEAD * (n + 1), 6, :], v_win[:, half * CH + HEAD * n:half * CH + HEAD * (n + 1)],
                                              pT[:, n, :].rearrange("p (j a t) -> p a j t", j=GQA, a=2)[:, half],
                                              start=(half == 0), stop=(half == 1))
                    mm.then_inc(S["att_done"], 1)

            ST = slice(N_PROMPT, TOK)
            pe.wait_ge(S["attc_done"], N_CH + 1)
            pe.wait_ge(S["s_upd"], N_CH + 1)
            pe.wait_ge(S["vw_done"], N_CH + VW_CREDIT)
            pe.wait_ge(S["kw_done"], N_CH + KW_CREDIT)
            nc.tensor.matmul(PS[:, 6, 0:TPH * N_SAMPLE], mixc[:, M_ROT:M_ROT + P], q_reg[:, :, ST], start=True, stop=True)
            nc.tensor.matmul(PS[:, 6, 32:32 + N_SAMPLE], mixc[:, M_ROT:M_ROT + P], kv[:, 0, ST], start=True, stop=True)
            nc.tensor.transpose(PS[0:N_SAMPLE, 7, 0:P], kv[:, 1, ST], ident[:])
            for j in range(TPH):
                tr = nc.tensor.transpose(PS[0:N_SAMPLE, 5, j * P:(j + 1) * P], hi_reg[:, j, ST], ident[:])
            tr.then_inc(S["a_s"], 1)
            pe.wait_ge(S["v_ps"], 2)
            pe.wait_ge(S["smp_in"], 64)
            for b in range(N_SAMPLE):
                for o in range(2):
                    mm = nc.tensor.matmul(PS[HEAD * o:HEAD * (o + 1), b // 2, 256 * (b % 2):256 * (b % 2) + 256],
                                          pick[0:N_SAMPLE, b, :],
                                          hv_s[0:N_SAMPLE, :].rearrange("b (t o v) -> b o t v", o=2, v=HEAD)[:, o],
                                          start=True, stop=True)
            mm.then_inc(S["a_s"], 1)
            pe.wait_ge(S["d_s"], 1)
            pe.wait_ge(S["a_ps"], 1)
            for n in range(2):
                for b in range(N_SAMPLE):
                    at_ = n * N_SAMPLE + b
                    mm = nc.tensor.matmul(PS[0:GQA, at_ // 4, CH * (at_ % 4):CH * (at_ % 4) + CH],
                                          q_s[HEAD * n:HEAD * (n + 1), :, b], k_win_s[HEAD * n:HEAD * (n + 1), b, :],
                                          start=True, stop=True)
            mm.then_inc(S["a_s"], 1)
            pe.wait_ge(S["d_s"], 2)
            for b in range(N_SAMPLE):
                for hd in range(N_HEADS):
                    p0, t = HEAD * (hd % 2), hd // 2
                    mm = nc.tensor.matmul(PS[p0:p0 + HEAD, 7, t * N_SAMPLE + b:t * N_SAMPLE + b + 1],
                                          state_s[p0:p0 + HEAD, t, b, :], hq_reg[p0:p0 + HEAD, t, N_PROMPT + b:N_PROMPT + b + 1],
                                          start=True, stop=True)
            mm.then_inc(S["a_s"], 1)
            pe.wait_ge(S["d_s"], 3)
            for at_ in range(2 * N_SAMPLE):
                mm = nc.tensor.transpose(PS[:, 4, at_ * GQA:(at_ + 1) * GQA], sm_s[0:GQA, at_, :], ident[0:GQA, 0:GQA])
            mm.then_inc(S["a_s"], 1)
            pe.wait_ge(S["v_ps"], 3)
            pe.wait_ge(S["p_ps"], 16)
            for n in range(2):
                for b in range(N_SAMPLE):
                    at_ = n * N_SAMPLE + b
                    mm = nc.tensor.matmul(PS[HEAD * n:HEAD * (n + 1), 5, :].rearrange("p (x j b) -> p x j b", x=16, b=N_SAMPLE)[:, 0, :, b],
                                          v_win_s[:, b, HEAD * n:HEAD * (n + 1)], pT_s[:, at_ * GQA:(at_ + 1) * GQA],
                                          start=True, stop=True)
            mm.then_inc(S["a_s"], 1)

            pe.wait_ge(S["v_ps"], 5)

            def cat_ready(g):
                for k in ((0, 1) if g == 0 else (g + 1,) if g + 1 < NG else ()):
                    pe.wait_ge(S["csq_done"], k + 1)
                    if k:
                        pe.wait_ge(S["croot_done"], k)
                    for j in range(TPH):
                        mm = nc.tensor.matmul(PS[:, 3 + j, :GW], head_ones[:], c_sq[:, j, :], start=True, stop=True)
                    mm.then_inc(S["css_done"], 1)
                pe.wait_ge(S["cat_lo_a"], g + 1)
                pe.wait_ge(S["cat_lo_h"], g + 1)

            pair_by_group(G_OUT, U_OUT, cat_ready)
            with pe.Fori(1, KT // 2 - 1) as p:
                for o in range(2):
                    project(G_OUT + 2 * p + o, o, U_OUT + 6 * p + 3 * o)
            pair_by_group(G_OUT + KT - 2, U_OUT + 3 * (KT - 2), mid=lambda: norm_sum(("F", 1, 0)))
            border_units(1, G_FFN2, U_FFN2)
            ffn(G_FFN2, U_FFN2, 1, 2)
            for g in range(1, NG):
                norm_sum(("F", 2, g))

        @block.gpsimd
        def _(pool):
            nc.gpsimd.memset(ones[:], 1.0).then_inc(S["ones_done"], 1)
            nc.gpsimd.memset(eps[:], EPS).then_inc(S["ones_done"], 1)

            def gain(s, use, col):
                pool.wait_ge(raw_full[s], 16 * use + 16)
                wv = raw[s][:].rearrange("p (k c) -> p k c", k=KT)
                gv = vecs[:, col:col + KT].unsqueeze(2).broadcast_to([P, KT, P])
                nc.gpsimd.tensor_tensor(wv, wv, gv, ALU.mult).then_inc(S["w_gained"], 1)

            def border_pool(b):
                def lo(g):
                    pool.wait_ge(S["x_split_hi"], NG * (b + 1) + g + 1)
                    t = slice(0, KT if g < NG - 1 else KT // 2)
                    nc.gpsimd.tensor_tensor(x_lo[:, g, t], resid[:, g, t], x_hi[:, g, t].bitcast(F32), ALU.subtract)\
                        .then_inc(S["x_split_lo"], 1)

                def fold(g):
                    pool.wait_ge(S["sq_done"], norm_no[("S", b + 1, g)] + 1)
                    nc.gpsimd.tensor_tensor(sq[:, 0:KT // 2], sq[:, 0:KT // 2], sq[:, KT // 2:], ALU.add).then_inc(S["sq_folded"], 1)

                lo(0)
                fold(0)
                lo(1)
                lo(2)
                fold(1)
                fold(2)

            pool.wait_ge(S["consts_in"], 48)
            gain(0, 0, V_GAIN["ffn1_pre"])
            gain(1, 0, V_GAIN["ffn1_pre"])
            border_pool(-1)
            nc.gpsimd.memset(y[:], 0.0).then_inc(S["y_zero"], 1)
            gain(2, 0, V_GAIN["ffn1_pre"])
            gain(0, 1, V_GAIN["ffn1_pre"])
            with pool.Fori(1, FFN_STEPS) as i:
                for o in range(4):
                    gain(o % 3, 2 * i + o // 3, V_GAIN["ffn1_pre"])
            gain(0, G_IN // 3, V_GAIN["mix_pre"])
            gain(1, G_IN // 3, V_GAIN["mix_pre"])
            border_pool(0)
            gain(0, G_IN // 3 + 1, V_GAIN["mix_pre"])
            with pool.Fori(1, IN_TILES // 2 - 1) as p:
                gain(1, G_IN // 3 + p, V_GAIN["mix_pre"])
                gain(0, G_IN // 3 + 1 + p, V_GAIN["mix_pre"])
            gain(1, G_IN // 3 + IN_TILES // 2 - 1, V_GAIN["mix_pre"])
            pool.wait_ge(S["unit_done"], UNIT_CREDIT + U_OUT)
            nc.gpsimd.memset(state[:], 0.0).then_inc(S["st_zero"], 1)
            nc.gpsimd.memset(k_win[:], 0.0).then_inc(S["st_zero"], 1)
            nc.gpsimd.memset(v_win[:], 0.0).then_inc(S["st_zero"], 1)
            nc.gpsimd.memset(k_dec[:], 0.0).then_inc(S["st_zero"], 1)
            pool.sem_inc(S["qk_done"], 12)
            pool.wait_ge(S["fmax_done"], 1)
            pool.wait_ge(S["mixc_in"], 48)
            pool.wait_ge(S["unit_evac"], EVAC_CREDIT + U_OUT)
            pool.wait_ge(S["st_zero"], 4)
            hq_of = lambda c: chunk(1, c)
            kg_of = lambda c: k_gate[:, :, bass.ds(c * CH, CH)]
            def held():
                pool.sem_inc(S["pool_held"], 1)

            with pool.Fori(0, N_CH) as c:
                def over_sum(n):
                    pool.wait_ge(S["rd_done"], 2 * c + n + 1)
                    pv = sm[:, n, :].rearrange("p (j t) -> p j t", j=GQA)
                    nc.gpsimd.tensor_tensor(pv, pv, rden[:, n, :].unsqueeze(2).broadcast_to([P, GQA, 2 * CH]),
                                            ALU.mult).then_inc(S["p_done"], 1)

                def level(l):
                    pool.wait_ge(S["lvl_done"], (5 + 5 * c + l - 1) if l >= 2 else (5 * c + 5 - l))
                    b = LEVELS[l - 1]
                    halves = lambda ap: ap.rearrange("p t (n a b) -> p t n a b", a=2, b=b)
                    pool.wait_ge(S["e_done"], 8 + 8 * c + 2 + l + 1)
                    held()
                    nc.gpsimd.tensor_tensor(q_dec[:, l % 2, :, 0:CH // 2].rearrange("p t (n b) -> p t n b", b=b),
                                            halves(hq_of(c))[:, :, :, 1], halves(dec[:, l % 2])[:, :, :, 1],
                                            ALU.mult).then_inc(S["qk_done"], 1)
                    nc.gpsimd.tensor_tensor(halves(k_dec[:, l % 2])[:, :, :, 0], halves(kg_of(c))[:, :, :, 0],
                                            halves(dec[:, l % 2])[:, :, :, 0], ALU.mult).then_inc(S["qk_done"], 1)

                pool.wait_ge(S["ts_done"], 2 * c + 2)
                pool.wait_ge(S["kw_done"], c + KW_CREDIT)
                held()
                nc.gpsimd.tensor_tensor(rot_c[:], chunk(3, c),
                                        rope_c[:, bass.ds(c * CH, CH)].unsqueeze(1).broadcast_to([P, TPH, CH]),
                                        ALU.mult).then_inc(S["t0_done"], 1)
                nc.gpsimd.tensor_tensor(rotk_c[:], kv[:, 0, bass.ds(c * CH, CH)], rope_c[:, bass.ds(c * CH, CH)],
                                        ALU.mult).then_inc(S["t0_done"], 1)
                pool.wait_ge(S["e_done"], 8 + 8 * c + 1)
                pool.wait_ge(S["o_done"], c + 1)
                held()
                nc.gpsimd.tensor_tensor(qg[:], hq_of(c), dec[:, 0], ALU.mult).then_inc(S["qk_done"], 1)
                pool.wait_ge(S["att_done"], 2 * c + 2)
                held()
                nc.gpsimd.tensor_copy(k_win[:, 0:CH], k_win[:, CH:]).then_inc(S["kw_shift"], 1)
                nc.gpsimd.tensor_copy(v_win[:, 0:CH], v_win[:, CH:]).then_inc(S["kw_shift"], 1)
                pool.wait_ge(S["lvl_done"], 5 * c + 5)
                pool.wait_ge(S["e_done"], 8 + 8 * c + 2)
                held()
                nc.gpsimd.tensor_tensor(q_dec[:, 0], hq_of(c), dec[:, 1], ALU.mult).then_inc(S["qk_done"], 1)
                pool.wait_ge(S["e_done"], 8 + 8 * c + 3)
                held()
                nc.gpsimd.tensor_tensor(k_dec[:, 0], kg_of(c), dec[:, 0], ALU.mult).then_inc(S["qk_done"], 1)
                level(1)
                level(2)
                level(3)
                level(4)
                pool.wait_ge(S["e_done"], 8 + 8 * c + 8)
                pool.wait_ge(S["kdt_done"], c + 1)
                held()
                nc.gpsimd.tensor_tensor(kd[:], kg_of(c), dec[:, 1], ALU.mult).then_inc(S["qk_done"], 1)
                over_sum(0)
                over_sum(1)
            for g in range(NG):
                pool.wait_ge(S["cat_hi_a"], g + 1)
                nc.gpsimd.tensor_tensor(x_lo[:, g, 0:TPH], q_reg[:, :, g * GW:(g + 1) * GW],
                                        x_hi[:, g, 0:TPH].bitcast(F32), ALU.subtract).then_inc(S["cat_lo_a"], 1)
            gain(0, 37, V_GAIN["ffn2_pre"])
            gain(1, 37, V_GAIN["ffn2_pre"])
            border_pool(1)
            gain(2, 22, V_GAIN["ffn2_pre"])
            nc.gpsimd.memset(y[:], 0.0).then_inc(S["y_zero"], 1)
            gain(0, 38, V_GAIN["ffn2_pre"])
            with pool.Fori(1, FFN_STEPS) as i:
                for o in range(4):
                    gain(o % 3, (22 if o == 2 else 37) + 2 * i + o // 3, V_GAIN["ffn2_pre"])

        @block.scalar
        def _(act):
            def split_hi(s, n_gained, use, prior_unit):
                if n_gained is None:
                    act.wait_ge(raw_full[s], 16 * use + 16)
                else:
                    act.wait_ge(S["w_gained"], n_gained)
                act.wait_ge(S["unit_done"], UNIT_CREDIT + prior_unit)
                nc.scalar.activation(w_hi[s][:], raw[s][:], ACT.Copy).then_inc(S["w_hi_done"], 1)

            def square(n, src):
                i = norm_no[n]
                if i >= 1:
                    act.wait_ge(S["ss_done"], i)
                nc.scalar.activation(sq[:], src, ACT.Square, scale=D_MODEL ** -0.5).then_inc(S["sq_done"], 1)

            def inverse(n):
                i = norm_no[n]
                kind, b, g = n
                act.wait_ge(S["ss_done"], i + 1)
                if i >= 2:
                    act.wait_ge(S["rms_done"], i - 1)
                nc.scalar.activation(root[:, i % 2, :], PS[:, 3 + i % 2, :GW], ACT.Ln, bias=eps[:]).then_inc(S["root_done"], 1)
                act.wait_ge(S["root_done"], i + 1)
                if kind == "F" and g == 2:
                    act.wait_ge(S["x_new"], NG * b + 1)
                dst = rms[:, g, :] if kind == "S" else rms_y[:, g % 2, :]
                nc.scalar.activation(dst, root[:, i % 2, :], ACT.Exp, scale=-0.5).then_inc(S["rms_done"], 1)

            def border_act(b, y_evac, first_pair):
                def square_y(g):
                    act.wait_ge(S["unit_evac"], EVAC_CREDIT + y_evac[g])
                    square(("F", b, g), y[:, g])

                def hi(g):
                    if b < 0:
                        act.wait_ge(resid_full[g], 16)
                    else:
                        act.wait_ge(S["x_new"], NG * b + g + 1)
                    nc.scalar.activation(x_hi[:, g], resid[:, g], ACT.Copy).then_inc(S["x_split_hi"], 1)

                if b >= 0:
                    square_y(0)
                    inverse(("F", b, 0))
                    square_y(1)
                    first_pair()
                    inverse(("F", b, 1))
                    square_y(2)
                    if b == 2:
                        inverse(("F", b, 2))
                        return
                hi(0)
                if b >= 0:
                    inverse(("F", b, 2))
                square(("S", b + 1, 0), resid[:, 0])
                hi(1)
                hi(2)
                if b < 0:
                    first_pair()
                inverse(("S", b + 1, 0))
                for g in (1, 2):
                    square(("S", b + 1, g), resid[:, g])
                    inverse(("S", b + 1, g))

            def ffn(u0, f, slot_uses, gained0, b, next_pair):
                def silus(i, t, first):
                    for g in range(NG):
                        act.wait_ge(S["unit_evac"], EVAC_CREDIT + u0 + 36 * i + 6 * t + (2 * g if first and t == 0 else g) + 1)
                        nc.scalar.activation(silu_g[:, g], silu_g[:, g], ACT.Silu).then_inc(S["silu_done"], 1)

                def h_his(i, t):
                    for g in range(NG):
                        act.wait_ge(S["h_ready"], 6 * FFN_STEPS * f + 6 * i + 3 * t + g + 1)
                        if t == 0 and g == 0:
                            act.wait_ge(S["unit_done"], UNIT_CREDIT + u0 + 36 * i)
                        nc.scalar.activation(h[:, g, 2 * t, :], prod[:, g], ACT.Copy).then_inc(S["h_hi_done"], 1)

                def step(i, first, last):
                    u = u0 + 36 * i
                    g0 = gained0 + 4 * i
                    use = lambda s, k: slot_uses[s] + 2 * i + k
                    if not first:
                        split_hi(1, g0 + 2, use(1, 0), u)
                    silus(i, 0, first)
                    split_hi(2, g0 + 3, use(2, 0), u)
                    if first:
                        split_hi(0, g0 + 4, use(0, 1), u + 6)
                        h_his(i, 0)
                    else:
                        h_his(i, 0)
                        split_hi(0, g0 + 4, use(0, 1), u + 3)
                    silus(i, 1, first)
                    split_hi(1, None, use(1, 1), u + 6)
                    split_hi(2, None, use(2, 1), u + 9)
                    h_his(i, 1)
                    if not last:
                        split_hi(0, g0 + 5, use(0, 2), u + 12)

                step(0, True, False)
                with act.Fori(1, FFN_STEPS - 1) as i:
                    step(i, False, False)
                step(FFN_STEPS - 1, False, True)
                border_act(b, [u0 + 36 * (FFN_STEPS - 1) + 12 + KT * (g + 1) for g in range(NG)], next_pair)

            act.wait_ge(S["ones_done"], 2)
            act.wait_ge(S["dve_seq"], 3)
            nc.scalar.activation(lb[:, 0:2], lb[:, 0:2], ACT.Exp).then_inc(S["cleared"], 1)
            def in_hi(n, s, use):
                split_hi(s, 44 + n + 1, use, U_IN + 3 * (n - 1))

            def in_his(p):
                in_hi(2 * p + 1, 1, 22 + p)
                in_hi(2 * p + 2, 0, 23 + p)

            def ffn1_pair():
                for s in range(2):
                    split_hi(s, s + 1, 0, -24)

            def in_pair():
                split_hi(0, 45, 22, U_IN - 24)
                split_hi(1, 46, 22, U_IN)

            border_act(-1, None, ffn1_pair)
            ffn(0, 0, [0, 0, 0], 0, 0, in_pair)
            split_hi(0, 47, 23, U_IN + 5)
            in_hi(3, 1, 23)
            in_hi(4, 0, 24)
            act.wait_ge(S["unit_evac"], EVAC_CREDIT + U_IN + 3 * TPH)
            nc.scalar.activation(f_reg, f_reg, ACT.Sigmoid).then_inc(S["sig_done"], 1)
            in_hi(5, 1, 24)
            in_hi(6, 0, 25)
            act.wait_ge(S["fmax_done"], 1)
            nc.scalar.activation(f_reg, f_reg, ACT.Ln).then_inc(S["ln_done"], 1)
            with act.Fori(3, IN_TILES // 2 - 1) as p:
                in_his(p)
            in_hi(IN_TILES - 1, 1, 22 + IN_TILES // 2 - 1)
            act.wait_ge(S["unit_evac"], EVAC_CREDIT + U_IN + 3 * 5 * TPH)
            nc.scalar.activation(hg_reg, hg_reg, ACT.Silu).then_inc(S["cg_done"], 1)
            split_hi(0, None, 22 + IN_TILES // 2, U_IN + 3 * (IN_TILES - 1))
            split_hi(1, None, 22 + IN_TILES // 2, U_OUT)

            act.sem_inc(S["e_done"], 8)
            act.sem_inc(S["ptc_done"], 2)
            act.sem_inc(S["attc_done"], 1)
            act.sem_inc(S["vw_done"], VW_CREDIT)
            act.wait_ge(S["unit_evac"], EVAC_CREDIT + U_OUT)
            act.wait_ge(S["st_zero"], 4)
            READS = [1, 2, 3, 5, 7, 9, 11, 12]
            with act.Fori(0, N_CH) as c:
                def decay(e, out, src, scale):
                    act.wait_ge(S["qk_done"], 12 + 12 * c + READS[e - 2] if e >= 2 else 12 * c + READS[6 + e])
                    nc.scalar.activation(out, src, ACT.Exp, scale=scale).then_inc(S["e_done"], 1)

                def level(l):
                    act.wait_ge(S["d_done"], 10 * c + 1 + 2 * l)
                    decay(2 + l, dec[:, l % 2], dif[:, l % 2], 1.0)

                def exponentials(n):
                    act.wait_ge(S["es_ready"], 2 * c + n + 1)
                    nc.scalar.activation(es[:, n, :], es[:, n, :], ACT.Exp).then_inc(S["es_done"], 1)
                    for j in range(GQA):
                        cols = sm[:, n, j * 2 * CH:(j + 1) * 2 * CH]
                        last = nc.scalar.activation(cols, cols, ACT.Exp, bias=nm[:, n, j:j + 1], accum_out=rsum[:, n, j:j + 1])
                    last.then_inc(S["exp_done"], 1)

                def probs(n):
                    act.wait_ge(S["pt_done"], 2 * c + n + 1)
                    act.wait_ge(S["att_done"], 2 * c + n + 1)
                    nc.scalar.activation(pT[:, n, :], PS[:, 4:6, :].rearrange("p a b -> p (a b)"),
                                         ACT.Copy).then_inc(S["ptc_done"], 1)

                act.wait_ge(S["kvp_done"], c + 1)
                nc.scalar.activation(v_c[:], kv[:, 1, bass.ds(c * CH, CH)], ACT.Copy).then_inc(S["vst_done"], 1)
                act.wait_ge(S["scan_done"], 4 * c + 4)
                decay(0, dec[:, 0], G[:], 1.0)
                act.wait_ge(S["d_done"], 10 * c + 1)
                decay(1, dec[:, 1], dif[:, 0], 1.0)
                act.wait_ge(S["kvp_done"], c + 2)
                act.wait_ge(S["kw_shift"], 2 * c + 2)
                nc.scalar.activation(v_win[:, CH:], PS[:, 5, CH:2 * CH], ACT.Copy).then_inc(S["vw_done"], 1)
                decay(2, dec[:, 0], dif[:, 0], -1.0)
                act.wait_ge(S["vt_done"], c + VT_CREDIT)
                nc.scalar.activation(hi_c[:], chunk(2, c), ACT.Copy).then_inc(S["hic_done"], 1)
                act.wait_ge(S["s_upd"], c + 1)
                nc.scalar.activation(g_end[:], G[:, :, CH - 1], ACT.Exp).then_inc(S["gend_done"], 1)
                level(1)
                level(2)
                act.wait_ge(S["vt_done"], c + VT_CREDIT + 1)
                act.wait_ge(S["s_done"], c + SD_CREDIT)
                nc.scalar.activation(V[:], PS[:, 6, :], ACT.Copy).then_inc(S["vc_done"], 1)
                level(3)
                level(4)
                exponentials(0)
                act.wait_ge(S["d_done"], 10 * c + 10)
                decay(7, dec[:, 1], dif[:, 1], 1.0)
                exponentials(1)
                act.wait_ge(S["kdt_done"], c + 2)
                nc.scalar.activation(kdT[:], PS[:, 7, :], ACT.Copy).then_inc(S["kdtc_done"], 1)
                probs(0)
                act.wait_ge(S["o_done"], c + 2)
                nc.scalar.activation(chunk(1, c), PS[:, 6, :].rearrange("p (t c) -> p t c", t=TPH),
                                     ACT.Copy).then_inc(S["oc_done"], 1)
                probs(1)
                act.wait_ge(S["att_done"], 2 * c + 4)
                nc.scalar.activation(chunk(3, c), PS[:, 6, :].rearrange("p (t c) -> p t c", t=TPH),
                                     ACT.Copy).then_inc(S["attc_done"], 1)

            ST = slice(N_PROMPT, TOK)
            act.wait_ge(S["a_s"], 1)
            nc.scalar.activation(v_row[0:N_SAMPLE], PS[0:N_SAMPLE, 7, 0:P], ACT.Copy).then_inc(S["v_ps"], 1)
            nc.scalar.activation(hv_s[0:N_SAMPLE], PS[0:N_SAMPLE, 5, :], ACT.Copy).then_inc(S["v_ps"], 1)
            act.wait_ge(S["v_s"], 1)
            nc.scalar.activation(st_s[0:GQA, 3, :], st_s[0:GQA, 3, :], ACT.Exp).then_inc(S["sig_done"], 1)
            nc.scalar.activation(sm_s[0:GQA], sm_s[0:GQA], ACT.Exp).then_inc(S["sig_done"], 1)
            act.wait_ge(S["a_s"], 5)
            nc.scalar.activation(pT_s[:], PS[:, 4, 0:2 * N_SAMPLE * GQA], ACT.Copy).then_inc(S["v_ps"], 1)
            nc.scalar.activation(hq_reg[:, :, ST], PS[:, 7, 0:TPH * N_SAMPLE].rearrange("p (t b) -> p t b", t=TPH),
                                 ACT.Copy).then_inc(S["v_ps"], 1)
            act.wait_ge(S["a_s"], 6)
            nc.scalar.activation(q_reg[:, :, ST], PS[:, 5, 0:TPH * N_SAMPLE].rearrange("p (t b) -> p t b", t=TPH),
                                 ACT.Copy).then_inc(S["v_ps"], 1)

            act.wait_ge(S["v_ps"], 5)
            gs = lambda r, g: r[:, :, g * GW:(g + 1) * GW]
            act.wait_ge(S["out_in"], 96)

            def late_hi(g):
                act.wait_ge(S["ch_done"], g + 1)
                nc.scalar.activation(x_hi[:, g, TPH:], gs(hq_reg, g), ACT.Copy).then_inc(S["cat_hi_h"], 1)

            for g in range(NG):
                if g >= 1:
                    act.wait_ge(S["css_done"], g)
                nc.scalar.activation(c_sq[:], gs(hq_reg, g), ACT.Square, scale=HEAD ** -0.5).then_inc(S["csq_done"], 1)
                nc.scalar.activation(x_hi[:, g, 0:TPH], gs(q_reg, g), ACT.Copy).then_inc(S["cat_hi_a"], 1)
                if g >= 1:
                    late_hi(g - 1)
                act.wait_ge(S["css_done"], g + 1)
                nc.scalar.activation(c_root[:], PS[:, 3:7, :GW], ACT.Ln, bias=eps[:]).then_inc(S["croot_done"], 1)
                act.wait_ge(S["croot_done"], g + 1)
                nc.scalar.activation(c_root[:], c_root[:], ACT.Exp, scale=-0.5).then_inc(S["crms_done"], 1)
            late_hi(NG - 1)

            split_hi(0, None, 34, U_OUT + 5)
            split_hi(1, None, 34, U_OUT + 6)
            with act.Fori(2, KT // 2) as p:
                split_hi(0, None, 33 + p, U_OUT + 6 * p - 3)
                split_hi(1, None, 33 + p, U_OUT + 6 * p)

            def ffn2_pair():
                for s in range(2):
                    split_hi(s, 67 + s, 37, U_FFN2)

            border_act(1, [U_OUT + 3 * (KT - 2) + 2 * (g + 1) for g in range(NG)], ffn2_pair)
            ffn(U_FFN2, 1, [37, 37, 22], 66, 2, lambda: None)

        @block.vector
        def _(dve):
            seq = Seq(dve, S["dve_seq"])
            dve.sem_inc(S["unit_evac"], EVAC_CREDIT)
            dve.sem_inc(S["w_ready"], READY_CREDIT)
            dve.wait_ge(S["consts_in"], 48)
            for j, name in enumerate(("ffn1_post", "ffn2_post")):
                nc.vector.tensor_scalar(half_gain[:, j, :], vecs[:, V_GAIN[name]:V_GAIN[name] + 8], 0.5, None, ALU.mult)\
                    .then_inc(S["gain_done"], 1)
            dve.wait_ge(S["gain_done"], 2)

            def split_lo(n, s):
                dve.wait_ge(S["w_hi_done"], n + 1)
                nc.vector.tensor_tensor(w_lo[s][:], raw[s][:], w_hi[s][:].bitcast(F32), ALU.subtract)\
                    .then_inc(S["w_ready"], 1)

            def fold(n):
                dve.wait_ge(S["sq_done"], norm_no[n] + 1)
                nc.vector.tensor_tensor(sq[:, 0:KT // 2], sq[:, 0:KT // 2], sq[:, KT // 2:], ALU.add).then_inc(S["sq_folded"], 1)

            def finish(b, g):
                dve.wait_ge(S["rms_done"], norm_no[("F", b, g)] + 1)
                rb = rms_y[:, g % 2, :].unsqueeze(1).broadcast_to([P, KT, GW])
                nc.vector.tensor_tensor(y[:, g], y[:, g], rb, ALU.mult).then_inc(S["y_scaled"], 1)
                dve.wait_ge(S["y_scaled"], NG * b + g + 1)
                dve.wait_ge(resid_full[g], 16 if b == 0 else 32)
                for m in range(KT):
                    st = nc.vector.scalar_tensor_tensor(resid[:, g, m, :], y[:, g, m, :], GAIN_F[b][:, m:m + 1],
                                                        resid[:, g, m, :], ALU.mult, ALU.add)
                st.then_inc(S["x_new"], 1)

            def border_dve(b, next_pair):
                if b >= 0:
                    fold(("F", b, 1))
                    finish(b, 0)
                    fold(("F", b, 2))
                    next_pair()
                    finish(b, 1)
                    finish(b, 2)
                    if b == 2:
                        return
                else:
                    next_pair()
                g, t = NG - 1, slice(KT // 2, KT)
                dve.wait_ge(S["x_split_hi"], NG * (b + 2))
                nc.vector.tensor_tensor(x_lo[:, g, t], resid[:, g, t], x_hi[:, g, t].bitcast(F32), ALU.subtract)\
                    .then_inc(S["x_split_lo_late"], 1)

            def ffn(n0, u0, f, b, next_pair):
                def evac(u):
                    dve.wait_ge(S["unit_done"], UNIT_CREDIT + u + 1)

                def step(i, first, last):
                    u, n = u0 + 36 * i, n0 + 6 * i
                    for t in range(2):
                        by_group = first and t == 0

                        def gate(g):
                            v = 2 * g if by_group else g
                            evac(u + 6 * t + v)
                            nc.vector.tensor_tensor(silu_g[:, g], PS[:, v % 3, :GW], rms[:, g], ALU.mult).then_inc(S["unit_evac"], 1)

                        def up(g):
                            v = 2 * g + 1 if by_group else 3 + g
                            evac(u + 6 * t + v)
                            nc.vector.tensor_tensor(prod[:, g], PS[:, v % 3, :GW], rms[:, g], ALU.mult).then_inc(S["unit_evac"], 1)

                        def gated(g):
                            v = 2 * g + 1 if by_group else 3 + g
                            dve.wait_ge(S["unit_evac"], EVAC_CREDIT + u + 6 * t + v + 1)
                            dve.wait_ge(S["silu_done"], 6 * FFN_STEPS * f + 6 * i + 3 * t + g + 1)
                            nc.vector.tensor_tensor(prod[:, g], prod[:, g], silu_g[:, g], ALU.mult).then_inc(S["h_ready"], 1)

                        if by_group:
                            for g in range(NG):
                                dve.wait_ge(S["rms_done"], norm_no[("S", 2 * f, g)] + 1)
                                gate(g)
                                if g == NG - 1:
                                    split_lo(n + 2, 2)
                                up(g)
                            for g in range(NG):
                                gated(g)
                        else:
                            split_lo(n + 2 * t + 1, (2 * t + 1) % 3)
                            for g in range(NG):
                                gate(g)
                            split_lo(n + 2 * t + 2, (2 * t + 2) % 3)
                            if t == 1:
                                split_lo(n + 5, 2)
                            for g in range(NG):
                                up(g)
                                gated(g)
                        for g in range(NG):
                            dve.wait_ge(S["h_hi_done"], 6 * FFN_STEPS * f + 6 * i + 3 * t + g + 1)
                            nc.vector.tensor_tensor(h[:, g, 2 * t + 1, :], prod[:, g], h[:, g, 2 * t, :].bitcast(F32),
                                                    ALU.subtract).then_inc(S["h_lo_done"], 1)
                    if not last:
                        split_lo(n + 6, 0)
                    if first:
                        dve.wait_ge(S["y_zero"], f + 1)
                    for d in range(NG * KT):
                        g, m = d // KT, d % KT
                        if last and (g, m) == (NG - 1, 0):
                            fold(("F", b, 0))
                        evac(u + 12 + d)
                        nc.vector.tensor_tensor(y[:, g, m, :], y[:, g, m, :], PS[:, d % 3, :GW], ALU.add).then_inc(S["unit_evac"], 1)

                step(0, True, False)
                with dve.Fori(1, FFN_STEPS - 1) as i:
                    step(i, False, False)
                step(FFN_STEPS - 1, False, True)
                border_dve(b, next_pair)

            def splits(n):
                return lambda: (split_lo(n, 0), split_lo(n + 1, 1))

            seq(nc.vector.tensor_tensor(lb[:, 0], vecs[:, V_LB0:V_LB0 + TPH], vecs[:, V_LB1:V_LB1 + TPH], ALU.max))
            seq(nc.vector.tensor_tensor(lb[:, 1], vecs[:, V_LB1:V_LB1 + TPH], lb[:, 0], ALU.subtract))
            seq(nc.vector.tensor_tensor(lb[:, 0], vecs[:, V_LB0:V_LB0 + TPH], lb[:, 0], ALU.subtract))
            dve.wait_ge(S["cleared"], 1)
            seq(nc.vector.tensor_tensor(lb[:, 2], lb[:, 0], lb[:, 1], ALU.add))
            seq(nc.vector.reciprocal(lb[:, 2], lb[:, 2]))
            seq(nc.vector.tensor_tensor(lb[:, 0], lb[:, 0], lb[:, 2], ALU.mult))
            seq(nc.vector.tensor_scalar(lb[:, 1], lb[:, 0], -1.0, 1.0, ALU.mult, ALU.add))

            border_dve(-1, splits(0))
            ffn(0, 0, 0, 0, splits(G_IN))

            def in_tile(n, o, dst, scale, split=True):
                if split:
                    split_lo(G_IN + n + 1, 1 - o)
                for g in range(NG):
                    dve.wait_ge(S["unit_done"], UNIT_CREDIT + U_IN + 3 * n + g + 1)
                    if scale is None:
                        ev = nc.vector.tensor_tensor(dst(g), PS[:, g, :GW], rms[:, g], ALU.mult)
                    else:
                        ev = nc.vector.scalar_tensor_tensor(dst(g), PS[:, g, :GW], scale, rms[:, g], ALU.mult, ALU.mult)
                    ev.then_inc(S["unit_evac"], 1)

            def in_pair(p, scale=None):
                for o in range(2):
                    in_tile(2 * p + o, o, lambda g: R[:, 2 * p + o, g * GW:(g + 1) * GW], scale)

            for g in range(NG):
                dve.wait_ge(S["rms_done"], norm_no[("S", 1, g)] + 1)
                for o in range(2):
                    if (g, o) == (NG - 1, 1):
                        split_lo(G_IN + 2, 0)
                    dve.wait_ge(S["unit_done"], UNIT_CREDIT + U_IN + 2 * g + o + 1)
                    nc.vector.tensor_tensor(R[:, o, g * GW:(g + 1) * GW], PS[:, (2 * g + o) % 3, :GW], rms[:, g],
                                            ALU.mult).then_inc(S["unit_evac"], 1)
            in_pair(1)
            dve.wait_ge(S["sig_done"], 1)
            dve.wait_ge(S["spilled"], 16 * NG)
            for j in range(TPH):
                last = nc.vector.tensor_scalar(f_reg[:, j], f_reg[:, j], lb[:, 1, j:j + 1], lb[:, 0, j:j + 1], ALU.mult, ALU.add)
            seq(last)
            nc.vector.tensor_copy(f_s[:], f_reg[:, :, N_PROMPT:])
            seq(nc.vector.tensor_scalar(k_gate[:], f_reg, -1.0, 1.0, ALU.mult, ALU.add))
            nc.vector.tensor_scalar(f_reg, f_reg, F_MIN, None, ALU.max).then_inc(S["fmax_done"], 1)
            with dve.Fori(2, 4) as p:
                in_pair(p, HEAD ** -0.5)
            with dve.Fori(4, IN_TILES // 2 - 1) as p:
                in_pair(p)
            for o in range(2):
                in_tile(IN_TILES - 2 + o, o, lambda g: kv[:, o, g * GW:(g + 1) * GW], None)
            split_lo(G_OUT + 1, 1)

            dve.sem_inc(S["lvl_done"], 5)
            dve.sem_inc(S["gend_done"], GE_CREDIT)
            dve.sem_inc(S["o_done"], 1)
            dve.sem_inc(S["kdt_done"], 1)
            dve.sem_inc(S["s_upd"], 1)
            dve.sem_inc(S["vt_done"], VT_CREDIT)
            dve.sem_inc(S["s_done"], SD_CREDIT)
            dve.sem_inc(S["kvp_done"], 1)
            dve.sem_inc(S["att_done"], 2)
            dve.sem_inc(S["ts_done"], 2)
            dve.sem_inc(S["kw_done"], KW_CREDIT)
            dve.wait_ge(S["mixc_in"], 48)
            dve.wait_ge(S["ln_done"], 1)
            dve.wait_ge(S["st_zero"], 4)
            DREADS = [3, 4, 5, 6, 7, 8]

            with dve.Fori(0, N_CH) as c:
                seq.enter(c, 9)
                tok = bass.ds(c * CH, CH)
                dve.wait_ge(S["gend_done"], c + GE_CREDIT)
                for j in range(TPH):
                    nc.vector.tensor_tensor_scan(G[:, j], ones[:], R[:, j, tok], 0.0, ALU.mult, ALU.add)\
                        .then_inc(S["scan_done"], 1)
                dve.wait_ge(S["scan_done"], 4 * c + 4)

                def free(d):
                    dve.wait_ge(S["e_done"], 8 + 8 * c + DREADS[d - 2] if d >= 2 else 8 * c + DREADS[4 + d])

                def blocks(ap, b):
                    return ap.rearrange("p t (n b) -> p (t n) b", b=b)

                def intra():
                    free(0)
                    gv = blocks(G[:], SUB)
                    nc.vector.tensor_tensor(blocks(dif[:, 0], SUB), gv,
                                            gv[:, :, SUB // 2 - 1:SUB // 2].broadcast_to([P, TPH * CH // SUB, SUB]),
                                            ALU.subtract).then_inc(S["d_done"], 1)

                def level(l):
                    b = LEVELS[l - 1]
                    gv, dv = blocks(G[:], 2 * b), blocks(dif[:, l % 2], 2 * b)
                    ref = gv[:, :, b - 1:b].broadcast_to([P, TPH * CH // (2 * b), b])
                    free(l)
                    nc.vector.tensor_tensor(dv[:, :, 0:b], ref, gv[:, :, 0:b], ALU.subtract).then_inc(S["d_done"], 1)
                    nc.vector.tensor_tensor(dv[:, :, b:], gv[:, :, b:], ref, ALU.subtract).then_inc(S["d_done"], 1)

                def to_end():
                    free(5)
                    nc.vector.tensor_tensor(dif[:, 1], G[:, :, CH - 1:CH].broadcast_to([P, TPH, CH]), G[:],
                                            ALU.subtract).then_inc(S["d_done"], 1)

                def weights(l):
                    dve.wait_ge(S["lvl_done"], 5 + 5 * c + l + 1)
                    if l == 0:
                        dve.wait_ge(S["o_done"], c + 1)
                        mask = mixc[:, M_SUB:M_SUB + CH].unsqueeze(1).broadcast_to([P, N_HEADS, CH])
                        nc.vector.tensor_tensor(A[:], PS[:, 0:2, :].rearrange("p a (h t) -> p (a h) t", t=CH), mask,
                                                ALU.mult).then_inc(S["a_done"], 1)
                        return
                    b, at_ = LEVELS[l - 1], M_LVL + (l - 1) * CH
                    late = lambda ap: ap.rearrange("p h (n a b) -> p h n a b", a=2, b=b)[:, :, :, 1]
                    mask = late(mixc[:, at_:at_ + CH].bitcast(U32).unsqueeze(1)).broadcast_to([P, TPH, CH // (2 * b), b])
                    dve.wait_ge(S["a_done"], 5 * c + l)
                    dve.sem_inc(S["dve_held"], 1)
                    for odd in range(2):
                        src = PS[:, 2 * (l % 2) + odd, 0:TPH * CH // 2].rearrange("p (h n b) -> p h n b", h=TPH, b=b)
                        cp = nc.vector.copy_predicated(late(A[:, TPH * odd:TPH * (odd + 1), :]), mask, src)
                    cp.then_inc(S["a_done"], 1)

                def sub_max(n):
                    dve.wait_ge(S["sc_done"], 2 * c + n + 1)
                    sv = sm[:, n, :].rearrange("p (j t) -> p j t", j=GQA)
                    nc.vector.scalar_tensor_tensor(sv, PS[:, 4:6, :].rearrange("p a (j t) -> p (a j) t", t=2 * CH),
                                                   HEAD ** -0.5, m_cur.unsqueeze(1).broadcast_to([P, GQA, 2 * CH]),
                                                   ALU.mult, ALU.add).then_inc(S["sm_done"], 1)
                    dve.wait_ge(S["sm_done"], 2 * c + n + 1)
                    sinks = vecs[:, V_SINK + GQA * n:V_SINK + GQA * (n + 1)]
                    seq(nc.vector.tensor_reduce(mx[:, n, :], sv, AX_X, ALU.max))
                    seq(nc.vector.tensor_tensor(mx[:, n, :], mx[:, n, :], sinks, ALU.max))
                    seq(nc.vector.tensor_scalar(nm[:, n, :], mx[:, n, :], -1.0, None, ALU.mult))
                    nc.vector.tensor_tensor(es[:, n, :], sinks, mx[:, n, :], ALU.subtract).then_inc(S["es_ready"], 1)

                def over(n):
                    dve.wait_ge(S["exp_done"], 2 * c + n + 1)
                    seq(nc.vector.tensor_tensor(rsum[:, n, :], rsum[:, n, :], es[:, n, :], ALU.add))
                    nc.vector.reciprocal(rden[:, n, :], rsum[:, n, :]).then_inc(S["rd_done"], 1)

                intra()
                level(1)
                dve.wait_ge(S["ropq_done"], c + 1)
                nc.vector.tensor_tensor(rot_s[:], PS[:, 4, :].rearrange("p (t c) -> p t c", t=TPH),
                                        rope_s[:, tok].unsqueeze(1).broadcast_to([P, TPH, CH]), ALU.mult).then_inc(S["ts_done"], 1)
                dve.wait_ge(S["ts_done"], 2 * c + 3)
                dve.wait_ge(S["t0_done"], 2 * c + 2)
                nc.vector.tensor_tensor(q_rot[:], rot_c[:], rot_s[:], ALU.add).then_inc(S["qs_done"], 1)
                dve.wait_ge(S["vw_done"], c + 1 + VW_CREDIT)
                nc.vector.tensor_tensor(rotk_s[:], PS[:, 5, 0:CH], rope_s[:, tok], ALU.mult).then_inc(S["ts_done"], 1)
                dve.wait_ge(S["ts_done"], 2 * c + 4)
                dve.wait_ge(S["kw_shift"], 2 * c + 2)
                nc.vector.tensor_tensor(k_win[:, CH:], rotk_c[:], rotk_s[:], ALU.add).then_inc(S["kw_done"], 1)
                level(2)
                weights(0)
                level(3)
                weights(1)
                level(4)
                sub_max(0)
                weights(2)
                to_end()
                weights(3)
                sub_max(1)
                over(0)
                weights(4)
                seq(nc.vector.tensor_copy(m_cur, mixc[:, M_BAND:M_BAND + 2 * CH]))
                over(1)
                dve.wait_ge(S["gend_done"], c + 1 + GE_CREDIT)
                dve.wait_ge(S["o_done"], c + 2)
                nc.vector.tensor_tensor(state[:], state[:], g_end[:].unsqueeze(2).broadcast_to([P, TPH, HEAD]),
                                        ALU.mult).then_inc(S["s_scaled"], 1)
                dve.wait_ge(S["s_scaled"], c + 1)
                dve.wait_ge(S["s_done"], c + 1 + SD_CREDIT)
                nc.vector.tensor_tensor(state[:], state[:], PS[:, 7, 0:TPH * HEAD].rearrange("p (t v) -> p t v", t=TPH),
                                        ALU.add).then_inc(S["s_upd"], 1)
                seq.leave(N_CH)

            ST = slice(N_PROMPT, TOK)
            rc8 = rope_c[:, ST].unsqueeze(1).broadcast_to([P, TPH, N_SAMPLE])
            rs8 = rope_s[:, ST].unsqueeze(1).broadcast_to([P, TPH, N_SAMPLE])
            dve.wait_ge(S["a_s"], 1)
            dve.wait_ge(S["smp_in"], 48)
            nc.vector.tensor_tensor(qt_s[:], q_reg[:, :, ST], rc8, ALU.mult)
            nc.vector.tensor_tensor(qu_s[:], PS[:, 6, 0:TPH * N_SAMPLE].rearrange("p (t b) -> p t b", t=TPH), rs8, ALU.mult)
            nc.vector.tensor_tensor(kt_s[:, 0], kv[:, 0, ST], rope_c[:, ST], ALU.mult)
            seq(nc.vector.tensor_tensor(kt_s[:, 1], PS[:, 6, 32:32 + N_SAMPLE], rope_s[:, ST], ALU.mult))
            seq(nc.vector.tensor_tensor(q_s[:], qt_s[:], qu_s[:], ALU.add))
            nc.vector.tensor_tensor(k_win_s[:, :, WINDOW - 1], kt_s[:, 0], kt_s[:, 1], ALU.add).then_inc(S["d_s"], 1)
            seq(nc.vector.tensor_tensor(state_s[:].rearrange("p t b v -> p (t b) v"), state_s[:].rearrange("p t b v -> p (t b) v"),
                                        f_s[:].rearrange("p t b -> p (t b)").unsqueeze(2).broadcast_to([P, TPH * N_SAMPLE, HEAD]), ALU.mult))
            dve.wait_ge(S["a_s"], 2)
            for t in range(TPH):
                src = PS[:, 0:4, :].rearrange("p a (b t v) -> p t (a b) v", b=2, t=TPH)[:, t]
                kvp = nc.vector.tensor_tensor(kv_s[:, t], src, k_gate[:, t, ST].unsqueeze(2).broadcast_to([P, N_SAMPLE, HEAD]), ALU.mult)
            kvp.then_inc(S["a_ps"], 1)
            dve.wait_ge(S["a_ps"], 1)
            nc.vector.tensor_tensor(state_s[:], state_s[:], kv_s[:], ALU.add).then_inc(S["d_s"], 1)
            dve.wait_ge(S["a_s"], 3)
            W = 2 * N_SAMPLE
            seq(nc.vector.tensor_scalar(sm_s[0:GQA], PS[0:GQA, 0:4, :].rearrange("p a (i t) -> p (a i) t", t=CH),
                                        HEAD ** -0.5, None, ALU.mult))
            seq(nc.vector.tensor_reduce(st_s[0:GQA, 0, :], sm_s[0:GQA], AX_X, ALU.max))
            seq(nc.vector.tensor_copy(st_s[0:GQA, 1, :].rearrange("p (n b) -> p n b", n=2),
                                      vecs[0:GQA, V_SINKT:V_SINKT + 2].unsqueeze(2).broadcast_to([GQA, 2, N_SAMPLE])))
            seq(nc.vector.tensor_tensor(st_s[0:GQA, 2, :], st_s[0:GQA, 0, :], st_s[0:GQA, 1, :], ALU.max))
            nc.vector.tensor_tensor(st_s[0:GQA, 3, :], st_s[0:GQA, 1, :], st_s[0:GQA, 2, :], ALU.subtract)
            nc.vector.tensor_tensor(sm_s[0:GQA], sm_s[0:GQA], st_s[0:GQA, 2, :].unsqueeze(2).broadcast_to([GQA, W, WINDOW]),
                                    ALU.subtract).then_inc(S["v_s"], 1)
            dve.wait_ge(S["sig_done"], 3)
            seq(nc.vector.tensor_reduce(st_s[0:GQA, 4, :], sm_s[0:GQA], AX_X, ALU.add))
            seq(nc.vector.tensor_tensor(st_s[0:GQA, 5, :], st_s[0:GQA, 4, :], st_s[0:GQA, 3, :], ALU.add))
            seq(nc.vector.reciprocal(st_s[0:GQA, 6, :], st_s[0:GQA, 5, :]))
            nc.vector.tensor_tensor(sm_s[0:GQA], sm_s[0:GQA], st_s[0:GQA, 6, :].unsqueeze(2).broadcast_to([GQA, W, WINDOW]),
                                    ALU.mult).then_inc(S["d_s"], 1)

            gs = lambda r, g: r[:, :, g * GW:(g + 1) * GW]
            dve.wait_ge(S["out_in"], 96)
            dve.wait_ge(S["cg_done"], 1)
            for g in range(NG):
                dve.wait_ge(S["crms_done"], g + 1)
                nc.vector.tensor_tensor(gs(hq_reg, g), gs(hq_reg, g), c_root[:], ALU.mult).then_inc(S["co_done"], 1)
                dve.wait_ge(S["co_done"], g + 1)
                nc.vector.scalar_tensor_tensor(gs(hq_reg, g), gs(hq_reg, g), vecs[:, V_OUTG:V_OUTG + 1], gs(hg_reg, g),
                                               ALU.mult, ALU.mult).then_inc(S["ch_done"], 1)
                dve.wait_ge(S["cat_hi_h"], g + 1)
                nc.vector.tensor_tensor(x_lo[:, g, TPH:], gs(hq_reg, g), x_hi[:, g, TPH:].bitcast(F32),
                                        ALU.subtract).then_inc(S["cat_lo_h"], 1)

            def out_by_group(p, between):
                for g in range(NG):
                    for o in range(2):
                        if (g, o) in between:
                            between[g, o]()
                        v = 6 * p + 2 * g + o
                        dve.wait_ge(S["unit_done"], UNIT_CREDIT + U_OUT + v + 1)
                        nc.vector.tensor_copy(y[:, g, 2 * p + o, :], PS[:, v % 3, :GW]).then_inc(S["unit_evac"], 1)

            out_by_group(0, {(NG - 1, 1): lambda: split_lo(G_OUT + 2, 0)})
            with dve.Fori(1, KT // 2 - 1) as p:
                for o in range(2):
                    split_lo(G_OUT + 2 * p + o + 1, 1 - o)
                    for g in range(NG):
                        dve.wait_ge(S["unit_done"], UNIT_CREDIT + U_OUT + 6 * p + 3 * o + g + 1)
                        nc.vector.tensor_copy(y[:, g, 2 * p + o, :], PS[:, g, :GW]).then_inc(S["unit_evac"], 1)
            split_lo(G_OUT + KT - 1, 1)
            out_by_group(KT // 2 - 1, {(NG - 1, 0): lambda: fold(("F", 1, 0))})
            border_dve(1, splits(G_FFN2))
            ffn(G_FFN2, U_FFN2, 1, 2, lambda: None)


VW_CREDIT = KW_CREDIT = VT_CREDIT = SD_CREDIT = GE_CREDIT = 1


def tables():
    ident = np.eye(P, dtype=np.float32)
    head_ones = np.kron(np.eye(2), np.ones((HEAD, HEAD))).astype(np.float32)
    s, t = np.arange(CH)[:, None], np.arange(CH)[None]
    mixc = np.zeros((P, NM), np.float32)
    for i, b in enumerate(LEVELS):
        mixc[:, M_LVL + i * CH:M_LVL + (i + 1) * CH] = (s // (2 * b) == t // (2 * b)) & (s // b < t // b)
    mixc[:, M_SUB:M_SUB + CH] = (s // SUB == t // SUB) & (s <= t)
    key = np.arange(2 * CH)[None]
    rel = s + WINDOW - key
    band = (rel >= 0) & (rel < WINDOW)
    mixc[:, M_BAND:M_BAND + 2 * CH] = np.where(band, 0.0, NEG)
    mixc[:, M_FIRST:M_FIRST + 2 * CH] = np.where(band & (key >= WINDOW), 0.0, NEG)
    half = ROT // 2
    inv = np.float32(THETA) ** (-np.arange(half, dtype=np.float32) / np.float32(half))
    pos = np.concatenate([np.arange(N_PROMPT), np.full(N_SAMPLE, PAST_LEN)]).astype(np.float32)
    ang = inv[:, None] * pos[None]
    rope = np.zeros((2, P, TOK), np.float32)
    rope[0] = 1.0
    for h0 in (0, HEAD):
        for d in range(half):
            mixc[h0 + half + d, M_ROT + h0 + d] = -1.0
            mixc[h0 + d, M_ROT + h0 + half + d] = 1.0
            for at in (h0 + d, h0 + half + d):
                rope[0, at], rope[1, at] = np.cos(ang[d]), np.sin(ang[d])
    pick = np.repeat(np.eye(N_SAMPLE, dtype=np.float32)[:, :, None], HEAD, axis=2)
    return {"ident": ident, "head_ones": head_ones, "mixc": mixc, "rope": rope, "pick": pick}


def kernel(**inputs):
    import concourse.bacc as bacc
    from concourse.bass_utils import run_bass_kernel_spmd as run

    c = np.ascontiguousarray
    x = np.concatenate([inputs["x_prompt"][0], inputs["x_sample"][:, 0]], axis=0)
    arrays = {"x": c(x.reshape(NG, GW, KT, P).transpose(0, 3, 2, 1))}
    for f in ("1", "2"):
        w = inputs[f"ffn{f}_w_gu"][0].reshape(KT, P, 2, HT, P)
        arrays["w_gu" + f] = c(w.transpose(3, 2, 1, 0, 4)).reshape(2 * HT, P, KT * P)
        arrays["w_down" + f] = c(inputs[f"ffn{f}_w_down"][0].reshape(HT, P, D_MODEL))
    cols = [inputs[n][0].reshape(KT, P).T for n in
            ("ffn1_pre_g", "ffn1_post_g", "mix_pre_g", "mix_post_g", "ffn2_pre_g", "ffn2_post_g")]
    cols += [inputs["hgrn_lb"][r].reshape(TPH, P).T for r in range(2)]
    cols += [np.tile(inputs["hgrn_out_g"][0], 2)[:, None], np.tile(inputs["attn_sinks"][0][None], (P, 1)),
             np.tile(inputs["attn_sinks"][0].reshape(N_KV, GQA).T, (P // GQA, 1))]
    arrays["vecs"] = c(np.concatenate(cols, axis=1))
    w_in = inputs["w_in"][0]
    q, k, v, hq, hf, hi, hg = np.split(w_in, np.cumsum([512, 128, 128, 512, 512, 512])[:6], axis=1)
    q = q.reshape(D_MODEL, N_KV, GQA, HEAD).transpose(0, 2, 1, 3).reshape(D_MODEL, 512)
    w_in = np.concatenate([hf, hq, hi, q, hg, k, v], axis=1)
    arrays["w_in"] = c(w_in.reshape(KT, P, IN_TILES, P).transpose(2, 1, 0, 3)).reshape(IN_TILES, P, KT * P)
    w_out = inputs["w_out"][0]
    w_att = w_out[:512].reshape(N_KV, GQA, HEAD, D_MODEL).transpose(1, 0, 2, 3).reshape(512, D_MODEL)
    w_out = np.concatenate([w_att, w_out[512:]], axis=0)
    arrays["w_out"] = c(w_out.reshape(KT, P, KT, P).transpose(2, 1, 0, 3)).reshape(KT, P, KT * P)
    kc, vc = inputs["cache_win_k"][0], inputs["cache_win_v"][0]
    arrays["k_cache"] = c(kc[:, 1:].reshape(N_SAMPLE, WINDOW - 1, P).transpose(2, 0, 1))
    arrays["v_cache"] = c(vc[:, 1:].reshape(N_SAMPLE, WINDOW - 1, P).transpose(1, 0, 2))
    arrays["state"] = c(inputs["state_hgrn"][0].reshape(N_SAMPLE, TPH, 2, HEAD, HEAD)
                        .transpose(2, 3, 1, 0, 4)).reshape(P, TPH, N_SAMPLE, HEAD)
    arrays.update(tables())

    nc = bacc.Bacc("TRN2", target_bir_lowering=False, num_devices=1)
    ins = {k: nc.dram_tensor("in_" + k, v.shape, F32, kind="ExternalInput").ap() for k, v in arrays.items()}
    stream = (NG, P, KT, GW)
    shapes = {"y": stream, "k_win": (P, CH), "v_win": (P, CH), "state": (P, TPH, HEAD),
              "k_win_s": (P, N_SAMPLE, WINDOW), "v_win_s": (P, N_SAMPLE, P), "state_s": (P, TPH, N_SAMPLE, HEAD)}
    outs = {k: nc.dram_tensor("out_" + k, s, F32, kind="ExternalOutput").ap() for k, s in shapes.items()}
    for k in ("x1", "x2"):
        outs[k] = nc.dram_tensor("stream_" + k, stream, F32, kind="Internal").ap()
    build(nc, ins, outs)
    r = run(nc, [{"in_" + k: v for k, v in arrays.items()}], core_ids=[0]).results[0]
    yv = r["out_y"].transpose(0, 3, 2, 1).reshape(TOK, D_MODEL)
    kp = r["out_k_win"].T.reshape(1, 1, CH, N_KV, HEAD)
    vp = r["out_v_win"].reshape(1, 1, CH, N_KV, HEAD)
    sp = r["out_state"].reshape(2, HEAD, TPH, HEAD).transpose(2, 0, 1, 3).reshape(1, 1, N_HEADS, HEAD, HEAD)
    ks = r["out_k_win_s"].transpose(1, 2, 0).reshape(1, N_SAMPLE, WINDOW, N_KV, HEAD)
    vs = r["out_v_win_s"].transpose(1, 0, 2).reshape(1, N_SAMPLE, WINDOW, N_KV, HEAD)
    ss = r["out_state_s"].reshape(2, HEAD, TPH, N_SAMPLE, HEAD).transpose(3, 2, 0, 1, 4)\
        .reshape(1, N_SAMPLE, N_HEADS, HEAD, HEAD)
    return tuple(map(c, (yv[:N_PROMPT][None], yv[N_PROMPT:][:, None], kp, vp, sp, ks, vs, ss)))
```

```python
from contextlib import ExitStack

import numpy as np

import concourse.bass as bass
from concourse import mybir

F32 = mybir.dt.float32
F32R = mybir.dt.float32r
U32 = mybir.dt.uint32
ALU = mybir.AluOpType
ACT = mybir.ActivationFunctionType
AX_X = mybir.AxisListType.X

P = 128
D_MODEL, D_FF = 1024, 2816
N_PROMPT, N_SAMPLE, PAST_LEN = 1024, 8, 2048
TOK = N_PROMPT + N_SAMPLE
NG = 3
GW = TOK // NG
KT = D_MODEL // P
HT = D_FF // P
HEAD, N_HEADS, N_KV, GQA = 64, 8, 2, 4
WINDOW, ROT, THETA = 128, 16, 500000.0
EPS, NEG = 1e-6, -1e30
CH = 128
N_CH = N_PROMPT // CH
TPH = 4
POOL_TILES = 3
IN_TILES = 22
F_MIN = 2.0 ** -32
LEVELS = (8, 16, 32, 64)
SUB = 8

FFN_STEPS = HT // 2
FFN_GRANULES, FFN_UNITS = 6, 4 * NG + NG * KT
G_IN = FFN_STEPS * FFN_GRANULES
G_OUT = G_IN + IN_TILES
G_FFN2 = G_OUT + KT
U_IN = FFN_STEPS * FFN_UNITS
U_OUT = U_IN + NG * IN_TILES
U_FFN2 = U_OUT + NG * KT
Q_CREDIT, K_CREDIT = 5, 7
UNIT_CREDIT, EVAC_CREDIT, READY_CREDIT = FFN_UNITS, NG, 3
VW_CREDIT = KW_CREDIT = VT_CREDIT = SD_CREDIT = GE_CREDIT = 1

V_GAIN = {"ffn1_pre": 0, "ffn1_post": 8, "mix_pre": 16, "mix_post": 24, "ffn2_pre": 32, "ffn2_post": 40}
V_LB0, V_LB1, V_OUTG, V_SINK, V_SINKT, NV = 48, 52, 56, 57, 65, 67
M_LVL, M_SUB, M_BAND, M_FIRST, M_ROT, NM = 0, 512, 640, 896, 1152, 1280


class Seq:

    def __init__(self, eng, sem):
        self.eng, self.sem, self.n, self.i, self.per, self.left = eng, sem, 0, None, 0, 0

    def __call__(self, ins):
        self.n += 1
        ins.then_inc(self.sem, 1)
        self.eng.wait_ge(self.sem, self.n if self.i is None else self.i * self.per + self.n)

    def enter(self, i, per):
        self.i, self.per, self.at = i, per, self.n

    def leave(self, times):
        assert self.n - self.at == self.per, (self.n - self.at, self.per)
        self.n = self.at + times * self.per
        self.i = None


def build(nc, ins, outs):
    ctx = ExitStack()
    with ctx:
        sems = {}

        def sem(name):
            sems[name] = ctx.enter_context(nc.semaphore(name))
            return sems[name]

        at = [(nc.sbuf_base + 31) // 32 * 32]
        end = nc.sbuf_usable_end

        def put(name, shape, dt, offset=None):
            size = 4 * int(np.prod(shape[1:]))
            if offset is None:
                offset = at[0]
                at[0] += (size + 31) // 32 * 32
            assert offset + size <= end, (name, offset + size - end)
            return nc.alloc_sbuf_tensor_at(name, shape, dt, offset=offset)

        vecs = put("vecs", [P, NV], F32)
        half_gain = put("half_gain", [P, 2, KT], F32)
        lb = put("lb", [P, 3, TPH], F32)
        ident = put("ident", [P, P], F32)
        ones = put("ones", [P, P], F32)
        eps = put("eps", [P, 1], F32)
        head_ones = put("head_ones", [P, P], F32)
        rms = put("rms", [P, NG, GW], F32)
        raw = [put(f"raw{s}", [P, 1024], F32) for s in range(2)]
        w_hi = [put(f"w_hi{s}", [P, 1024], F32R) for s in range(2)]
        w_lo = [put(f"w_lo{s}", [P, 1024], F32R) for s in range(2)]
        x_at = at[0]
        x_hi = put("x_hi", [P, NG, KT, GW], F32R)
        x_lo = put("x_lo", [P, NG, KT, GW], F32R)
        x_end = zone = at[0]

        y = put("y", [P, NG, KT, GW], F32)
        resid = put("resid", [P, NG, KT, GW], F32)
        h_at = at[0]
        h = put("h", [P, NG, 4, GW], F32R)
        sq_bufs = [put("sq_a", [P, KT, GW], F32), put("sq_b", [P, KT, GW], F32, h_at + 4 * GW * 4)]
        raw.append(put("raw2", [P, 1024], F32))
        w_hi.append(put("w_hi2", [P, 1024], F32R))
        w_lo.append(put("w_lo2", [P, 1024], F32R))
        silu_at = at[0]
        silu_g = put("silu_g", [P, NG, GW], F32)
        prod = put("prod", [P, NG, GW], F32)
        root = put("root", [P, 2, GW], F32, h_at + 2 * GW * 4)
        rms_y = put("rms_y", [P, 2, GW], F32, silu_at + NG * GW * 4)

        at[0] = zone
        R = put("proj", [P, 5 * TPH, TOK], F32)
        f_reg, hq_reg, hi_reg, q_reg, hg_reg = (R[:, TPH * j:TPH * (j + 1), :] for j in range(5))
        chunk = lambda j, c: R[:, TPH * j:TPH * (j + 1), bass.ds(c * CH, CH)]
        k_gate = put("k_gate", [P, TPH, TOK], F32)
        kv = put("kv", [P, 2, TOK], F32)
        f_s = put("f_s", [P, TPH, N_SAMPLE], F32)
        mixc = put("mixc", [P, NM], F32)
        kt_s = put("kt_s", [P, 2, N_SAMPLE], F32)
        qu_s = put("qu_s", [P, TPH, N_SAMPLE], F32)
        qt_s = put("qt_s", [P, TPH, N_SAMPLE], F32)
        q_s = put("q_s", [P, TPH, N_SAMPLE], F32)
        k_win = put("k_win", [P, 2 * CH], F32)
        hi_c = put("hi_c", [P, TPH, CH], F32)
        hi_at = zone + 2 * TPH * TOK * 4
        state_s = put("state_s", [P, TPH, N_SAMPLE, HEAD], F32, zone)
        k_win_s = put("k_win_s", [P, N_SAMPLE, WINDOW], F32, zone + 8192)
        v_win_s = put("v_win_s", [P, N_SAMPLE, P], F32, zone + 12288)
        c_sq = put("c_sq", [P, TPH, GW], F32, hi_at)
        c_root = put("c_root", [P, TPH, GW], F32, hi_at + 8192)
        at[0] = x_at
        rope_c = put("rope_c", [P, TOK], F32)
        rope_s = put("rope_s", [P, TOK], F32)
        G = put("G", [P, TPH, CH], F32)
        dif = put("dif", [P, 2, TPH, CH], F32)
        dec = put("dec", [P, 2, TPH, CH], F32)
        q_dec = put("q_dec", [P, 2, TPH, 2, CH], F32)
        k_dec = put("k_dec", [P, 2, TPH, CH], F32)
        A = put("A", [P, N_HEADS, CH], F32)
        V = put("V", [P, N_HEADS * HEAD], F32)
        kdT_at = at[0]
        kdT = put("kdT", [P, N_HEADS * HEAD], F32)
        qg = put("qg", [P, TPH, CH], F32)
        state = put("state", [P, TPH, HEAD], F32)
        g_end = put("g_end", [P, TPH], F32)
        q_rot = put("q_rot", [P, TPH, CH], F32, kdT_at)
        rc_at = at[0]
        rot_c = put("rot_c", [P, TPH, CH], F32)
        rs_at = at[0]
        rot_s = put("rot_s", [P, TPH, CH], F32)
        kd = put("kd", [P, TPH, CH], F32, rs_at)
        v_win = put("v_win", [P, 2 * CH], F32)
        v_at = at[0]
        v_c = put("v_c", [P, CH], F32)
        rotk_c = put("rotk_c", [P, CH], F32)
        rotk_s = put("rotk_s", [P, CH], F32)
        sm_at = at[0]
        sm = put("sm", [P, 2, GQA * 2 * CH], F32)
        pt_at = at[0]
        pT = put("pT", [P, 2, GQA * 2 * CH], F32)
        m_cur = mixc[:, M_FIRST:M_FIRST + 2 * CH]
        mx = put("mx", [P, 2, GQA], F32)
        nm = put("nm", [P, 2, GQA], F32)
        es = put("es", [P, 2, GQA], F32)
        rsum = put("rsum", [P, 2, GQA], F32)
        rden = put("rden", [P, 2, GQA], F32)
        pT_s = put("pT_s", [P, 2 * N_SAMPLE * GQA], F32)
        st_s = put("st_s", [P, 8, 2 * N_SAMPLE], F32)
        hv_s = put("hv_s", [P, N_HEADS * HEAD], F32, rc_at)
        pick = put("pick", [P, N_SAMPLE, HEAD], F32, rs_at)
        v_row = put("v_row", [P, P], F32, v_at)
        sm_s = put("sm_s", [P, 2 * N_SAMPLE, WINDOW], F32, sm_at)
        kv_s = put("kv_s", [P, TPH, N_SAMPLE, HEAD], F32, pt_at)
        assert at[0] <= x_end, at[0] - x_end

        PS = ctx.enter_context(nc.psum_tensor("PS", [P, 8, 512], F32))

        raw_full = [sem(f"raw_full{s}") for s in range(3)]
        for n in ("consts_in w_gained w_hi_done w_ready unit_done unit_evac x_split_lo x_split_hi x_new y_scaled "
                  "sq_done ss_done sq_folded root_done rms_done spilled gain_done ones_done y_zero silu_done "
                  "h_ready mixc_in smp_in out_in sig_done fmax_done ln_done scan_done hic_done vt_done vc_done "
                  "d_done e_done gend_done end_done q_done k_done lvl_done a_done kdt_done kdtc_done o_done "
                  "oc_done s_done s_scaled s_upd st_zero vst_done ropq_done kvp_done t0_done ts_done qs_done "
                  "kw_shift kw_done vw_done sc_done sm_done es_ready es_done exp_done rd_done p_done pt_done "
                  "ptc_done att_done attc_done csq_done css_done croot_done crms_done co_done cg_done ch_done "
                  "cat_hi_a cat_hi_h cat_lo_a cat_lo_h x_split_lo_late pool_held dve_held a_ps p_ps v_ps d_s a_s "
                  "v_s h_hi_done h_lo_done dve_seq cleared").split():
            sem(n)
        resid_full = [sem(f"resid_full{g}") for g in range(NG)]
        S = sems

        norms = [("S", 0, g) for g in range(NG)]
        for b in range(3):
            norms += [("F", b, g) for g in range(NG)] + [("S", b + 1, g) for g in range(NG) if b < 2]
        norm_no = {n: i for i, n in enumerate(norms)}
        sq_no = {n: 1 if n[:1] + n[2:] in (("F", 2), ("S", 1)) else 0 for n in norms}
        folded = [n for n in norms if n[0] == "S" or n[2] == 0]
        fold_no = {n: k for k, n in enumerate(folded)}

        GAIN_F = {0: half_gain[:, 0, :], 1: vecs[:, V_GAIN["mix_post"]:V_GAIN["mix_post"] + 8], 2: half_gain[:, 1, :]}

        block = ctx.enter_context(nc.Block())

        @block.sync
        def _(sp):
            sp.dma_start(resid[:, 0], ins["x"][0]).then_inc(resid_full[0], 16)
            sp.dma_start(vecs[:], ins["vecs"]).then_inc(S["consts_in"], 16)
            sp.dma_start(ident[:], ins["ident"]).then_inc(S["consts_in"], 16)
            sp.dma_start(head_ones[:], ins["head_ones"]).then_inc(S["consts_in"], 16)
            def load(n, s, src):
                sp.wait_ge(S["w_ready"], n + 2)
                sp.dma_start(raw[s][:], src).then_inc(raw_full[s], 16)

            def store_stream(b, to, then=lambda g: None):
                for g in range(NG):
                    then(g)
                    sp.wait_ge(S["x_new"], NG * b + g + 1)
                    sp.dma_start(to[g], resid[:, g]).then_inc(S["spilled"], 16)

            def ffn1_step(i, first):
                for o in range(2 if first else 0, 4):
                    load(6 * i + o, o % 3, ins["w_gu1"][4 * i + o])
                for o in range(2):
                    load(6 * i + 4 + o, (4 + o) % 3, ins["w_down1"][2 * i + o])

            load(0, 0, ins["w_gu1"][0])
            load(1, 1, ins["w_gu1"][1])
            for g in range(1, NG):
                sp.dma_start(resid[:, g], ins["x"][g]).then_inc(resid_full[g], 16)
            ffn1_step(0, True)
            with sp.Fori(1, FFN_STEPS) as i:
                ffn1_step(i, False)
            load(G_IN, 0, ins["w_in"][0])
            load(G_IN + 1, 1, ins["w_in"][1])
            load(G_IN + 2, 0, ins["w_in"][2])
            store_stream(0, outs["x1"], lambda g: load(G_IN + 3, 1, ins["w_in"][3]) if g == 1 else None)
            sp.wait_ge(S["rms_done"], norm_no[("S", 1, NG - 1)] + 1)
            sp.dma_start(mixc[:], ins["mixc"]).then_inc(S["mixc_in"], 16)
            with sp.Fori(2, IN_TILES // 2) as p:
                for o in range(2):
                    load(G_IN + 2 * p + o, o, ins["w_in"][2 * p + o])
            for o in range(2):
                load(G_OUT + o, o, ins["w_out"][o])
            sp.wait_ge(S["unit_done"], UNIT_CREDIT + U_OUT)
            sp.dma_start(rope_c[:], ins["rope"][0]).then_inc(S["mixc_in"], 16)
            sp.dma_start(rope_s[:], ins["rope"][1]).then_inc(S["mixc_in"], 16)
            sp.wait_ge(S["scan_done"], 4 * N_CH)
            sp.dma_start(state_s[:], ins["state"]).then_inc(S["smp_in"], 16)
            sp.dma_start(k_win_s[:, :, 0:WINDOW - 1], ins["k_cache"]).then_inc(S["smp_in"], 16)
            sp.dma_start(v_win_s[0:WINDOW - 1], ins["v_cache"]).then_inc(S["smp_in"], 16)
            sp.wait_ge(S["kw_done"], N_CH + 1)
            sp.dma_start(outs["k_win"], k_win[:, CH:]).then_inc(S["out_in"], 16)
            sp.wait_ge(S["vw_done"], N_CH + 1)
            sp.dma_start(outs["v_win"], v_win[:, CH:]).then_inc(S["out_in"], 16)
            sp.wait_ge(S["s_upd"], N_CH + 1)
            sp.dma_start(outs["state"], state[:]).then_inc(S["out_in"], 16)
            sp.wait_ge(S["smp_in"], 48)
            sp.wait_ge(S["a_s"], 1)
            sp.dma_start(pick[0:N_SAMPLE], ins["pick"]).then_inc(S["smp_in"], 16)
            sp.wait_ge(S["v_ps"], 1)
            sp.dma_start(v_win_s[WINDOW - 1:WINDOW], v_row[0:N_SAMPLE]).then_inc(S["p_ps"], 16)
            sp.wait_ge(S["p_ps"], 16)
            sp.dma_start(outs["v_win_s"], v_win_s[:]).then_inc(S["out_in"], 16)
            sp.wait_ge(S["d_s"], 1)
            sp.dma_start(outs["k_win_s"], k_win_s[:]).then_inc(S["out_in"], 16)
            sp.wait_ge(S["d_s"], 2)
            sp.dma_start(outs["state_s"], state_s[:]).then_inc(S["out_in"], 16)
            with sp.Fori(1, KT // 2) as p:
                for o in range(2):
                    load(G_OUT + 2 * p + o, o, ins["w_out"][2 * p + o])
            load(G_FFN2, 0, ins["w_gu2"][0])
            load(G_FFN2 + 1, 1, ins["w_gu2"][1])
            sp.wait_ge(S["spilled"], 16 * NG)
            sp.wait_ge(S["out_in"], 96)
            sp.wait_ge(S["unit_done"], UNIT_CREDIT + U_OUT + 2 * NG - 1)
            for g in range(NG):
                sp.dma_start(resid[:, g], outs["x1"][g]).then_inc(resid_full[g], 16)
            load(G_FFN2 + 2, 2, ins["w_gu2"][2])
            load(G_FFN2 + 3, 0, ins["w_gu2"][3])
            for o in range(2):
                load(G_FFN2 + 4 + o, 1 + o, ins["w_down2"][o])
            with sp.Fori(1, FFN_STEPS) as i:
                for o in range(4):
                    load(G_FFN2 + 6 * i + o, o % 3, ins["w_gu2"][4 * i + o])
                for o in range(2):
                    load(G_FFN2 + 6 * i + 4 + o, 1 + o, ins["w_down2"][2 * i + o])
            store_stream(2, outs["y"])
            sp.wait_ge(S["spilled"], 32 * NG)

        @block.tensor
        def _(pe):
            pe.sem_inc(S["unit_done"], UNIT_CREDIT)

            def unit(bank, u, pairs):
                pe.wait_ge(S["unit_evac"], u + 1)
                last = len(pairs) - 1
                for k, (w, v) in enumerate(pairs):
                    (wh, wl), (vh, vl) = w, v
                    nc.tensor.matmul(PS[:, bank, :GW], wh, vh, start=(k == 0), stop=False)
                    nc.tensor.matmul(PS[:, bank, :GW], wh, vl, start=False, stop=False)
                    mm = nc.tensor.matmul(PS[:, bank, :GW], wl, vh, start=False, stop=(k == last))
                mm.then_inc(S["unit_done"], 1)

            def project(n, s, u):
                pe.wait_ge(S["w_ready"], READY_CREDIT + n + 1)
                for g in range(NG):
                    unit(g, u + g, [((w_hi[s][:, k * P:(k + 1) * P], w_lo[s][:, k * P:(k + 1) * P]),
                                     (x_hi[:, g, k, :], x_lo[:, g, k, :])) for k in range(KT)])

            def pair_by_group(n, u, ready=None, mid=None):
                assert u % 3 == 0
                for g in range(NG):
                    if ready is not None:
                        ready(g)
                    for o in range(2):
                        if g == 0:
                            pe.wait_ge(S["w_ready"], READY_CREDIT + n + o + 1)
                        unit((2 * g + o) % 3, u + 2 * g + o,
                             [((w_hi[o][:, k * P:(k + 1) * P], w_lo[o][:, k * P:(k + 1) * P]),
                               (x_hi[:, g, k, :], x_lo[:, g, k, :])) for k in range(KT)])
                        if mid is not None and o == 0:
                            mid(g)

            def norm_sum(n):
                i = norm_no[n]
                if n in fold_no:
                    pe.wait_ge(S["sq_folded"], fold_no[n] + 1)
                else:
                    pe.wait_ge(S["sq_done"], i + 1)
                tiles = KT // 2 if n in fold_no else KT
                if i >= 2:
                    pe.wait_ge(S["root_done"], i - 1)
                for m in range(tiles):
                    mm = nc.tensor.matmul(PS[:, 3 + i % 2, :GW], ones[:], sq_bufs[sq_no[n]][:, m, :],
                                          start=(m == 0), stop=(m == tiles - 1))
                mm.then_inc(S["ss_done"], 1)

            def border_units(b, n, u):
                def ready(g):
                    if b >= 0 and g == 0:
                        norm_sum(("F", b, 1))
                        norm_sum(("F", b, 2))
                    pe.wait_ge(S["x_split_lo"], NG * (b + 1) + g + 1)
                    pe.wait_ge(S["x_split_lo_late"], NG * (b + 1) + g + 1)

                pair_by_group(n, u, ready, lambda g: norm_sum(("S", b + 1, g)))

            def down(g, i, u, step_h, tiles=range(KT)):
                pe.wait_ge(S["h_lo_done"], step_h + NG + g + 1)
                for m in tiles:
                    unit((g * KT + m) % 3, u + 12 + g * KT + m,
                         [((w_hi[1 + t][:, m * P:(m + 1) * P], w_lo[1 + t][:, m * P:(m + 1) * P]),
                           (h[:, g, 2 * t, :], h[:, g, 2 * t + 1, :])) for t in range(2)])

            def ffn(n0, u0, f, b):
                def step(i, first, last):
                    u, step_h = u0 + 36 * i, 6 * FFN_STEPS * f + 6 * i
                    for o in range(2 if first else 0, 4):
                        project(n0 + 6 * i + o, o % 3, u + 3 * o)
                    pe.wait_ge(S["w_ready"], READY_CREDIT + n0 + 6 * i + 6)
                    for g in range(NG - 1 if last else NG):
                        down(g, i, u, step_h)
                    if last:
                        down(NG - 1, i, u, step_h, range(KT // 2))
                        norm_sum(("F", b, 0))
                        down(NG - 1, i, u, step_h, range(KT // 2, KT))

                step(0, True, False)
                with pe.Fori(1, FFN_STEPS - 1) as i:
                    step(i, False, False)
                step(FFN_STEPS - 1, False, True)

            pe.wait_ge(S["ones_done"], 1)
            pe.wait_ge(S["consts_in"], 48)
            border_units(-1, 0, 0)
            ffn(0, 0, 0, 0)
            border_units(0, G_IN, U_IN)

            with pe.Fori(1, IN_TILES // 2) as p:
                for o in range(2):
                    project(G_IN + 2 * p + o, o, U_IN + 6 * p + 3 * o)

            def pair(j):
                return PS[:, 2 * j:2 * j + 2, :].rearrange("p a b -> p (a b)")

            def to_tokens(bank, src, first_col=0):
                for j in range(TPH):
                    mm = nc.tensor.transpose(PS[:, bank, j * P:(j + 1) * P], src[:, j, :], ident[:])
                return mm

            pe.wait_ge(S["unit_evac"], EVAC_CREDIT + U_OUT)
            pe.wait_ge(S["mixc_in"], 48)
            pe.wait_ge(S["st_zero"], 5)
            def rotate(c):
                pe.wait_ge(S["ptc_done"], 2 + 2 * c)
                nc.tensor.matmul(PS[:, 4, :], mixc[:, M_ROT:M_ROT + P], chunk(3, c),
                                 start=True, stop=True).then_inc(S["ropq_done"], 1)
                pe.wait_ge(S["vst_done"], c + 1)
                nc.tensor.matmul(PS[:, 5, 0:CH], mixc[:, M_ROT:M_ROT + P], kv[:, 0, bass.ds(c * CH, CH)], start=True, stop=True)
                nc.tensor.transpose(PS[:, 5, CH:2 * CH], v_c[:], ident[:]).then_inc(S["kvp_done"], 1)

            def body(c, more):
                def level(l):
                    pe.wait_ge(S["q_done"], Q_CREDIT + 5 * c + l + 1)
                    pe.wait_ge(S["k_done"], K_CREDIT + 7 * c + (l + 2 if l else 1))
                    if l >= 2:
                        pe.wait_ge(S["a_done"], 5 * c + l - 1)
                    for t in range(TPH):
                        q = q_dec[:, l % 2, t]
                        if l:
                            q = q.rearrange("p o (n a b) -> p o n a b", a=2, b=LEVELS[l - 1])[:, :, :, 1]
                        w = 2 * CH if l == 0 else CH
                        mm = nc.tensor.matmul(PS[:, 2 * (l % 2) + t // 2, (t % 2) * w:(t % 2 + 1) * w],
                                              k_dec[:, l % 2, t, :], q, start=True, stop=True)
                    mm.then_inc(S["lvl_done"], 1)

                def scores(n):
                    for j in range(GQA):
                        mm = nc.tensor.matmul(pair(2)[:, j * 2 * CH:(j + 1) * 2 * CH], q_rot[HEAD * n:HEAD * (n + 1), j, :],
                                              k_win[HEAD * n:HEAD * (n + 1), :], start=True, stop=True)
                    mm.then_inc(S["sc_done"], 1)

                def probs_by_key(n):
                    pe.wait_ge(S["p_done"], 2 * c + n + 1)
                    if n == 0:
                        pe.wait_ge(S["sm_done"], 2 * c + 2)
                    else:
                        pe.wait_ge(S["ptc_done"], 2 + 2 * c + 1)
                    for b in range(2 * GQA):
                        mm = nc.tensor.transpose(pair(2)[:, b * CH:(b + 1) * CH], sm[:, n, b * CH:(b + 1) * CH], ident[:])
                    mm.then_inc(S["pt_done"], 1)

                level(0)
                pe.wait_ge(S["hic_done"], c + 1)
                pe.wait_ge(S["attc_done"], c + 1)
                to_tokens(6, hi_c).then_inc(S["vt_done"], 1)
                level(1)
                pe.wait_ge(S["qs_done"], c + 1)
                pe.wait_ge(S["kw_done"], c + 1 + KW_CREDIT)
                pe.wait_ge(S["vw_done"], c + 1 + VW_CREDIT)
                scores(0)
                level(2)
                level(3)
                pe.wait_ge(S["sm_done"], 2 * c + 1)
                scores(1)
                level(4)
                pe.wait_ge(S["k_done"], K_CREDIT + 7 * c + 7)
                pe.wait_ge(S["s_upd"], c + 1)
                to_tokens(7, kd).then_inc(S["kdt_done"], 1)
                probs_by_key(0)
                pe.wait_ge(S["k_done"], K_CREDIT + 7 * c + 2)
                pe.wait_ge(S["vc_done"], c + 1)
                pe.wait_ge(S["a_done"], 5 * c + 5)
                for hd in range(N_HEADS):
                    p0, t = HEAD * (hd % 2), hd // 2
                    nc.tensor.matmul(PS[p0:p0 + HEAD, 6, t * CH:(t + 1) * CH], V[:, hd * HEAD:(hd + 1) * HEAD],
                                     A[:, hd, :], start=True, stop=False)
                    mm = nc.tensor.matmul(PS[p0:p0 + HEAD, 6, t * CH:(t + 1) * CH], state[p0:p0 + HEAD, t, :],
                                          qg[p0:p0 + HEAD, t, :], start=False, stop=True)
                mm.then_inc(S["o_done"], 1)
                pe.wait_ge(S["kdtc_done"], c + 1)
                for hd in range(N_HEADS):
                    p0, t = HEAD * (hd % 2), hd // 2
                    mm = nc.tensor.matmul(PS[p0:p0 + HEAD, 7, t * HEAD:(t + 1) * HEAD], kdT[:, hd * HEAD:(hd + 1) * HEAD],
                                          V[:, hd * HEAD:(hd + 1) * HEAD], start=True, stop=True)
                mm.then_inc(S["s_done"], 1)
                probs_by_key(1)
                pe.wait_ge(S["oc_done"], c + 1)
                for n in range(2):
                    pe.wait_ge(S["ptc_done"], 2 + 2 * c + n + 1)
                    for half in range(2):
                        mm = nc.tensor.matmul(PS[HEAD * n:HEAD * (n + 1), 6, :], v_win[:, half * CH + HEAD * n:half * CH + HEAD * (n + 1)],
                                              pT[:, n, :].rearrange("p (j a t) -> p a j t", j=GQA, a=2)[:, half],
                                              start=(half == 0), stop=(half == 1))
                    mm.then_inc(S["att_done"], 1)
                if more:
                    rotate(c + 1)

            rotate(0)
            with pe.Fori(0, N_CH - 1) as c:
                body(c, True)
            body(N_CH - 1, False)

            ST = slice(N_PROMPT, TOK)
            pe.wait_ge(S["attc_done"], N_CH + 1)
            pe.wait_ge(S["s_upd"], N_CH + 1)
            pe.wait_ge(S["vw_done"], N_CH + VW_CREDIT)
            pe.wait_ge(S["kw_done"], N_CH + KW_CREDIT)
            nc.tensor.matmul(PS[:, 6, 0:TPH * N_SAMPLE], mixc[:, M_ROT:M_ROT + P], q_reg[:, :, ST], start=True, stop=True)
            nc.tensor.matmul(PS[:, 6, 32:32 + N_SAMPLE], mixc[:, M_ROT:M_ROT + P], kv[:, 0, ST], start=True, stop=True)
            nc.tensor.transpose(PS[0:N_SAMPLE, 7, 0:P], kv[:, 1, ST], ident[:])
            for j in range(TPH):
                tr = nc.tensor.transpose(PS[0:N_SAMPLE, 5, j * P:(j + 1) * P], hi_reg[:, j, ST], ident[:])
            tr.then_inc(S["a_s"], 1)
            pe.wait_ge(S["d_s"], 1)
            pe.wait_ge(S["v_ps"], 2)
            for n in range(2):
                for b in range(N_SAMPLE):
                    at_ = n * N_SAMPLE + b
                    mm = nc.tensor.matmul(PS[0:GQA, 4 + at_ // 4, CH * (at_ % 4):CH * (at_ % 4) + CH],
                                          q_s[HEAD * n:HEAD * (n + 1), :, b], k_win_s[HEAD * n:HEAD * (n + 1), b, :],
                                          start=True, stop=True)
            mm.then_inc(S["a_s"], 1)
            pe.wait_ge(S["smp_in"], 64)
            for b in range(N_SAMPLE):
                for o in range(2):
                    mm = nc.tensor.matmul(PS[HEAD * o:HEAD * (o + 1), b // 2, 256 * (b % 2):256 * (b % 2) + 256],
                                          pick[0:N_SAMPLE, b, :],
                                          hv_s[0:N_SAMPLE, :].rearrange("b (t o v) -> b o t v", o=2, v=HEAD)[:, o],
                                          start=True, stop=True)
            mm.then_inc(S["a_s"], 1)

            def head_sums(g):
                pe.wait_ge(S["csq_done"], g + 1)
                if g:
                    pe.wait_ge(S["croot_done"], g)
                for j in range(TPH):
                    mm = nc.tensor.matmul(PS[:, 4 + j, :GW], head_ones[:], c_sq[:, j, :], start=True, stop=True)
                mm.then_inc(S["css_done"], 1)

            pe.wait_ge(S["v_s"], 1)
            head_sums(0)
            pe.wait_ge(S["d_s"], 2)
            for b in range(N_SAMPLE):
                if b == N_SAMPLE // 2:
                    head_sums(1)
                for hd in range(N_HEADS):
                    p0, t = HEAD * (hd % 2), hd // 2
                    mm = nc.tensor.matmul(PS[p0:p0 + HEAD, 0, t * N_SAMPLE + b:t * N_SAMPLE + b + 1],
                                          state_s[p0:p0 + HEAD, t, b, :], hq_reg[p0:p0 + HEAD, t, N_PROMPT + b:N_PROMPT + b + 1],
                                          start=True, stop=True)
            mm.then_inc(S["a_s"], 1)
            pe.wait_ge(S["d_s"], 3)
            for at_ in range(2 * N_SAMPLE):
                mm = nc.tensor.transpose(PS[:, 1, at_ * GQA:(at_ + 1) * GQA], sm_s[0:GQA, at_, :], ident[0:GQA, 0:GQA])
            mm.then_inc(S["a_s"], 1)
            pe.wait_ge(S["v_ps"], 4)
            pe.wait_ge(S["p_ps"], 16)
            for n in range(2):
                for b in range(N_SAMPLE):
                    at_ = n * N_SAMPLE + b
                    mm = nc.tensor.matmul(PS[HEAD * n:HEAD * (n + 1), 2, :].rearrange("p (x j b) -> p x j b", x=16, b=N_SAMPLE)[:, 0, :, b],
                                          v_win_s[:, b, HEAD * n:HEAD * (n + 1)], pT_s[:, at_ * GQA:(at_ + 1) * GQA],
                                          start=True, stop=True)
            mm.then_inc(S["a_s"], 1)

            head_sums(NG - 1)
            pe.wait_ge(S["v_ps"], 5)

            def cat_ready(g):
                pe.wait_ge(S["cat_lo_a"], g + 1)
                pe.wait_ge(S["cat_lo_h"], g + 1)

            pair_by_group(G_OUT, U_OUT, cat_ready)
            with pe.Fori(1, KT // 2 - 1) as p:
                for o in range(2):
                    project(G_OUT + 2 * p + o, o, U_OUT + 6 * p + 3 * o)
            pair_by_group(G_OUT + KT - 2, U_OUT + 3 * (KT - 2), mid=lambda g: norm_sum(("F", 1, 0)) if g == NG - 1 else None)
            border_units(1, G_FFN2, U_FFN2)
            ffn(G_FFN2, U_FFN2, 1, 2)
            for g in range(1, NG):
                norm_sum(("F", 2, g))

        @block.gpsimd
        def _(pool):
            nc.gpsimd.memset(ones[:], 1.0).then_inc(S["ones_done"], 1)
            nc.gpsimd.memset(eps[:], EPS).then_inc(S["ones_done"], 1)

            def gain(s, use, col):
                pool.wait_ge(raw_full[s], 16 * use + 16)
                wv = raw[s][:].rearrange("p (k c) -> p k c", k=KT)
                gv = vecs[:, col:col + KT].unsqueeze(2).broadcast_to([P, KT, P])
                nc.gpsimd.tensor_tensor(wv, wv, gv, ALU.mult).then_inc(S["w_gained"], 1)

            def border_pool(b):
                def lo(g):
                    pool.wait_ge(S["x_split_hi"], NG * (b + 1) + g + 1)
                    t = slice(0, POOL_TILES)
                    nc.gpsimd.tensor_tensor(x_lo[:, g, t], resid[:, g, t], x_hi[:, g, t].bitcast(F32), ALU.subtract)\
                        .then_inc(S["x_split_lo"], 1)

                def fold(g):
                    n = ("S", b + 1, g)
                    q = sq_bufs[sq_no[n]]
                    pool.wait_ge(S["sq_done"], norm_no[n] + 1)
                    nc.gpsimd.tensor_tensor(q[:, 0:KT // 2], q[:, 0:KT // 2], q[:, KT // 2:], ALU.add).then_inc(S["sq_folded"], 1)

                for g in range(NG):
                    lo(g)
                    if b < 0 and g == 0:
                        gain(0, 0, V_GAIN["ffn1_pre"])
                        gain(1, 0, V_GAIN["ffn1_pre"])
                    fold(g)

            pool.wait_ge(S["consts_in"], 48)
            border_pool(-1)
            gain(2, 0, V_GAIN["ffn1_pre"])
            gain(0, 1, V_GAIN["ffn1_pre"])
            nc.gpsimd.memset(y[:], 0.0).then_inc(S["y_zero"], 1)
            with pool.Fori(1, FFN_STEPS) as i:
                for o in range(4):
                    gain(o % 3, 2 * i + o // 3, V_GAIN["ffn1_pre"])
            gain(0, G_IN // 3, V_GAIN["mix_pre"])
            gain(1, G_IN // 3, V_GAIN["mix_pre"])
            border_pool(0)
            gain(0, G_IN // 3 + 1, V_GAIN["mix_pre"])
            with pool.Fori(1, IN_TILES // 2 - 1) as p:
                gain(1, G_IN // 3 + p, V_GAIN["mix_pre"])
                gain(0, G_IN // 3 + 1 + p, V_GAIN["mix_pre"])
            gain(1, G_IN // 3 + IN_TILES // 2 - 1, V_GAIN["mix_pre"])
            pool.wait_ge(S["unit_done"], UNIT_CREDIT + U_OUT)
            nc.gpsimd.memset(state[:], 0.0).then_inc(S["st_zero"], 1)
            nc.gpsimd.memset(k_win[:], 0.0).then_inc(S["st_zero"], 1)
            nc.gpsimd.memset(v_win[:], 0.0).then_inc(S["st_zero"], 1)
            nc.gpsimd.memset(k_dec[:], 0.0).then_inc(S["st_zero"], 1)
            nc.gpsimd.memset(q_dec[:], 0.0).then_inc(S["st_zero"], 1)
            pool.sem_inc(S["k_done"], K_CREDIT)
            pool.sem_inc(S["end_done"], 1)
            pool.wait_ge(S["fmax_done"], 1)
            pool.wait_ge(S["mixc_in"], 48)
            pool.wait_ge(S["unit_evac"], EVAC_CREDIT + U_OUT)
            pool.wait_ge(S["st_zero"], 5)
            hq_of = lambda c: chunk(1, c)
            kg_of = lambda c: k_gate[:, :, bass.ds(c * CH, CH)]
            def held():
                pool.sem_inc(S["pool_held"], 1)

            def start(c):
                pool.wait_ge(S["ts_done"], 2 * c + 2)
                pool.wait_ge(S["kw_done"], c + KW_CREDIT)
                held()
                nc.gpsimd.tensor_tensor(rot_c[:], chunk(3, c),
                                        rope_c[:, bass.ds(c * CH, CH)].unsqueeze(1).broadcast_to([P, TPH, CH]),
                                        ALU.mult).then_inc(S["t0_done"], 1)
                nc.gpsimd.tensor_tensor(rotk_c[:], kv[:, 0, bass.ds(c * CH, CH)], rope_c[:, bass.ds(c * CH, CH)],
                                        ALU.mult).then_inc(S["t0_done"], 1)
                pool.wait_ge(S["lvl_done"], 5 * c + 5)
                pool.wait_ge(S["e_done"], 8 + 8 * c + 2)
                held()
                nc.gpsimd.tensor_tensor(k_dec[:, 0], kg_of(c), dec[:, 1], ALU.mult).then_inc(S["k_done"], 1)

            def body(c, more):
                def over_sum(n):
                    pool.wait_ge(S["rd_done"], 2 * c + n + 1)
                    pv = sm[:, n, :].rearrange("p (j t) -> p j t", j=GQA)
                    nc.gpsimd.tensor_tensor(pv, pv, rden[:, n, :].unsqueeze(2).broadcast_to([P, GQA, 2 * CH]),
                                            ALU.mult).then_inc(S["p_done"], 1)

                def level(l):
                    pool.wait_ge(S["lvl_done"], (5 + 5 * c + l - 1) if l >= 2 else (5 * c + 5 - l))
                    b = LEVELS[l - 1]
                    halves = lambda ap: ap.rearrange("p t (n a b) -> p t n a b", a=2, b=b)
                    pool.wait_ge(S["e_done"], 8 + 8 * c + 2 + l + 1)
                    held()
                    nc.gpsimd.tensor_tensor(halves(k_dec[:, l % 2])[:, :, :, 0], halves(kg_of(c))[:, :, :, 0],
                                            halves(dec[:, l % 2])[:, :, :, 0], ALU.mult).then_inc(S["k_done"], 1)

                pool.wait_ge(S["att_done"], 2 * c + 2)
                held()
                nc.gpsimd.tensor_copy(k_win[:, 0:CH], k_win[:, CH:]).then_inc(S["kw_shift"], 1)
                nc.gpsimd.tensor_copy(v_win[:, 0:CH], v_win[:, CH:]).then_inc(S["kw_shift"], 1)
                pool.wait_ge(S["e_done"], 8 + 8 * c + 3)
                pool.wait_ge(S["o_done"], c + 1)
                held()
                nc.gpsimd.tensor_tensor(qg[:], hq_of(c), dec[:, 0], ALU.mult).then_inc(S["k_done"], 1)
                for l in range(1, 4):
                    level(l)
                pool.wait_ge(S["e_done"], 8 + 8 * c + 6)
                nc.gpsimd.tensor_tensor(dif[:, 1], G[:, :, CH - 1:CH].broadcast_to([P, TPH, CH]), G[:],
                                        ALU.subtract).then_inc(S["end_done"], 1)
                level(4)
                pool.wait_ge(S["e_done"], 8 + 8 * c + 8)
                pool.wait_ge(S["kdt_done"], c + 1)
                held()
                nc.gpsimd.tensor_tensor(kd[:], kg_of(c), dec[:, 1], ALU.mult).then_inc(S["k_done"], 1)
                over_sum(0)
                over_sum(1)
                if more:
                    start(c + 1)

            start(0)
            with pool.Fori(0, N_CH - 1) as c:
                body(c, True)
            body(N_CH - 1, False)
            for g in range(NG):
                pool.wait_ge(S["cat_hi_a"], g + 1)
                nc.gpsimd.tensor_tensor(x_lo[:, g, 0:TPH], q_reg[:, :, g * GW:(g + 1) * GW],
                                        x_hi[:, g, 0:TPH].bitcast(F32), ALU.subtract).then_inc(S["cat_lo_a"], 1)
            gain(0, 37, V_GAIN["ffn2_pre"])
            gain(1, 37, V_GAIN["ffn2_pre"])
            border_pool(1)
            gain(2, 22, V_GAIN["ffn2_pre"])
            gain(0, 38, V_GAIN["ffn2_pre"])
            nc.gpsimd.memset(y[:], 0.0).then_inc(S["y_zero"], 1)
            with pool.Fori(1, FFN_STEPS) as i:
                for o in range(4):
                    gain(o % 3, (22 if o == 2 else 37) + 2 * i + o // 3, V_GAIN["ffn2_pre"])

        @block.scalar
        def _(act):
            def split_hi(s, n_gained, use, prior_unit):
                if n_gained is None:
                    act.wait_ge(raw_full[s], 16 * use + 16)
                else:
                    act.wait_ge(S["w_gained"], n_gained)
                act.wait_ge(S["unit_done"], UNIT_CREDIT + prior_unit)
                nc.scalar.activation(w_hi[s][:], raw[s][:], ACT.Copy).then_inc(S["w_hi_done"], 1)

            def square(n, src):
                prior = [m for m in norms[:norm_no[n]] if sq_no[m] == sq_no[n]]
                if prior:
                    act.wait_ge(S["ss_done"], norm_no[prior[-1]] + 1)
                nc.scalar.activation(sq_bufs[sq_no[n]][:], src, ACT.Square, scale=D_MODEL ** -0.5).then_inc(S["sq_done"], 1)

            def inverse(n):
                i = norm_no[n]
                kind, b, g = n
                act.wait_ge(S["ss_done"], i + 1)
                if i >= 2:
                    act.wait_ge(S["rms_done"], i - 1)
                nc.scalar.activation(root[:, i % 2, :], PS[:, 3 + i % 2, :GW], ACT.Ln, bias=eps[:]).then_inc(S["root_done"], 1)
                act.wait_ge(S["root_done"], i + 1)
                if kind == "F" and g == 2:
                    act.wait_ge(S["x_new"], NG * b + 1)
                dst = rms[:, g, :] if kind == "S" else rms_y[:, g % 2, :]
                nc.scalar.activation(dst, root[:, i % 2, :], ACT.Exp, scale=-0.5).then_inc(S["rms_done"], 1)

            def border_act(b, y_evac, first_pair):
                def square_y(g):
                    act.wait_ge(S["unit_evac"], EVAC_CREDIT + y_evac[g])
                    square(("F", b, g), y[:, g])

                def hi(g):
                    if b < 0:
                        act.wait_ge(resid_full[g], 16)
                    else:
                        act.wait_ge(S["x_new"], NG * b + g + 1)
                    nc.scalar.activation(x_hi[:, g], resid[:, g], ACT.Copy).then_inc(S["x_split_hi"], 1)

                def square_x(g):
                    square(("S", b + 1, g), resid[:, g])

                if b >= 0:
                    square_y(0)
                    inverse(("F", b, 0))
                    square_y(1)
                    square_y(2)
                    first_pair()
                    if b < 2:
                        hi(0)
                    inverse(("F", b, 1))
                    if b == 2:
                        inverse(("F", b, 2))
                        return
                else:
                    hi(0)
                square_x(0)
                if b >= 0:
                    inverse(("F", b, 2))
                else:
                    first_pair()
                hi(1)
                square_x(1)
                inverse(("S", b + 1, 0))
                hi(2)
                square_x(2)
                inverse(("S", b + 1, 1))
                inverse(("S", b + 1, 2))

            def ffn(u0, f, slot_uses, gained0, b, next_pair):
                def silus(i, t, first):
                    for g in range(NG):
                        act.wait_ge(S["unit_evac"], EVAC_CREDIT + u0 + 36 * i + 6 * t + (2 * g if first and t == 0 else g) + 1)
                        nc.scalar.activation(silu_g[:, g], silu_g[:, g], ACT.Silu).then_inc(S["silu_done"], 1)

                def h_his(i, t):
                    for g in range(NG):
                        act.wait_ge(S["h_ready"], 6 * FFN_STEPS * f + 6 * i + 3 * t + g + 1)
                        if t == 0 and g == 0:
                            act.wait_ge(S["unit_done"], UNIT_CREDIT + u0 + 36 * i)
                        nc.scalar.activation(h[:, g, 2 * t, :], prod[:, g], ACT.Copy).then_inc(S["h_hi_done"], 1)

                def step(i, first, last):
                    u = u0 + 36 * i
                    g0 = gained0 + 4 * i
                    use = lambda s, k: slot_uses[s] + 2 * i + k
                    if not first:
                        split_hi(1, g0 + 2, use(1, 0), u)
                    if first:
                        split_hi(2, g0 + 3, use(2, 0), u)
                        silus(i, 0, first)
                    else:
                        silus(i, 0, first)
                        split_hi(2, g0 + 3, use(2, 0), u)
                    if first:
                        split_hi(0, g0 + 4, use(0, 1), u + 6)
                        h_his(i, 0)
                    else:
                        h_his(i, 0)
                        split_hi(0, g0 + 4, use(0, 1), u + 3)
                    silus(i, 1, first)
                    split_hi(1, None, use(1, 1), u + 6)
                    split_hi(2, None, use(2, 1), u + 9)
                    h_his(i, 1)
                    if not last:
                        split_hi(0, g0 + 5, use(0, 2), u + 12)

                step(0, True, False)
                with act.Fori(1, FFN_STEPS - 1) as i:
                    step(i, False, False)
                step(FFN_STEPS - 1, False, True)
                border_act(b, [u0 + 36 * (FFN_STEPS - 1) + 12 + KT * (g + 1) for g in range(NG)], next_pair)

            act.wait_ge(S["ones_done"], 2)
            act.wait_ge(S["dve_seq"], 3)
            nc.scalar.activation(lb[:, 0:2], lb[:, 0:2], ACT.Exp).then_inc(S["cleared"], 1)
            def in_hi(n, s, use):
                split_hi(s, 44 + n + 1, use, U_IN + 3 * (n - 1))

            def in_his(p):
                in_hi(2 * p + 1, 1, 22 + p)
                in_hi(2 * p + 2, 0, 23 + p)

            def ffn1_pair():
                for s in range(2):
                    split_hi(s, s + 1, 0, -24)

            def in_pair():
                split_hi(0, 45, 22, U_IN - 24)
                split_hi(1, 46, 22, U_IN)

            border_act(-1, None, ffn1_pair)
            ffn(0, 0, [0, 0, 0], 0, 0, in_pair)
            split_hi(0, 47, 23, U_IN + 5)
            in_hi(3, 1, 23)
            in_hi(4, 0, 24)
            act.wait_ge(S["unit_evac"], EVAC_CREDIT + U_IN + 3 * TPH)
            nc.scalar.activation(f_reg, f_reg, ACT.Sigmoid).then_inc(S["sig_done"], 1)
            in_hi(5, 1, 24)
            in_hi(6, 0, 25)
            act.wait_ge(S["fmax_done"], 1)
            nc.scalar.activation(f_reg, f_reg, ACT.Ln).then_inc(S["ln_done"], 1)
            with act.Fori(3, IN_TILES // 2 - 1) as p:
                in_his(p)
            in_hi(IN_TILES - 1, 1, 22 + IN_TILES // 2 - 1)
            act.wait_ge(S["unit_evac"], EVAC_CREDIT + U_IN + 3 * 5 * TPH)
            nc.scalar.activation(hg_reg, hg_reg, ACT.Silu).then_inc(S["cg_done"], 1)
            split_hi(0, None, 22 + IN_TILES // 2, U_IN + 3 * (IN_TILES - 1))
            split_hi(1, None, 22 + IN_TILES // 2, U_OUT)

            act.sem_inc(S["e_done"], 8)
            act.sem_inc(S["ptc_done"], 2)
            act.sem_inc(S["attc_done"], 1)
            act.sem_inc(S["vw_done"], VW_CREDIT)
            act.wait_ge(S["unit_evac"], EVAC_CREDIT + U_OUT)
            act.wait_ge(S["st_zero"], 5)
            USES = [(1, 0), (0, 1), (0, 2), (2, 3), (3, 4), (4, 5), (5, 6), (0, 7)]
            def decay(c, e, src, scale):
                q, k = USES[e - 2]
                if q:
                    act.wait_ge(S["q_done"], 5 * c + q + (Q_CREDIT if e >= 2 else 0))
                if k:
                    act.wait_ge(S["k_done"], 7 * c + k + (K_CREDIT if e >= 2 else 0))
                nc.scalar.activation(dec[:, e % 2], src, ACT.Exp, scale=scale).then_inc(S["e_done"], 1)

            def start(c):
                act.wait_ge(S["kvp_done"], c + 1)
                nc.scalar.activation(v_c[:], kv[:, 1, bass.ds(c * CH, CH)], ACT.Copy).then_inc(S["vst_done"], 1)
                act.wait_ge(S["vt_done"], c + VT_CREDIT)
                nc.scalar.activation(hi_c[:], chunk(2, c), ACT.Copy).then_inc(S["hic_done"], 1)
                act.wait_ge(S["d_done"], 9 * c + 1)
                decay(c, 0, dif[:, 0], 1.0)
                decay(c, 1, dif[:, 0], -1.0)

            def body(c, more):
                def level(l):
                    act.wait_ge(S["d_done"], 9 * c + 1 + 2 * l)
                    decay(c, 2 + l, dif[:, l % 2], 1.0)

                def exponentials(n):
                    act.wait_ge(S["es_ready"], 2 * c + n + 1)
                    nc.scalar.activation(es[:, n, :], es[:, n, :], ACT.Exp).then_inc(S["es_done"], 1)
                    for j in range(GQA):
                        cols = sm[:, n, j * 2 * CH:(j + 1) * 2 * CH]
                        last = nc.scalar.activation(cols, cols, ACT.Exp, bias=nm[:, n, j:j + 1], accum_out=rsum[:, n, j:j + 1])
                    last.then_inc(S["exp_done"], 1)

                def probs(n):
                    act.wait_ge(S["pt_done"], 2 * c + n + 1)
                    act.wait_ge(S["att_done"], 2 * c + n + 1)
                    nc.scalar.activation(pT[:, n, :], PS[:, 4:6, :].rearrange("p a b -> p (a b)"),
                                         ACT.Copy).then_inc(S["ptc_done"], 1)

                act.wait_ge(S["kvp_done"], c + 2)
                act.wait_ge(S["kw_shift"], 2 * c + 2)
                nc.scalar.activation(v_win[:, CH:], PS[:, 5, CH:2 * CH], ACT.Copy).then_inc(S["vw_done"], 1)
                act.wait_ge(S["scan_done"], 4 * c + 4)
                decay(c, 2, G[:], 1.0)
                act.wait_ge(S["s_upd"], c + 1)
                nc.scalar.activation(g_end[:], G[:, :, CH - 1], ACT.Exp).then_inc(S["gend_done"], 1)
                level(1)
                level(2)
                act.wait_ge(S["vt_done"], c + VT_CREDIT + 1)
                act.wait_ge(S["s_done"], c + SD_CREDIT)
                nc.scalar.activation(V[:], PS[:, 6, :], ACT.Copy).then_inc(S["vc_done"], 1)
                level(3)
                level(4)
                exponentials(0)
                act.wait_ge(S["end_done"], c + 2)
                decay(c, 7, dif[:, 1], 1.0)
                exponentials(1)
                act.wait_ge(S["kdt_done"], c + 2)
                nc.scalar.activation(kdT[:], PS[:, 7, :], ACT.Copy).then_inc(S["kdtc_done"], 1)
                probs(0)
                if more:
                    start(c + 1)
                act.wait_ge(S["o_done"], c + 2)
                nc.scalar.activation(chunk(1, c), PS[:, 6, :].rearrange("p (t c) -> p t c", t=TPH),
                                     ACT.Copy).then_inc(S["oc_done"], 1)
                probs(1)
                act.wait_ge(S["att_done"], 2 * c + 4)
                nc.scalar.activation(chunk(3, c), PS[:, 6, :].rearrange("p (t c) -> p t c", t=TPH),
                                     ACT.Copy).then_inc(S["attc_done"], 1)

            start(0)
            with act.Fori(0, N_CH - 1) as c:
                body(c, True)
            body(N_CH - 1, False)

            ST = slice(N_PROMPT, TOK)
            act.wait_ge(S["a_s"], 1)
            nc.scalar.activation(v_row[0:N_SAMPLE], PS[0:N_SAMPLE, 7, 0:P], ACT.Copy).then_inc(S["v_ps"], 1)
            nc.scalar.activation(hv_s[0:N_SAMPLE], PS[0:N_SAMPLE, 5, :], ACT.Copy).then_inc(S["v_ps"], 1)

            gs = lambda r, g: r[:, :, g * GW:(g + 1) * GW]

            def head_squares(g):
                if g:
                    act.wait_ge(S["css_done"], g)
                nc.scalar.activation(c_sq[:], gs(hq_reg, g), ACT.Square, scale=HEAD ** -0.5).then_inc(S["csq_done"], 1)

            def head_inverse(g):
                act.wait_ge(S["css_done"], g + 1)
                if g:
                    act.wait_ge(S["co_done"], g)
                nc.scalar.activation(c_root[:], PS[:, 4:8, :GW], ACT.Ln, bias=eps[:]).then_inc(S["croot_done"], 1)
                act.wait_ge(S["croot_done"], g + 1)
                nc.scalar.activation(c_root[:], c_root[:], ACT.Exp, scale=-0.5).then_inc(S["crms_done"], 1)

            def hi_attention(g):
                nc.scalar.activation(x_hi[:, g, 0:TPH], gs(q_reg, g), ACT.Copy).then_inc(S["cat_hi_a"], 1)

            def hi_hgrn(g):
                act.wait_ge(S["ch_done"], g + 1)
                nc.scalar.activation(x_hi[:, g, TPH:], gs(hq_reg, g), ACT.Copy).then_inc(S["cat_hi_h"], 1)

            act.wait_ge(S["v_ps"], 2)
            head_squares(0)
            act.wait_ge(S["v_s"], 1)
            nc.scalar.activation(st_s[0:GQA, 3, :], st_s[0:GQA, 3, :], ACT.Exp).then_inc(S["sig_done"], 1)
            nc.scalar.activation(sm_s[0:GQA], sm_s[0:GQA], ACT.Exp).then_inc(S["sig_done"], 1)
            head_squares(1)
            head_inverse(0)
            act.wait_ge(S["out_in"], 96)
            hi_attention(0)
            hi_hgrn(0)
            head_inverse(1)
            act.wait_ge(S["a_s"], 4)
            nc.scalar.activation(hq_reg[:, :, ST], PS[:, 0, 0:TPH * N_SAMPLE].rearrange("p (t b) -> p t b", t=TPH),
                                 ACT.Copy).then_inc(S["v_ps"], 1)
            act.wait_ge(S["v_ps"], 3)
            head_squares(2)
            act.wait_ge(S["a_s"], 5)
            nc.scalar.activation(pT_s[:], PS[:, 1, 0:2 * N_SAMPLE * GQA], ACT.Copy).then_inc(S["v_ps"], 1)
            hi_hgrn(1)
            act.wait_ge(S["a_s"], 6)
            nc.scalar.activation(q_reg[:, :, ST], PS[:, 2, 0:TPH * N_SAMPLE].rearrange("p (t b) -> p t b", t=TPH),
                                 ACT.Copy).then_inc(S["v_ps"], 1)
            hi_attention(1)
            head_inverse(2)
            act.wait_ge(S["v_ps"], 5)
            hi_attention(2)
            hi_hgrn(2)

            split_hi(0, None, 34, U_OUT + 5)
            split_hi(1, None, 34, U_OUT + 6)
            with act.Fori(2, KT // 2) as p:
                split_hi(0, None, 33 + p, U_OUT + 6 * p - 3)
                split_hi(1, None, 33 + p, U_OUT + 6 * p)

            def ffn2_pair():
                for s in range(2):
                    split_hi(s, 67 + s, 37, U_FFN2)

            border_act(1, [U_OUT + 3 * (KT - 2) + 2 * (g + 1) for g in range(NG)], ffn2_pair)
            ffn(U_FFN2, 1, [37, 37, 22], 66, 2, lambda: None)

        @block.vector
        def _(dve):
            seq = Seq(dve, S["dve_seq"])
            dve.sem_inc(S["unit_evac"], EVAC_CREDIT)
            dve.sem_inc(S["w_ready"], READY_CREDIT)
            dve.wait_ge(S["consts_in"], 48)
            for j, name in enumerate(("ffn1_post", "ffn2_post")):
                nc.vector.tensor_scalar(half_gain[:, j, :], vecs[:, V_GAIN[name]:V_GAIN[name] + 8], 0.5, None, ALU.mult)\
                    .then_inc(S["gain_done"], 1)
            dve.wait_ge(S["gain_done"], 2)

            def split_lo(n, s):
                dve.wait_ge(S["w_hi_done"], n + 1)
                nc.vector.tensor_tensor(w_lo[s][:], raw[s][:], w_hi[s][:].bitcast(F32), ALU.subtract)\
                    .then_inc(S["w_ready"], 1)

            def fold(n):
                q = sq_bufs[sq_no[n]]
                dve.wait_ge(S["sq_done"], norm_no[n] + 1)
                nc.vector.tensor_tensor(q[:, 0:KT // 2], q[:, 0:KT // 2], q[:, KT // 2:], ALU.add).then_inc(S["sq_folded"], 1)

            def finish(b, g, between=lambda: None):
                dve.wait_ge(S["rms_done"], norm_no[("F", b, g)] + 1)
                rb = rms_y[:, g % 2, :].unsqueeze(1).broadcast_to([P, KT, GW])
                nc.vector.tensor_tensor(y[:, g], y[:, g], rb, ALU.mult).then_inc(S["y_scaled"], 1)
                between()
                dve.wait_ge(S["y_scaled"], NG * b + g + 1)
                dve.wait_ge(resid_full[g], 16 if b == 0 else 32)
                for m in range(KT):
                    st = nc.vector.scalar_tensor_tensor(resid[:, g, m, :], y[:, g, m, :], GAIN_F[b][:, m:m + 1],
                                                        resid[:, g, m, :], ALU.mult, ALU.add)
                st.then_inc(S["x_new"], 1)

            def border_dve(b, next_pair):
                def lo(g):
                    t = slice(POOL_TILES, KT)
                    dve.wait_ge(S["x_split_hi"], NG * (b + 1) + g + 1)
                    nc.vector.tensor_tensor(x_lo[:, g, t], resid[:, g, t], x_hi[:, g, t].bitcast(F32), ALU.subtract)\
                        .then_inc(S["x_split_lo_late"], 1)

                if b < 0:
                    lo(0)
                    next_pair()
                    lo(1)
                    lo(2)
                    return
                finish(b, 0)
                next_pair()
                if b < 2:
                    lo(0)
                finish(b, 1)
                finish(b, 2, (lambda: lo(1)) if b < 2 else lambda: None)
                if b < 2:
                    lo(2)

            def ffn(n0, u0, f, b, next_pair):
                def evac(u):
                    dve.wait_ge(S["unit_done"], UNIT_CREDIT + u + 1)

                def step(i, first, last):
                    u, n = u0 + 36 * i, n0 + 6 * i
                    for t in range(2):
                        by_group = first and t == 0

                        def gate(g):
                            v = 2 * g if by_group else g
                            evac(u + 6 * t + v)
                            nc.vector.tensor_tensor(silu_g[:, g], PS[:, v % 3, :GW], rms[:, g], ALU.mult).then_inc(S["unit_evac"], 1)

                        def up(g):
                            v = 2 * g + 1 if by_group else 3 + g
                            evac(u + 6 * t + v)
                            nc.vector.tensor_tensor(prod[:, g], PS[:, v % 3, :GW], rms[:, g], ALU.mult).then_inc(S["unit_evac"], 1)

                        def gated(g):
                            v = 2 * g + 1 if by_group else 3 + g
                            dve.wait_ge(S["unit_evac"], EVAC_CREDIT + u + 6 * t + v + 1)
                            dve.wait_ge(S["silu_done"], 6 * FFN_STEPS * f + 6 * i + 3 * t + g + 1)
                            nc.vector.tensor_tensor(prod[:, g], prod[:, g], silu_g[:, g], ALU.mult).then_inc(S["h_ready"], 1)

                        def h_lo(g):
                            dve.wait_ge(S["h_hi_done"], 6 * FFN_STEPS * f + 6 * i + 3 * t + g + 1)
                            nc.vector.tensor_tensor(h[:, g, 2 * t + 1, :], prod[:, g], h[:, g, 2 * t, :].bitcast(F32),
                                                    ALU.subtract).then_inc(S["h_lo_done"], 1)

                        if by_group:
                            for g in range(NG):
                                if g == NG - 1:
                                    split_lo(n + 2, 2)
                                dve.wait_ge(S["rms_done"], norm_no[("S", 2 * f, g)] + 1)
                                gate(g)
                                up(g)
                            for g in range(NG):
                                gated(g)
                            for g in range(NG):
                                h_lo(g)
                        else:
                            split_lo(n + 2 * t + 1, (2 * t + 1) % 3)
                            for g in range(NG):
                                gate(g)
                            split_lo(n + 2 * t + 2, (2 * t + 2) % 3)
                            if t == 1:
                                split_lo(n + 5, 2)
                            for g in range(NG):
                                up(g)
                                gated(g)
                                if g:
                                    h_lo(g - 1)
                            h_lo(NG - 1)
                    if first:
                        dve.wait_ge(S["y_zero"], f + 1)
                    for d in range(NG * KT):
                        g, m = d // KT, d % KT
                        if last and (g, m) == (NG - 1, 0):
                            fold(("F", b, 0))
                        if not last and d == KT:
                            split_lo(n + 6, 0)
                        evac(u + 12 + d)
                        nc.vector.tensor_tensor(y[:, g, m, :], y[:, g, m, :], PS[:, d % 3, :GW], ALU.add).then_inc(S["unit_evac"], 1)

                step(0, True, False)
                with dve.Fori(1, FFN_STEPS - 1) as i:
                    step(i, False, False)
                step(FFN_STEPS - 1, False, True)
                border_dve(b, next_pair)

            def splits(n):
                return lambda: (split_lo(n, 0), split_lo(n + 1, 1))

            seq(nc.vector.tensor_tensor(lb[:, 0], vecs[:, V_LB0:V_LB0 + TPH], vecs[:, V_LB1:V_LB1 + TPH], ALU.max))
            seq(nc.vector.tensor_tensor(lb[:, 1], vecs[:, V_LB1:V_LB1 + TPH], lb[:, 0], ALU.subtract))
            seq(nc.vector.tensor_tensor(lb[:, 0], vecs[:, V_LB0:V_LB0 + TPH], lb[:, 0], ALU.subtract))
            dve.wait_ge(S["cleared"], 1)
            seq(nc.vector.tensor_tensor(lb[:, 2], lb[:, 0], lb[:, 1], ALU.add))
            seq(nc.vector.reciprocal(lb[:, 2], lb[:, 2]))
            seq(nc.vector.tensor_tensor(lb[:, 0], lb[:, 0], lb[:, 2], ALU.mult))
            seq(nc.vector.tensor_scalar(lb[:, 1], lb[:, 0], -1.0, 1.0, ALU.mult, ALU.add))

            border_dve(-1, splits(0))
            ffn(0, 0, 0, 0, splits(G_IN))

            def in_tile(n, o, dst, scale, split=True, between=lambda g: None):
                if split:
                    split_lo(G_IN + n + 1, 1 - o)
                for g in range(NG):
                    between(g)
                    dve.wait_ge(S["unit_done"], UNIT_CREDIT + U_IN + 3 * n + g + 1)
                    if scale is None:
                        ev = nc.vector.tensor_tensor(dst(g), PS[:, g, :GW], rms[:, g], ALU.mult)
                    else:
                        ev = nc.vector.scalar_tensor_tensor(dst(g), PS[:, g, :GW], scale, rms[:, g], ALU.mult, ALU.mult)
                    ev.then_inc(S["unit_evac"], 1)

            def in_pair(p, scale=None):
                for o in range(2):
                    in_tile(2 * p + o, o, lambda g: R[:, 2 * p + o, g * GW:(g + 1) * GW], scale)

            for g in range(NG):
                dve.wait_ge(S["rms_done"], norm_no[("S", 1, g)] + 1)
                for o in range(2):
                    if (g, o) == (NG - 1, 1):
                        split_lo(G_IN + 2, 0)
                    dve.wait_ge(S["unit_done"], UNIT_CREDIT + U_IN + 2 * g + o + 1)
                    nc.vector.tensor_tensor(R[:, o, g * GW:(g + 1) * GW], PS[:, (2 * g + o) % 3, :GW], rms[:, g],
                                            ALU.mult).then_inc(S["unit_evac"], 1)
            in_pair(1)
            split_lo(G_IN + 5, 1)
            dve.wait_ge(S["sig_done"], 1)
            dve.wait_ge(S["spilled"], 16 * NG)
            for j in range(TPH):
                last = nc.vector.tensor_scalar(f_reg[:, j], f_reg[:, j], lb[:, 1, j:j + 1], lb[:, 0, j:j + 1], ALU.mult, ALU.add)
            seq(last)
            nc.vector.tensor_copy(f_s[:], f_reg[:, :, N_PROMPT:])

            def gate_step(g):
                if g == 1:
                    seq(nc.vector.tensor_scalar(k_gate[:], f_reg, -1.0, 1.0, ALU.mult, ALU.add))
                elif g == 2:
                    nc.vector.tensor_scalar(f_reg, f_reg, F_MIN, None, ALU.max).then_inc(S["fmax_done"], 1)

            in_tile(4, 0, lambda g: R[:, 4, g * GW:(g + 1) * GW], HEAD ** -0.5, split=False, between=gate_step)
            in_tile(5, 1, lambda g: R[:, 5, g * GW:(g + 1) * GW], HEAD ** -0.5)
            in_pair(3, HEAD ** -0.5)
            with dve.Fori(4, IN_TILES // 2 - 1) as p:
                in_pair(p)
            for o in range(2):
                in_tile(IN_TILES - 2 + o, o, lambda g: kv[:, o, g * GW:(g + 1) * GW], None)
            split_lo(G_OUT + 1, 1)

            dve.sem_inc(S["lvl_done"], 5)
            dve.sem_inc(S["q_done"], Q_CREDIT)
            dve.sem_inc(S["gend_done"], GE_CREDIT)
            dve.sem_inc(S["o_done"], 1)
            dve.sem_inc(S["kdt_done"], 1)
            dve.sem_inc(S["s_upd"], 1)
            dve.sem_inc(S["vt_done"], VT_CREDIT)
            dve.sem_inc(S["s_done"], SD_CREDIT)
            dve.sem_inc(S["kvp_done"], 1)
            dve.sem_inc(S["att_done"], 2)
            dve.sem_inc(S["ts_done"], 2)
            dve.sem_inc(S["kw_done"], KW_CREDIT)
            dve.wait_ge(S["mixc_in"], 48)
            dve.wait_ge(S["ln_done"], 1)
            dve.wait_ge(S["st_zero"], 5)
            DREADS = [2, 4, 5, 6, 7, 8]

            def blocks(ap, b):
                return ap.rearrange("p t (n b) -> p (t n) b", b=b)

            def free(c, d):
                dve.wait_ge(S["e_done"], 8 + 8 * c + DREADS[d - 2] if d >= 2 else 8 * c + DREADS[4 + d])

            def level(c, l):
                b = LEVELS[l - 1]
                gv, dv = blocks(G[:], 2 * b), blocks(dif[:, l % 2], 2 * b)
                ref = gv[:, :, b - 1:b].broadcast_to([P, TPH * CH // (2 * b), b])
                free(c, l)
                nc.vector.tensor_tensor(dv[:, :, 0:b], ref, gv[:, :, 0:b], ALU.subtract).then_inc(S["d_done"], 1)
                nc.vector.tensor_tensor(dv[:, :, b:], gv[:, :, b:], ref, ALU.subtract).then_inc(S["d_done"], 1)

            def q_decayed(c, l):
                halves = lambda ap: ap.rearrange("p t (n a b) -> p t n a b", a=2, b=LEVELS[l - 1])[:, :, :, 1] if l else ap
                dve.wait_ge(S["lvl_done"], (5 + 5 * c + l - 1) if l >= 2 else (5 * c + 5 - l))
                dve.wait_ge(S["e_done"], 8 + 8 * c + (3 + l if l else 1))
                for o in range(2):
                    r = slice(HEAD * o, HEAD * (o + 1))
                    dq = nc.vector.tensor_tensor(halves(q_dec[r, l % 2, :, o]), halves(chunk(1, c)[r]), halves(dec[r, l % 2]),
                                                 ALU.mult)
                dq.then_inc(S["q_done"], 1)

            def start(c):
                dve.wait_ge(S["gend_done"], c + GE_CREDIT)
                dve.wait_ge(S["end_done"], c + 1)
                for j in range(TPH):
                    nc.vector.tensor_tensor_scan(G[:, j], ones[:], R[:, j, bass.ds(c * CH, CH)], 0.0, ALU.mult, ALU.add)\
                        .then_inc(S["scan_done"], 1)
                dve.wait_ge(S["scan_done"], 4 * c + 4)
                free(c, 0)
                gv = blocks(G[:], SUB)
                nc.vector.tensor_tensor(blocks(dif[:, 0], SUB), gv,
                                        gv[:, :, SUB // 2 - 1:SUB // 2].broadcast_to([P, TPH * CH // SUB, SUB]),
                                        ALU.subtract).then_inc(S["d_done"], 1)
                level(c, 1)

            def body(c, more):
                tok = bass.ds(c * CH, CH)

                def weights(l):
                    dve.wait_ge(S["lvl_done"], 5 + 5 * c + l + 1)
                    if l == 0:
                        dve.wait_ge(S["o_done"], c + 1)
                        mask = mixc[:, M_SUB:M_SUB + CH].unsqueeze(1).broadcast_to([P, N_HEADS, CH])
                        nc.vector.tensor_tensor(A[:], PS[:, 0:2, :].rearrange("p a (h t) -> p (a h) t", t=CH), mask,
                                                ALU.mult).then_inc(S["a_done"], 1)
                        return
                    b, at_ = LEVELS[l - 1], M_LVL + (l - 1) * CH
                    late = lambda ap: ap.rearrange("p h (n a b) -> p h n a b", a=2, b=b)[:, :, :, 1]
                    mask = late(mixc[:, at_:at_ + CH].bitcast(U32).unsqueeze(1)).broadcast_to([P, TPH, CH // (2 * b), b])
                    dve.wait_ge(S["a_done"], 5 * c + l)
                    dve.sem_inc(S["dve_held"], 1)
                    for k in range(2):
                        src = PS[:, 2 * (l % 2) + k, 0:TPH * CH // 2].rearrange("p (h n b) -> p h n b", h=TPH, b=b)
                        cp = nc.vector.copy_predicated(late(A[:, TPH * k:TPH * (k + 1), :]), mask, src)
                    cp.then_inc(S["a_done"], 1)

                def sub_max(n):
                    dve.wait_ge(S["sc_done"], 2 * c + n + 1)
                    sv = sm[:, n, :].rearrange("p (j t) -> p j t", j=GQA)
                    nc.vector.scalar_tensor_tensor(sv, PS[:, 4:6, :].rearrange("p a (j t) -> p (a j) t", t=2 * CH),
                                                   HEAD ** -0.5, m_cur.unsqueeze(1).broadcast_to([P, GQA, 2 * CH]),
                                                   ALU.mult, ALU.add).then_inc(S["sm_done"], 1)
                    dve.wait_ge(S["sm_done"], 2 * c + n + 1)
                    sinks = vecs[:, V_SINK + GQA * n:V_SINK + GQA * (n + 1)]
                    seq(nc.vector.tensor_reduce(mx[:, n, :], sv, AX_X, ALU.max))
                    seq(nc.vector.tensor_tensor(mx[:, n, :], mx[:, n, :], sinks, ALU.max))
                    seq(nc.vector.tensor_scalar(nm[:, n, :], mx[:, n, :], -1.0, None, ALU.mult))
                    nc.vector.tensor_tensor(es[:, n, :], sinks, mx[:, n, :], ALU.subtract).then_inc(S["es_ready"], 1)

                def over(n):
                    dve.wait_ge(S["exp_done"], 2 * c + n + 1)
                    seq(nc.vector.tensor_tensor(rsum[:, n, :], rsum[:, n, :], es[:, n, :], ALU.add))
                    nc.vector.reciprocal(rden[:, n, :], rsum[:, n, :]).then_inc(S["rd_done"], 1)

                dve.wait_ge(S["ropq_done"], c + 1)
                nc.vector.tensor_tensor(rot_s[:], PS[:, 4, :].rearrange("p (t c) -> p t c", t=TPH),
                                        rope_s[:, tok].unsqueeze(1).broadcast_to([P, TPH, CH]), ALU.mult).then_inc(S["ts_done"], 1)
                dve.wait_ge(S["ts_done"], 2 * c + 3)
                dve.wait_ge(S["t0_done"], 2 * c + 2)
                nc.vector.tensor_tensor(q_rot[:], rot_c[:], rot_s[:], ALU.add).then_inc(S["qs_done"], 1)
                dve.wait_ge(S["vw_done"], c + 1 + VW_CREDIT)
                nc.vector.tensor_tensor(rotk_s[:], PS[:, 5, 0:CH], rope_s[:, tok], ALU.mult).then_inc(S["ts_done"], 1)
                dve.wait_ge(S["ts_done"], 2 * c + 4)
                dve.wait_ge(S["kw_shift"], 2 * c + 2)
                nc.vector.tensor_tensor(k_win[:, CH:], rotk_c[:], rotk_s[:], ALU.add).then_inc(S["kw_done"], 1)
                level(c, 2)
                q_decayed(c, 1)
                weights(0)
                q_decayed(c, 2)
                level(c, 3)
                weights(1)
                q_decayed(c, 3)
                level(c, 4)
                sub_max(0)
                weights(2)
                q_decayed(c, 4)
                weights(3)
                over(0)
                sub_max(1)
                weights(4)
                seq(nc.vector.tensor_copy(m_cur, mixc[:, M_BAND:M_BAND + 2 * CH]))
                if more:
                    start(c + 1)
                over(1)
                if more:
                    q_decayed(c + 1, 0)
                dve.wait_ge(S["gend_done"], c + 1 + GE_CREDIT)
                dve.wait_ge(S["o_done"], c + 2)
                nc.vector.tensor_tensor(state[:], state[:], g_end[:].unsqueeze(2).broadcast_to([P, TPH, HEAD]),
                                        ALU.mult).then_inc(S["s_scaled"], 1)
                dve.wait_ge(S["s_scaled"], c + 1)
                dve.wait_ge(S["s_done"], c + 1 + SD_CREDIT)
                nc.vector.tensor_tensor(state[:], state[:], PS[:, 7, 0:TPH * HEAD].rearrange("p (t v) -> p t v", t=TPH),
                                        ALU.add).then_inc(S["s_upd"], 1)

            start(0)
            q_decayed(0, 0)
            with dve.Fori(0, N_CH - 1) as c:
                seq.enter(c, 9)
                body(c, True)
                seq.leave(N_CH - 1)
            body(N_CH - 1, False)

            ST = slice(N_PROMPT, TOK)
            rc8 = rope_c[:, ST].unsqueeze(1).broadcast_to([P, TPH, N_SAMPLE])
            rs8 = rope_s[:, ST].unsqueeze(1).broadcast_to([P, TPH, N_SAMPLE])
            dve.wait_ge(S["a_s"], 1)
            dve.wait_ge(S["smp_in"], 48)
            nc.vector.tensor_tensor(qt_s[:], q_reg[:, :, ST], rc8, ALU.mult)
            nc.vector.tensor_tensor(qu_s[:], PS[:, 6, 0:TPH * N_SAMPLE].rearrange("p (t b) -> p t b", t=TPH), rs8, ALU.mult)
            nc.vector.tensor_tensor(kt_s[:, 0], kv[:, 0, ST], rope_c[:, ST], ALU.mult)
            seq(nc.vector.tensor_tensor(kt_s[:, 1], PS[:, 6, 32:32 + N_SAMPLE], rope_s[:, ST], ALU.mult))
            seq(nc.vector.tensor_tensor(q_s[:], qt_s[:], qu_s[:], ALU.add))
            nc.vector.tensor_tensor(k_win_s[:, :, WINDOW - 1], kt_s[:, 0], kt_s[:, 1], ALU.add).then_inc(S["d_s"], 1)
            seq(nc.vector.tensor_tensor(state_s[:].rearrange("p t b v -> p (t b) v"), state_s[:].rearrange("p t b v -> p (t b) v"),
                                        f_s[:].rearrange("p t b -> p (t b)").unsqueeze(2).broadcast_to([P, TPH * N_SAMPLE, HEAD]), ALU.mult))
            dve.wait_ge(S["a_s"], 2)
            W = 2 * N_SAMPLE
            scores = PS[0:GQA, 4:8, :].rearrange("p a (i t) -> p (a i) t", t=CH)
            seq(nc.vector.tensor_reduce(st_s[0:GQA, 0, :], scores, AX_X, ALU.max))
            seq(nc.vector.tensor_copy(st_s[0:GQA, 1, :].rearrange("p (n b) -> p n b", n=2),
                                      vecs[0:GQA, V_SINKT:V_SINKT + 2].unsqueeze(2).broadcast_to([GQA, 2, N_SAMPLE])))
            seq(nc.vector.scalar_tensor_tensor(st_s[0:GQA, 2, :], st_s[0:GQA, 0, :], HEAD ** -0.5, st_s[0:GQA, 1, :],
                                               ALU.mult, ALU.max))
            nc.vector.tensor_tensor(st_s[0:GQA, 3, :], st_s[0:GQA, 1, :], st_s[0:GQA, 2, :], ALU.subtract)
            nc.vector.scalar_tensor_tensor(sm_s[0:GQA], scores, HEAD ** -0.5,
                                           st_s[0:GQA, 2, :].unsqueeze(2).broadcast_to([GQA, W, WINDOW]),
                                           ALU.mult, ALU.subtract).then_inc(S["v_s"], 1)
            dve.wait_ge(S["a_s"], 3)
            for t in range(TPH):
                src = PS[:, 0:4, :].rearrange("p a (b t v) -> p t (a b) v", b=2, t=TPH)[:, t]
                kvp = nc.vector.tensor_tensor(kv_s[:, t], src, k_gate[:, t, ST].unsqueeze(2).broadcast_to([P, N_SAMPLE, HEAD]), ALU.mult)
            kvp.then_inc(S["a_ps"], 1)
            dve.wait_ge(S["a_ps"], 1)
            nc.vector.tensor_tensor(state_s[:], state_s[:], kv_s[:], ALU.add).then_inc(S["d_s"], 1)
            dve.wait_ge(S["sig_done"], 3)
            seq(nc.vector.tensor_reduce(st_s[0:GQA, 4, :], sm_s[0:GQA], AX_X, ALU.add))
            seq(nc.vector.tensor_tensor(st_s[0:GQA, 5, :], st_s[0:GQA, 4, :], st_s[0:GQA, 3, :], ALU.add))
            seq(nc.vector.reciprocal(st_s[0:GQA, 6, :], st_s[0:GQA, 5, :]))
            nc.vector.tensor_tensor(sm_s[0:GQA], sm_s[0:GQA], st_s[0:GQA, 6, :].unsqueeze(2).broadcast_to([GQA, W, WINDOW]),
                                    ALU.mult).then_inc(S["d_s"], 1)

            gs = lambda r, g: r[:, :, g * GW:(g + 1) * GW]
            dve.wait_ge(S["out_in"], 96)
            dve.wait_ge(S["cg_done"], 1)
            for g in range(NG):
                dve.wait_ge(S["crms_done"], g + 1)
                nc.vector.tensor_tensor(gs(hq_reg, g), gs(hq_reg, g), c_root[:], ALU.mult).then_inc(S["co_done"], 1)
                dve.wait_ge(S["co_done"], g + 1)
                nc.vector.scalar_tensor_tensor(gs(hq_reg, g), gs(hq_reg, g), vecs[:, V_OUTG:V_OUTG + 1], gs(hg_reg, g),
                                               ALU.mult, ALU.mult).then_inc(S["ch_done"], 1)
                dve.wait_ge(S["cat_hi_h"], g + 1)
                if g:
                    dve.wait_ge(S["a_s"], 6)
                nc.vector.tensor_tensor(x_lo[:, g, TPH:], gs(hq_reg, g), x_hi[:, g, TPH:].bitcast(F32),
                                        ALU.subtract).then_inc(S["cat_lo_h"], 1)

            def out_by_group(p, between):
                for g in range(NG):
                    for o in range(2):
                        if (g, o) in between:
                            between[g, o]()
                        v = 6 * p + 2 * g + o
                        dve.wait_ge(S["unit_done"], UNIT_CREDIT + U_OUT + v + 1)
                        nc.vector.tensor_copy(y[:, g, 2 * p + o, :], PS[:, v % 3, :GW]).then_inc(S["unit_evac"], 1)

            out_by_group(0, {(NG - 1, 1): lambda: split_lo(G_OUT + 2, 0)})
            with dve.Fori(1, KT // 2 - 1) as p:
                for o in range(2):
                    split_lo(G_OUT + 2 * p + o + 1, 1 - o)
                    for g in range(NG):
                        dve.wait_ge(S["unit_done"], UNIT_CREDIT + U_OUT + 6 * p + 3 * o + g + 1)
                        nc.vector.tensor_copy(y[:, g, 2 * p + o, :], PS[:, g, :GW]).then_inc(S["unit_evac"], 1)
            split_lo(G_OUT + KT - 1, 1)
            out_by_group(KT // 2 - 1, {(NG - 1, 0): lambda: fold(("F", 1, 0))})
            border_dve(1, splits(G_FFN2))
            ffn(G_FFN2, U_FFN2, 1, 2, lambda: None)




def tables():
    ident = np.eye(P, dtype=np.float32)
    head_ones = np.kron(np.eye(2), np.ones((HEAD, HEAD))).astype(np.float32)
    s, t = np.arange(CH)[:, None], np.arange(CH)[None]
    mixc = np.zeros((P, NM), np.float32)
    for i, b in enumerate(LEVELS):
        mixc[:, M_LVL + i * CH:M_LVL + (i + 1) * CH] = (s // (2 * b) == t // (2 * b)) & (s // b < t // b)
    mixc[:, M_SUB:M_SUB + CH] = (s // SUB == t // SUB) & (s <= t)
    key = np.arange(2 * CH)[None]
    rel = s + WINDOW - key
    band = (rel >= 0) & (rel < WINDOW)
    mixc[:, M_BAND:M_BAND + 2 * CH] = np.where(band, 0.0, NEG)
    mixc[:, M_FIRST:M_FIRST + 2 * CH] = np.where(band & (key >= WINDOW), 0.0, NEG)
    half = ROT // 2
    inv = np.float32(THETA) ** (-np.arange(half, dtype=np.float32) / np.float32(half))
    pos = np.concatenate([np.arange(N_PROMPT), np.full(N_SAMPLE, PAST_LEN)]).astype(np.float32)
    ang = inv[:, None] * pos[None]
    rope = np.zeros((2, P, TOK), np.float32)
    rope[0] = 1.0
    for h0 in (0, HEAD):
        for d in range(half):
            mixc[h0 + half + d, M_ROT + h0 + d] = -1.0
            mixc[h0 + d, M_ROT + h0 + half + d] = 1.0
            for at in (h0 + d, h0 + half + d):
                rope[0, at], rope[1, at] = np.cos(ang[d]), np.sin(ang[d])
    pick = np.repeat(np.eye(N_SAMPLE, dtype=np.float32)[:, :, None], HEAD, axis=2)
    return {"ident": ident, "head_ones": head_ones, "mixc": mixc, "rope": rope, "pick": pick}


def kernel(**inputs):
    import concourse.bacc as bacc
    from concourse.bass_utils import run_bass_kernel_spmd as run

    c = np.ascontiguousarray
    x = np.concatenate([inputs["x_prompt"][0], inputs["x_sample"][:, 0]], axis=0)
    arrays = {"x": c(x.reshape(NG, GW, KT, P).transpose(0, 3, 2, 1))}
    for f in ("1", "2"):
        w = inputs[f"ffn{f}_w_gu"][0].reshape(KT, P, 2, HT, P)
        arrays["w_gu" + f] = c(w.transpose(3, 2, 1, 0, 4)).reshape(2 * HT, P, KT * P)
        arrays["w_down" + f] = c(inputs[f"ffn{f}_w_down"][0].reshape(HT, P, D_MODEL))
    cols = [inputs[n][0].reshape(KT, P).T for n in
            ("ffn1_pre_g", "ffn1_post_g", "mix_pre_g", "mix_post_g", "ffn2_pre_g", "ffn2_post_g")]
    cols += [inputs["hgrn_lb"][r].reshape(TPH, P).T for r in range(2)]
    cols += [np.tile(inputs["hgrn_out_g"][0], 2)[:, None], np.tile(inputs["attn_sinks"][0][None], (P, 1)),
             np.tile(inputs["attn_sinks"][0].reshape(N_KV, GQA).T, (P // GQA, 1))]
    arrays["vecs"] = c(np.concatenate(cols, axis=1))
    w_in = inputs["w_in"][0]
    q, k, v, hq, hf, hi, hg = np.split(w_in, np.cumsum([512, 128, 128, 512, 512, 512])[:6], axis=1)
    q = q.reshape(D_MODEL, N_KV, GQA, HEAD).transpose(0, 2, 1, 3).reshape(D_MODEL, 512)
    w_in = np.concatenate([hf, hq, hi, q, hg, k, v], axis=1)
    arrays["w_in"] = c(w_in.reshape(KT, P, IN_TILES, P).transpose(2, 1, 0, 3)).reshape(IN_TILES, P, KT * P)
    w_out = inputs["w_out"][0]
    w_att = w_out[:512].reshape(N_KV, GQA, HEAD, D_MODEL).transpose(1, 0, 2, 3).reshape(512, D_MODEL)
    w_out = np.concatenate([w_att, w_out[512:]], axis=0)
    arrays["w_out"] = c(w_out.reshape(KT, P, KT, P).transpose(2, 1, 0, 3)).reshape(KT, P, KT * P)
    kc, vc = inputs["cache_win_k"][0], inputs["cache_win_v"][0]
    arrays["k_cache"] = c(kc[:, 1:].reshape(N_SAMPLE, WINDOW - 1, P).transpose(2, 0, 1))
    arrays["v_cache"] = c(vc[:, 1:].reshape(N_SAMPLE, WINDOW - 1, P).transpose(1, 0, 2))
    arrays["state"] = c(inputs["state_hgrn"][0].reshape(N_SAMPLE, TPH, 2, HEAD, HEAD)
                        .transpose(2, 3, 1, 0, 4)).reshape(P, TPH, N_SAMPLE, HEAD)
    arrays.update(tables())

    nc = bacc.Bacc("TRN2", target_bir_lowering=False, num_devices=1)
    ins = {k: nc.dram_tensor("in_" + k, v.shape, F32, kind="ExternalInput").ap() for k, v in arrays.items()}
    stream = (NG, P, KT, GW)
    shapes = {"y": stream, "k_win": (P, CH), "v_win": (P, CH), "state": (P, TPH, HEAD),
              "k_win_s": (P, N_SAMPLE, WINDOW), "v_win_s": (P, N_SAMPLE, P), "state_s": (P, TPH, N_SAMPLE, HEAD)}
    outs = {k: nc.dram_tensor("out_" + k, s, F32, kind="ExternalOutput").ap() for k, s in shapes.items()}
    for k in ("x1", "x2"):
        outs[k] = nc.dram_tensor("stream_" + k, stream, F32, kind="Internal").ap()
    build(nc, ins, outs)
    r = run(nc, [{"in_" + k: v for k, v in arrays.items()}], core_ids=[0]).results[0]
    yv = r["out_y"].transpose(0, 3, 2, 1).reshape(TOK, D_MODEL)
    kp = r["out_k_win"].T.reshape(1, 1, CH, N_KV, HEAD)
    vp = r["out_v_win"].reshape(1, 1, CH, N_KV, HEAD)
    sp = r["out_state"].reshape(2, HEAD, TPH, HEAD).transpose(2, 0, 1, 3).reshape(1, 1, N_HEADS, HEAD, HEAD)
    ks = r["out_k_win_s"].transpose(1, 2, 0).reshape(1, N_SAMPLE, WINDOW, N_KV, HEAD)
    vs = r["out_v_win_s"].transpose(1, 0, 2).reshape(1, N_SAMPLE, WINDOW, N_KV, HEAD)
    ss = r["out_state_s"].reshape(2, HEAD, TPH, N_SAMPLE, HEAD).transpose(3, 2, 0, 1, 4)\
        .reshape(1, N_SAMPLE, N_HEADS, HEAD, HEAD)
    return tuple(map(c, (yv[:N_PROMPT][None], yv[N_PROMPT:][:, None], kp, vp, sp, ks, vs, ss)))
```
